# Optimizing a Trainium2 kernel written in Bass

```python
import math
import jax
import jax.numpy as jnp
from jax import lax
import numpy as np

D_MODEL = 1024
BATCH = 1
SEQ = 256
DEPTH = 2

HEAD_DIM = 64
N_MIXERS = 4
GROUP_HEADS = D_MODEL // HEAD_DIM // N_MIXERS
GROUP_WIDTH = GROUP_HEADS * HEAD_DIM
MIX_WIDTH = N_MIXERS * GROUP_WIDTH

MLA_Q_RANK = 256
MLA_KV_RANK = 128
MLA_NOPE = 64
MLA_ROPE = 32
MLA_V = HEAD_DIM

DIL_CONFIGS = ((128, 1), (512, 4), (2048, 16))

DIFF_QK = HEAD_DIM // 2
DIFF_V = HEAD_DIM

D_FF_DENSE = 2816
N_EXPERTS = 8
TOP_K = 2
D_FF_EXPERT = 3584
N_DENSE = (DEPTH + 1) // 2
N_MOE = DEPTH // 2

ROPE_THETA = 10000.0
NORM_EPS = 1e-6
BLOCK = 128
NEG_INF = -1e30

IN_SIZES = (MLA_Q_RANK, MLA_KV_RANK, MLA_ROPE,
            GROUP_WIDTH, GROUP_WIDTH, GROUP_WIDTH,
            GROUP_WIDTH, GROUP_WIDTH, GROUP_WIDTH, GROUP_HEADS,
            GROUP_WIDTH, GROUP_WIDTH, GROUP_WIDTH)
IN_WIDTH = 2724

kernel_name = 'hybrid_parallel_group_decoder'

def _rmsnorm(x, g):
    xf = x.astype(jnp.float32)
    y = xf * lax.rsqrt(jnp.mean(xf * xf, axis=-1, keepdims=True) + NORM_EPS)
    return (y * g.astype(jnp.float32)).astype(x.dtype)

def _rope(x, pos):
    half = x.shape[-1] // 2
    inv = ROPE_THETA ** (-jnp.arange(half, dtype=jnp.float32) / half)
    ang = pos.astype(jnp.float32)[:, None] * inv[None, :]
    cos = jnp.cos(ang)[None, :, None, :]
    sin = jnp.sin(ang)[None, :, None, :]
    xf = x.astype(jnp.float32)
    x1, x2 = xf[..., :half], xf[..., half:]
    return jnp.concatenate([x1 * cos - x2 * sin, x2 * cos + x1 * sin], axis=-1).astype(x.dtype)

def _q_block(t, i):
    return lax.dynamic_slice_in_dim(t, i * BLOCK, BLOCK, axis=1)

def _causal_mask(i, s_len):
    q_pos = i * BLOCK + jnp.arange(BLOCK)
    return jnp.arange(s_len)[None, :] <= q_pos[:, None]

def _masked_softmax(s, mask):
    return jax.nn.softmax(jnp.where(mask, s, NEG_INF), axis=-1)

def _causal_sweep(block_fn, s_len):
    out = lax.map(block_fn, jnp.arange(s_len // BLOCK))
    nblk, b, blk, h, dv = out.shape
    return out.transpose(1, 0, 2, 3, 4).reshape(b, nblk * blk, h, dv)

def _mla(cq, ckv, kr, g_ql, g_kvl, w_uq, w_ukv, pos):
    b, s_len, _ = cq.shape
    q = (_rmsnorm(cq, g_ql) @ w_uq).reshape(b, s_len, GROUP_HEADS, MLA_NOPE + MLA_ROPE)
    q_nope, q_rot = q[..., :MLA_NOPE], _rope(q[..., MLA_NOPE:], pos)
    kv = (_rmsnorm(ckv, g_kvl) @ w_ukv).reshape(b, s_len, GROUP_HEADS, MLA_NOPE + MLA_V)
    k_nope, v = kv[..., :MLA_NOPE], kv[..., MLA_NOPE:]
    k_rot = _rope(kr[:, :, None, :], pos)[:, :, 0]
    scale = (MLA_NOPE + MLA_ROPE) ** -0.5

    def block_fn(i):
        s = (jnp.einsum('bqhd,bkhd->bhqk', _q_block(q_nope, i), k_nope)
             + jnp.einsum('bqhd,bkd->bhqk', _q_block(q_rot, i), k_rot)).astype(jnp.float32) * scale
        p = _masked_softmax(s, _causal_mask(i, s_len))
        return jnp.einsum('bhqk,bkhd->bqhd', p.astype(v.dtype), v)

    return _causal_sweep(block_fn, s_len)

def _dilated_branch(q, k, v, window, dilation):
    b, s_len, h, dh = q.shape
    n = window // dilation
    span = n * dilation
    s_pad = -(-s_len // span) * span
    nb = s_pad // span

    def to_sub(t):
        t = jnp.pad(t, ((0, 0), (0, s_pad - s_len), (0, 0), (0, 0)))
        t = t.reshape(b, s_pad // dilation, dilation, h, dh).transpose(0, 2, 3, 1, 4)
        return t.reshape(b, dilation, h, nb, n, dh)

    def with_prev(t):
        prev = jnp.concatenate([jnp.zeros_like(t[:, :, :, :1]), t[:, :, :, :-1]], axis=3)
        return jnp.concatenate([prev, t], axis=4)

    qs = to_sub(q)
    kk, vv = with_prev(to_sub(k)), with_prev(to_sub(v))
    s = jnp.einsum('brhnid,brhnjd->brhnij', qs, kk).astype(jnp.float32) * dh ** -0.5
    i_idx = jnp.arange(n)[:, None]
    c_idx = jnp.arange(2 * n)[None, :]
    band = (c_idx >= i_idx) & (c_idx <= i_idx + n)
    valid = band[None] & ((jnp.arange(nb) > 0)[:, None, None] | (c_idx >= n)[None])
    s = jnp.where(valid, s, NEG_INF)
    m = jnp.max(s, axis=-1, keepdims=True)
    p = jnp.exp(s - m)
    l = jnp.sum(p, axis=-1, keepdims=True)
    o = jnp.einsum('brhnij,brhnjd->brhnid', p.astype(v.dtype), vv).astype(jnp.float32) / l
    lse = (m + jnp.log(l))[..., 0]
    o = o.reshape(b, dilation, h, s_pad // dilation, dh).transpose(0, 3, 1, 2, 4).reshape(b, s_pad, h, dh)[:, :s_len]
    lse = lse.reshape(b, dilation, h, s_pad // dilation).transpose(0, 3, 1, 2).reshape(b, s_pad, h)[:, :s_len]
    return o, lse

def _dilated_attention(q, k, v):
    outs, lses = [], []
    for window, dilation in DIL_CONFIGS:
        o, lse = _dilated_branch(q, k, v, window, dilation)
        outs.append(o)
        lses.append(lse)
    w = jax.nn.softmax(jnp.stack(lses, axis=0), axis=0)
    return jnp.sum(w[..., None] * jnp.stack(outs, axis=0), axis=0)

def _forgetting_attention(q, k, v, f_logit):
    s_len = q.shape[1]
    log_f = jax.nn.log_sigmoid(f_logit.astype(jnp.float32))
    c = jnp.cumsum(log_f, axis=1).transpose(0, 2, 1)
    scale = HEAD_DIM ** -0.5

    def block_fn(i):
        c_q = lax.dynamic_slice_in_dim(c, i * BLOCK, BLOCK, axis=2)
        s = jnp.einsum('bqhd,bkhd->bhqk', _q_block(q, i), k).astype(jnp.float32) * scale
        s = s + c_q[..., :, None] - c[..., None, :]
        p = _masked_softmax(s, _causal_mask(i, s_len))
        return jnp.einsum('bhqk,bkhd->bqhd', p.astype(v.dtype), v)

    return _causal_sweep(block_fn, s_len)

def _differential_attention(q, k, v, lam, g_sub, lam_init, pos):
    b, s_len, _ = q.shape
    q = _rope(q.reshape(b, s_len, 2 * GROUP_HEADS, DIFF_QK), pos).reshape(b, s_len, GROUP_HEADS, 2, DIFF_QK)
    k = _rope(k.reshape(b, s_len, 2 * GROUP_HEADS, DIFF_QK), pos).reshape(b, s_len, GROUP_HEADS, 2, DIFF_QK)
    v = v.reshape(b, s_len, GROUP_HEADS, DIFF_V)
    q1, q2 = q[..., 0, :], q[..., 1, :]
    k1, k2 = k[..., 0, :], k[..., 1, :]
    scale = DIFF_QK ** -0.5

    def block_fn(i):
        mask = _causal_mask(i, s_len)
        s1 = jnp.einsum('bqhd,bkhd->bhqk', _q_block(q1, i), k1).astype(jnp.float32) * scale
        s2 = jnp.einsum('bqhd,bkhd->bhqk', _q_block(q2, i), k2).astype(jnp.float32) * scale
        p = _masked_softmax(s1, mask) - lam * _masked_softmax(s2, mask)
        return jnp.einsum('bhqk,bkhd->bqhd', p.astype(v.dtype), v)

    o = _causal_sweep(block_fn, s_len)
    return _rmsnorm(o, g_sub) * (1.0 - lam_init)

def _swiglu(h, w_gate, w_up, w_down):
    return (jax.nn.silu(h @ w_gate) * (h @ w_up)) @ w_down

def _moe(h, w_router, w_gate, w_up, w_down):
    b, s_len, d = h.shape
    t = h.reshape(b * s_len, d)
    logits = (t @ w_router).astype(jnp.float32)
    top_val, top_idx = lax.top_k(logits, TOP_K)
    weights = jax.nn.softmax(top_val, axis=-1)
    gates = jnp.sum(jax.nn.one_hot(top_idx, N_EXPERTS, dtype=jnp.float32) * weights[..., None], axis=1)
    y = jnp.zeros((b * s_len, d), jnp.float32)
    for e in range(N_EXPERTS):
        y = y + gates[:, e:e + 1] * _swiglu(t, w_gate[e], w_up[e], w_down[e]).astype(jnp.float32)
    return y.reshape(b, s_len, d).astype(h.dtype)

def _normal(key, shape, scale):
    return jax.random.normal(key, shape, jnp.float32) * scale

def setup_inputs(seed: int = 0) -> dict:
    key = jax.random.key(seed)
    ks = jax.random.split(key, 24)
    gain = lambda k, shape: 1.0 + _normal(k, shape, 0.01)
    return {
        'x': _normal(ks[0], (BATCH, SEQ, D_MODEL), 1.0),
        'g_mix': gain(ks[1], (DEPTH, D_MODEL)),
        'w_in': _normal(ks[2], (DEPTH, D_MODEL, IN_WIDTH), D_MODEL ** -0.5),
        'b_forget': _normal(ks[3], (DEPTH, GROUP_HEADS), 0.1),
        'g_q_lat': gain(ks[4], (DEPTH, MLA_Q_RANK)),
        'g_kv_lat': gain(ks[5], (DEPTH, MLA_KV_RANK)),
        'w_uq': _normal(ks[6], (DEPTH, MLA_Q_RANK, GROUP_HEADS * (MLA_NOPE + MLA_ROPE)), MLA_Q_RANK ** -0.5),
        'w_ukv': _normal(ks[7], (DEPTH, MLA_KV_RANK, GROUP_HEADS * (MLA_NOPE + MLA_V)), MLA_KV_RANK ** -0.5),
        'lambda_q1': _normal(ks[8], (DEPTH, DIFF_QK), 0.1),
        'lambda_k1': _normal(ks[9], (DEPTH, DIFF_QK), 0.1),
        'lambda_q2': _normal(ks[10], (DEPTH, DIFF_QK), 0.1),
        'lambda_k2': _normal(ks[11], (DEPTH, DIFF_QK), 0.1),
        'g_diff_sub': gain(ks[12], (DEPTH, DIFF_V)),
        'w_out': _normal(ks[13], (DEPTH, MIX_WIDTH, D_MODEL), MIX_WIDTH ** -0.5),
        'g_ffn': gain(ks[14], (DEPTH, D_MODEL)),
        'w_ffn_gate': _normal(ks[15], (N_DENSE, D_MODEL, D_FF_DENSE), D_MODEL ** -0.5),
        'w_ffn_up': _normal(ks[16], (N_DENSE, D_MODEL, D_FF_DENSE), D_MODEL ** -0.5),
        'w_ffn_down': _normal(ks[17], (N_DENSE, D_FF_DENSE, D_MODEL), D_FF_DENSE ** -0.5),
        'w_router': _normal(ks[18], (N_MOE, D_MODEL, N_EXPERTS), D_MODEL ** -0.5),
        'w_exp_gate': _normal(ks[19], (N_MOE, N_EXPERTS, D_MODEL, D_FF_EXPERT), D_MODEL ** -0.5),
        'w_exp_up': _normal(ks[20], (N_MOE, N_EXPERTS, D_MODEL, D_FF_EXPERT), D_MODEL ** -0.5),
        'w_exp_down': _normal(ks[21], (N_MOE, N_EXPERTS, D_FF_EXPERT, D_MODEL), D_FF_EXPERT ** -0.5),
        'g_final': gain(ks[22], (D_MODEL,)),
    }

def reference(x, g_mix, w_in, b_forget, g_q_lat, g_kv_lat, w_uq, w_ukv,
              lambda_q1, lambda_k1, lambda_q2, lambda_k2, g_diff_sub, w_out,
              g_ffn, w_ffn_gate, w_ffn_up, w_ffn_down,
              w_router, w_exp_gate, w_exp_up, w_exp_down, g_final):
    b, s_len, _ = x.shape
    pos = jnp.arange(s_len)
    offsets = []
    acc = 0
    for size in IN_SIZES[:-1]:
        acc += size
        offsets.append(acc)
    for l in range(DEPTH):
        h = _rmsnorm(x, g_mix[l])
        z = h @ w_in[l]
        (cq, ckv, kr, q_b, k_b, v_b, q_c, k_c, v_c, f_c, q_d, k_d, v_d) = jnp.split(z, offsets, axis=-1)
        heads = lambda t: t.reshape(b, s_len, GROUP_HEADS, HEAD_DIM)

        y_a = _mla(cq, ckv, kr, g_q_lat[l], g_kv_lat[l], w_uq[l], w_ukv[l], pos)
        y_b = _dilated_attention(_rope(heads(q_b), pos), _rope(heads(k_b), pos), heads(v_b))
        y_c = _forgetting_attention(heads(q_c), heads(k_c), heads(v_c), f_c + b_forget[l])
        lam_init = 0.8 - 0.6 * math.exp(-0.3 * l)
        lam = (jnp.exp(jnp.sum(lambda_q1[l] * lambda_k1[l]).astype(jnp.float32))
               - jnp.exp(jnp.sum(lambda_q2[l] * lambda_k2[l]).astype(jnp.float32)) + lam_init)
        y_d = _differential_attention(q_d, k_d, v_d, lam, g_diff_sub[l], lam_init, pos)

        y = jnp.concatenate([t.reshape(b, s_len, GROUP_WIDTH).astype(x.dtype) for t in (y_a, y_b, y_c, y_d)], axis=-1)
        x = x + y @ w_out[l]

        h = _rmsnorm(x, g_ffn[l])
        if l % 2 == 0:
            x = x + _swiglu(h, w_ffn_gate[l // 2], w_ffn_up[l // 2], w_ffn_down[l // 2])
        else:
            x = x + _moe(h, w_router[l // 2], w_exp_gate[l // 2], w_exp_up[l // 2], w_exp_down[l // 2])
    return _rmsnorm(x, g_final)


_drawn_inputs = setup_inputs


def setup_inputs(seed=0):
    import zlib

    import numpy as np

    out = dict(_drawn_inputs(seed))
    spreads = {}
    factors = {'g_mix': 3.965,
     'g_q_lat': 8.0,
     'g_kv_lat': 8.0,
     'g_diff_sub': 16.034,
     'g_final': 31.929,
     'g_ffn': 5.279}
    for name, (base, spread) in spreads.items():
        noise = np.random.default_rng([zlib.crc32(name.encode()), seed]).standard_normal(out[name].shape)
        drawn = base * np.exp(spread * noise) if base else spread * noise
        out[name] = jnp.asarray(drawn.astype(out[name].dtype))
    for name, factor in factors.items():
        out[name] = (out[name] * factor).astype(out[name].dtype)
    return out
```

```python
import math
from contextlib import ExitStack

import concourse.bass as bass
import numpy as np
from concourse import mybir

F32 = mybir.dt.float32
I32 = mybir.dt.int32
U32 = mybir.dt.uint32
ALU = mybir.AluOpType
ACT = mybir.ActivationFunctionType
AX = mybir.AxisListType

P = 128
D_MODEL, SEQ, DEPTH = 1024, 256, 2
TILES = SEQ // P
KC = D_MODEL // P
HEADS, HEAD_DIM = 4, 64
GROUP = HEADS * HEAD_DIM
Q_RANK, KV_RANK, NOPE, ROT = 256, 128, 64, 32
QK_A = NOPE + ROT
DIFF_QK = 32
IN_WIDTH = 2724
D_FF, D_FF_EXPERT, EXPERTS = 2816, 3584, 8
EPS = 1e-6
NEG = -1e30
DIL_CONFIGS = ((128, 1), (512, 4), (2048, 16))
AUG = HEAD_DIM + 2

CQ, CKV, KR = 0, 256, 384
QB, KB_, VB = 416, 672, 928
QCOL, KCOL, VCOL, FCOL = 1184, 1440, 1696, 1952
QD, KD, VD = 1956, 2212, 2468
Z_CUTS = (0, 416, 928, 1440, 1952, 2464, 2724)
NZ = len(Z_CUTS) - 1

RING = 7
SLOT = 4096
FW = 512
FF_STEPS = -(-D_FF // FW)
EX_STEPS = D_FF_EXPERT // FW
EX_CHUNKS = 3 * EX_STEPS
assert EX_CHUNKS % RING == 0
SLOTS = 128
ITEMS = EXPERTS * (SEQ // SLOTS)

JOBS = (("B", 0, 4, 0, 128), ("B", 1, 4, 0, 256), ("A", 0, 4, 0, 128), ("A", 1, 4, 0, 256),
        ("C", 0, 4, 0, 128), ("C", 1, 4, 0, 256), ("D", 0, 8, 0, 128), ("D", 1, 4, 0, 256),
        ("D", 1, 4, 4, 256))
NJ = len(JOBS)
SCALE = {"A": QK_A ** -0.5, "B": HEAD_DIM ** -0.5, "C": 1.0, "D": DIFF_QK ** -0.5}
YCOL = {"A": 0, "B": GROUP, "C": 2 * GROUP, "D": 3 * GROUP}
FIRST_D = 6

MIXER = ["Z0", "Z1", "LT", "Z2", "LM", "QB", "J0", "Z3", "QA", "J1", "Z4", "J2", "Z5", "CS", "QD",
         "J3", "QC", "J4", "J5", "J6", "J7", "J8", "J9", "J10"]

BATCH = {"LT": (0, 1), "QB": (2, 3), "QA": (4, 5, 6, 7), "CS": (8,), "QD": (9, 10),
         "QC": (11, 12, 13, 14), "YT": (15, 16, 17, 18)}
NEED = {"B": 4, "A": 8, "D": 11, "C": 15}


def pt_batches(k):
    return JOBS[k][4] // P if JOBS[k][0] != "D" else 1


def spot(k, s):
    g, _, n, _, _ = JOBS[k]
    if g == "B":
        return (s % 2) * 2 + s // 2
    return (s % 4) * 2 + s // 4 if n == 8 else s


def head_blocks(k):
    g, _, n, _, nk = JOBS[k]
    heads = range(n) if g != "D" else range(0, n, 2)
    nh = len(heads)
    all_ = [(spot(k, s), kb, kb * nh + i) for kb in range(nk // P) for i, s in enumerate(heads)]
    return [all_[i:i + 4] for i in range(0, len(all_), 4)]


def pt_done(k):
    return sum(pt_batches(j) for j in range(k + 1))


CONST = {}


def _constants():
    p = np.arange(P)[:, None]
    d1 = P + p - np.arange(SEQ)[None, :]
    count = sum(((d1 >= 0) & (d1 % dil == 0) & (d1 <= win)).astype(int) for win, dil in DIL_CONFIGS)
    parts = [
        ("ident", np.eye(P)),
        ("causal", np.where(d1 >= 0, 0.0, NEG)),
        ("dilated", np.where(count > 0, np.log(np.maximum(count, 1)), NEG)),
        ("tri", (p <= np.arange(P)[None, :]).astype(float)),
        ("ones", np.ones((P, P))),
        ("iota", np.broadcast_to(np.arange(P), (P, P))),
    ]
    for half in (16, 32):
        inv = np.float32(10000.0) ** (-np.arange(half, dtype=np.float32) / np.float32(half))
        for t in range(TILES):
            ang = (np.arange(P, dtype=np.float32)[:, None] + P * t) * inv[None, :].astype(np.float32)
            parts += [(f"cos{half}_{t}", np.cos(ang)), (f"sin{half}_{t}", np.sin(ang)),
                      (f"nsin{half}_{t}", -np.sin(ang))]
    at = 0
    for name, a in parts:
        CONST[name] = (at, a.shape[1])
        at += a.shape[1]
    return np.ascontiguousarray(np.concatenate([a for _, a in parts], axis=1).astype(np.float32))


CONSTANTS = _constants()


def plan_chunks(w):
    chunks = []

    def rows(src):
        return src.rearrange("(c p) f -> p c f", p=P)

    for l in range(DEPTH):
        for c in range(NZ):
            a, b = Z_CUTS[c], Z_CUTS[c + 1]
            if c == 3:
                chunks.append([(0, (2, HEADS * QK_A), rows(w["w_uq"][l])),
                               (2 * HEADS * QK_A, (1, 2 * GROUP), rows(w["w_ukv"][l]))])
            chunks.append([(0, (KC, b - a), rows(w["w_in"][l][:, a:b]))])
        for h in range(2):
            chunks.append([(0, (KC, FW), rows(w["w_out"][l][:, h * FW:(h + 1) * FW]))])
        if l == 0:
            for kind, s in ff_order(FF_STEPS):
                a, b = s * FW, min((s + 1) * FW, D_FF)
                if kind == "d":
                    chunks.append([(0, ((b - a) // P, D_MODEL), rows(w["w_ffn_down"][0][a:b, :]))])
                else:
                    src = w["w_ffn_gate"] if kind == "g" else w["w_ffn_up"]
                    chunks.append([(0, (KC, b - a), rows(src[0][:, a:b]))])
    return chunks


def ff_order(steps):
    out = []
    for s in range(steps):
        out.append(("g", s))
        if s:
            out.append(("d", s - 1))
        out.append(("u", s))
    return out + [("d", steps - 1)]


def ex_order():
    out = []
    for s in range(EX_STEPS):
        out += [("g", s), ("u", s)]
        if s:
            out.append(("d", s - 1))
    return out + [("d", EX_STEPS - 1)]


L_CHUNKS = NZ + 1 + 2
FF_AT = L_CHUNKS
L1_AT = L_CHUNKS + 3 * FF_STEPS
EX_AT = L1_AT + L_CHUNKS
EX_POS = {c: i for i, c in enumerate(ex_order())}
FF_POS = {c: FF_AT + i for i, c in enumerate(ff_order(FF_STEPS))}


def mixer_chunk(l, name):
    order = ["Z0", "Z1", "Z2", "LM", "Z3", "Z4", "Z5", "W0", "W1"]
    return (L1_AT if l else 0) + order.index(name)


def build(nc, w, out):
    chunks = plan_chunks(w)
    assert len(chunks) == EX_AT
    landed, fill = [], [0] * RING
    for n, loads in enumerate(chunks):
        fill[n % RING] += 16 * len(loads)
        landed.append(fill[n % RING])
    landed_ex = []
    for c in range(EX_CHUNKS):
        fill[(EX_AT + c) % RING] += 16
        landed_ex.append(fill[(EX_AT + c) % RING])
    EX_LAND = 16 * EX_CHUNKS // RING

    with ExitStack() as ctx:
        def sb(name, shape, dt=F32):
            return ctx.enter_context(nc.sbuf_tensor(name, shape, dt))

        def sem(name):
            return ctx.enter_context(nc.semaphore(name))

        ps = ctx.enter_context(nc.psum_tensor("ps", [P, 8, 512], F32))

        ring = sb("ring", [P, RING, SLOT])
        x = sb("x", [P, TILES, D_MODEL])
        hn = sb("hn", [P, TILES, D_MODEL])
        y = hn
        hT = sb("hT", [P, KC, SEQ])
        yT = hT
        z = sb("z", [P, TILES, IN_WIDTH])
        const = sb("const", [P, CONSTANTS.shape[1]])
        gains = sb("gains", [P, 2 * DEPTH, KC])
        g_lat = sb("g_lat", [P, DEPTH, 3])
        g_sub = sb("g_sub", [P, DEPTH])
        b_f = sb("b_f", [P, DEPTH, HEADS])
        lam_in = sb("lam_in", [P, 4, DEPTH, DIFF_QK])
        lam_s = sb("lam_s", [P, 2, DEPTH])
        lam_junk = sb("lam_junk", [P, DIFF_QK])
        neg_lam = sb("neg_lam", [P, DEPTH])
        w_r = sb("w_r", [P, KC, EXPERTS])
        sumsq = sb("sumsq", [P, 5, TILES])
        rstd = sb("rstd", [P, 5, TILES])
        half_neg = sb("half_neg", [P, 8])

        kA = sb("kA", [P, TILES, HEADS, QK_A])
        vA = sb("vA", [P, TILES, GROUP])
        tmp_a = sb("tmp_a", [P, 512])
        tmp_b = sb("tmp_b", [P, 512])
        qC = sb("qC", [P, TILES, HEADS, AUG])
        kC = sb("kC", [P, TILES, HEADS, AUG])
        wideT = sb("wideT", [P, 2, HEADS, SEQ])
        pairT = sb("pairT", [P, 2, 2, SEQ])
        E = sb("E", [P, 2, 1024])
        pT = sb("pT", [P, 2, 8, P])
        neg_max = sb("neg_max", [P, NJ, 8])
        row_sum = sb("row_sum", [P, NJ, 8])
        row_inv = sb("row_inv", [P, NJ, 8])
        lat_ss = sb("lat_ss", [P, TILES, 2])
        lat_r = sb("lat_r", [P, TILES, 2])
        fg = sb("fg", [P, 6, TILES, HEADS])
        c_sum = sb("c_sum", [P, TILES, HEADS])
        d_ss = sb("d_ss", [P, 8])
        d_r = sb("d_r", [P, 8])
        qA = z[:, :, 0:HEADS * QK_A]
        latn = E[:, :, :].rearrange("p a b -> p (a b)")[:, 0:TILES * 384].rearrange("p (t n) -> p t n", t=TILES)
        latT = pT[:, :, :, :].rearrange("p a b c -> p (a b c)")[:, 0:3 * SEQ].rearrange("p (c n) -> p c n", c=3)

        zf = z[:, :, :].rearrange("p t n -> p (t n)")
        at = [0]

        def over_z(n):
            at[0] += n
            assert at[0] <= TILES * IN_WIDTH
            return zf[:, at[0] - n:at[0]]

        ff_silu = over_z(1024)
        ff_act = over_z(1024).rearrange("p (q n) -> p q n", q=4)
        at[0] = 0
        sel = over_z(TILES * SLOTS).rearrange("p (t n) -> p t n", t=TILES)
        sel_g = over_z(TILES * SLOTS).rearrange("p (t n) -> p t n", t=TILES)
        sel_gT = over_z(SEQ)
        xgT = over_z(KC * SLOTS).rearrange("p (c n) -> p c n", c=KC)
        ex_silu = over_z(FW)
        ex_act = over_z(FW)
        ex_actT = over_z(4 * SLOTS).rearrange("p (q n) -> p q n", q=4)
        ex_out = over_z(D_MODEL)
        g_fin = over_z(D_MODEL)
        logits = sb("logits", [P, TILES, EXPERTS])
        top = sb("top", [P, TILES, 8])
        top_i = sb("top_i", [P, TILES, 8], U32)
        top_f = sb("top_f", [P, TILES, 8])
        route = sb("route", [P, 4, TILES])
        hot = sb("hot", [P, 4, TILES, EXPERTS])
        chosen = sb("chosen", [P, TILES, EXPERTS])
        place = sb("place", [P, TILES, ITEMS + 1])
        gate = sb("gate", [P, TILES, ITEMS + 1])
        most = sb("most", [P, 1])
        most_i = sb("most_i", [P, 1], I32)

        def cst(name):
            a, n = CONST[name]
            return const[:, a:a + n]

        ident, tri, ones = cst("ident"), cst("tri"), cst("ones")

        x_in = sem("x_in")
        small_in = sem("small_in")
        gfin_in = sem("gfin_in")
        slot_in = [sem(f"slot_in{i}") for i in range(RING)]
        chunk_done = sem("chunk_done")
        sq_done = sem("sq_done")
        rstd_done = sem("rstd_done")
        hn_done = sem("hn_done")
        hT_ps = sem("hT_ps")
        hT_done = sem("hT_done")
        x_done = sem("x_done")
        dve_c, act_c, pool_c = sem("dve_c"), sem("act_c"), sem("pool_c")
        lam_sum, lam_exp = sem("lam_sum"), sem("lam_exp")

        def per_layer(name):
            return [sem(f"{name}_{l}") for l in range(DEPTH)]

        z_ps = per_layer("z_ps")
        z_done = per_layer("z_done")
        lat_sq = per_layer("lat_sq")
        lat_rs = per_layer("lat_rs")
        lat_done = per_layer("lat_done")
        lm_ps = per_layer("lm_ps")
        uq_done = per_layer("uq_done")
        ukv_done = per_layer("ukv_done")
        rope_done = per_layer("rope_done")
        bt_ps = per_layer("bt_ps")
        bt_done = per_layer("bt_done")
        f_in = per_layer("f_in")
        f_log = per_layer("f_log")
        lf_done = per_layer("lf_done")
        aug_done = per_layer("aug_done")
        c_done = per_layer("c_done")
        s_ps = per_layer("s_ps")
        mask_done = per_layer("mask_done")
        max_done = per_layer("max_done")
        exp_done = per_layer("exp_done")
        comb_done = per_layer("comb_done")
        pt_ps = per_layer("pt_ps")
        pt_ev = per_layer("pt_ev")
        pv_ps = per_layer("pv_ps")
        y_done = per_layer("y_done")
        d_sq = per_layer("d_sq")
        d_rs = per_layer("d_rs")
        yd_done = per_layer("yd_done")
        w_ps = per_layer("w_ps")
        ff_sd = sem("ff_silu")
        ff_ad = sem("ff_act")
        logit_ps, top_done, route_exp, chosen_done = sem("logit_ps"), sem("top_done"), sem("route_exp"), sem("chosen_done")
        count_ps, count_done = sem("count_ps"), sem("count_done")
        sel_done = sem("sel_done")
        gather_ps = sem("gather_ps")
        xgT_done = sem("xgT_done")
        selT_ps = sem("selT_ps")
        selT_done = sem("selT_done")
        silu_done = sem("silu_done")
        act_done = sem("act_done")
        actT_ps = sem("actT_ps")
        actT_done = sem("actT_done")
        eo_done = sem("eo_done")
        scatter_ps = sem("scatter_ps")
        y_added = sem("y_added")
        x_final = sem("x_final")
        out_ready = sem("out_ready")
        stored = sem("stored")

        block = ctx.enter_context(nc.Block())

        def bc(ap, axis, shape):
            return ap.unsqueeze(axis).to_broadcast(shape)

        def slot_view(n, first, shape):
            a, b = shape
            return ring[:, n % RING, first:first + a * b].rearrange("p (a b) -> p a b", a=a)

        def score_places(k):
            g, _, n, _, _ = JOBS[k]
            banks = ps[:, 2 if g == "D" else 4:6, :]
            return banks.rearrange("p a b -> p (a b)").rearrange("p (s n) -> p s n", s=n)

        def xcols(h):
            return slice(h * 512, (h + 1) * 512)

        @block.sync
        def _(sp):
            def load(n):
                if n >= RING:
                    sp.wait_ge(chunk_done, n - RING + 1)
                for first, shape, src in chunks[n]:
                    sp.dma_start(slot_view(n, first, shape), src).then_inc(slot_in[n % RING], 16)

            sp.dma_start(x[:, :, :], w["x"][0].rearrange("(t p) d -> p t d", p=P)).then_inc(x_in, 16)
            for n in range(EX_AT):
                load(n)

            gate_w = w["w_exp_gate"].rearrange("l e (c p) f -> p (l e c) f", p=P)
            up_w = w["w_exp_up"].rearrange("l e (c p) f -> p (l e c) f", p=P)
            down_w = w["w_exp_down"].rearrange("l e (q p) d -> p (l e q) d", p=P)
            FQ = D_FF_EXPERT // P

            def expert_items(first):
                with sp.Fori(first, first + EXPERTS) as i:
                    e = i - first
                    for (kind, s), c in EX_POS.items():
                        n = EX_AT + c
                        sp.wait_ge(chunk_done, i * EX_CHUNKS + (n - RING + 1))
                        if kind == "d":
                            dst = slot_view(n, 0, (4, D_MODEL))
                            src = down_w[:, bass.ds(e * FQ + 4 * s, 4), :]
                        else:
                            dst = slot_view(n, 0, (KC, FW))
                            src = (gate_w if kind == "g" else up_w)[:, bass.ds(e * KC, KC), s * FW:(s + 1) * FW]
                        sp.dma_start(dst, src).then_inc(slot_in[n % RING], 16)

            expert_items(0)
            sp.wait_ge(count_done, 1)
            count = sp.value_load(most_i[0:1, 0:1], min_val=0, max_val=SEQ)
            with sp.If(count > SLOTS):
                expert_items(EXPERTS)
            for t in range(TILES):
                sp.wait_ge(out_ready, t + 1)
                sp.dma_start(out[0].rearrange("(t p) d -> p t d", p=P)[:, t, :], x[:, t, :]).then_inc(stored, 16)
            sp.wait_ge(stored, 16 * TILES)

        @block.gpsimd
        def _(pool):
            links = [0]

            def link(ins):
                links[0] += 1
                ins.then_inc(pool_c, 1)
                pool.wait_ge(pool_c, links[0])

            def rsqrt_mean(dst, src, n, width, signal):
                link(pool.tensor_scalar(dst, src, 1.0 / n, EPS, ALU.mult, ALU.add))
                pool.tensor_tensor(dst, dst, half_neg[:, 0:width], ALU.pow).then_inc(signal, 1)

            def norm(n):
                pool.wait_ge(sq_done, TILES * (n + 1))
                rsqrt_mean(rstd[:, n, :], sumsq[:, n, :], D_MODEL, TILES, rstd_done)

            def mixer(l):
                norm(2 * l)
                pool.wait_ge(lat_sq[l], 1)
                link(pool.tensor_scalar(lat_r[:, :, 0], lat_ss[:, :, 0], 1.0 / Q_RANK, EPS, ALU.mult, ALU.add))
                link(pool.tensor_scalar(lat_r[:, :, 1], lat_ss[:, :, 1], 1.0 / KV_RANK, EPS, ALU.mult, ALU.add))
                flat = lat_r[:, :, :].rearrange("p a b -> p (a b)")
                pool.tensor_tensor(flat, flat, half_neg[:, 0:4], ALU.pow).then_inc(lat_rs[l], 1)
                pool.wait_ge(z_done[l], 2 * 4)
                for t in range(TILES):
                    q = z[:, t, QCOL:QCOL + GROUP].rearrange("p (h d) -> p h d", h=HEADS)
                    k = z[:, t, KCOL:KCOL + GROUP].rearrange("p (h d) -> p h d", h=HEADS)
                    pool.tensor_scalar(qC[:, t, :, 0:HEAD_DIM], q, HEAD_DIM ** -0.5, None, ALU.mult).then_inc(aug_done[l], 1)
                    pool.tensor_copy(kC[:, t, :, 0:HEAD_DIM], k).then_inc(aug_done[l], 1)
                pool.wait_ge(d_sq[l], 1)
                rsqrt_mean(d_r[:, :], d_ss[:, :], HEAD_DIM, 8, d_rs[l])

            link(pool.memset(half_neg[:, :], -0.5))
            for l in range(DEPTH):
                mixer(l)
                norm(2 * l + 1)
            norm(2 * DEPTH)

        @block.scalar
        def _(act):
            loads = [(const[:, :], w["const"]),
                     (w_r[:, :, :], w["w_router"][0].rearrange("(c p) e -> p c e", p=P))]
            for l in range(DEPTH):
                for half in range(2):
                    loads.append((g_sub[half * HEAD_DIM:(half + 1) * HEAD_DIM, l:l + 1],
                                  w["g_diff_sub"][l].rearrange("(p o) -> p o", o=1)))
                loads += [(gains[:, 2 * l, :], w["g_mix"][l].rearrange("(c p) -> p c", p=P)),
                          (gains[:, 2 * l + 1, :], w["g_ffn"][l].rearrange("(c p) -> p c", p=P)),
                          (g_lat[:, l, 0:2], w["g_q_lat"][l].rearrange("(c p) -> p c", p=P)),
                          (g_lat[:, l, 2:3], w["g_kv_lat"][l].rearrange("(c p) -> p c", p=P)),
                          (b_f[:, l, :], w["b_forget"][l].partition_broadcast(P))]
                for i, name in enumerate(("lambda_q1", "lambda_k1", "lambda_q2", "lambda_k2")):
                    loads.append((lam_in[:, i, l, :], w[name][l].partition_broadcast(P)))
            assert 16 * len(loads) == SMALL_IN
            for dst, src in loads:
                act.dma_start(dst, src).then_inc(small_in, 16)

            links = [0]

            def link(ins):
                links[0] += 1
                ins.then_inc(act_c, 1)
                act.wait_ge(act_c, links[0])

            def squares(n, t):
                act.activation(hn[:, t, :], x[:, t, :], ACT.Square, accum_out=sumsq[:, n, t:t + 1]).then_inc(sq_done, 1)

            def norm(n):
                for t in range(TILES):
                    if n == 0:
                        act.wait_ge(x_in, 16)
                    else:
                        act.wait_ge(x_done, 2 * (n - 1) + t + 1)
                    squares(n, t)
                act.wait_ge(rstd_done, n + 1)
                act.wait_ge(sq_done, TILES * (n + 1))
                for t in range(TILES):
                    act.activation(hn[:, t, :], x[:, t, :], ACT.Copy, scale=rstd[:, n, t:t + 1]).then_inc(hn_done, 1)

            def mixer(l):
                def z_chunk(c):
                    a, b = Z_CUTS[c], Z_CUTS[c + 1]
                    for t in range(TILES):
                        if t == 0:
                            act.wait_ge(z_ps[l], c + 1)
                        else:
                            act.wait_ge(chunk_done, mixer_chunk(l, f"Z{c}") + 1)
                        act.activation(z[:, t, a:b], ps[:, 2 + t, 0:b - a], ACT.Copy).then_inc(z_done[l], 1)

                def exps(k):
                    act.wait_ge(max_done[l], k + 1)
                    _, _, n, _, nk = JOBS[k]
                    for s in range(n):
                        e = E[:, k % 2, s * nk:(s + 1) * nk]
                        ins = act.activation(e, e, ACT.Exp, bias=neg_max[:, k, s:s + 1],
                                             accum_out=row_sum[:, k, s:s + 1])
                    ins.then_inc(exp_done[l], 1)

                def pt_copy(k):
                    for b in range(pt_batches(k)):
                        act.wait_ge(pt_ps[l], pt_done(k) - pt_batches(k) + b + 1)
                        act.activation(pT[:, k % 2, 4 * b:4 * b + 4, :],
                                       ps[:, 7, :].rearrange("p (b n) -> p b n", b=4),
                                       ACT.Copy).then_inc(pt_ev[l], 1)

                norm(2 * l)
                for step in MIXER:
                    if step[0] == "Z":
                        z_chunk(int(step[1]))
                    elif step == "LM":
                        for t in range(TILES):
                            if t == 0:
                                act.wait_ge(lm_ps[l], 2)
                            else:
                                act.wait_ge(chunk_done, mixer_chunk(l, "LM") + 1)
                            kv = ps[:, 7, :].rearrange("p (h d) -> p h d", h=HEADS)
                            act.activation(kA[:, t, :, 0:NOPE], kv[:, :, 0:NOPE], ACT.Copy)
                            act.activation(vA[:, t, :].rearrange("p (h d) -> p h d", h=HEADS),
                                           kv[:, :, NOPE:], ACT.Copy).then_inc(ukv_done[l], 1)
                    elif step == "CS":
                        act.wait_ge(f_in[l], 1)
                        link(act.activation(fg[:, 3], fg[:, 2], ACT.Exp))
                        act.activation(fg[:, 4], fg[:, 3], ACT.Ln, bias=1.0).then_inc(f_log[l], 1)
                    elif step[0] == "J":
                        k = int(step[1:])
                        if 1 <= k <= NJ:
                            pt_copy(k - 1)
                        if k < NJ:
                            exps(k)

            def dense_ff():
                for s in range(FF_STEPS):
                    nq = min(4, (D_FF - s * FW) // P)
                    act.wait_ge(chunk_done, FF_POS[("g", s)] + 1)
                    if s:
                        act.wait_ge(ff_ad, s)
                    act.activation(ff_silu[:, 0:nq * SEQ].rearrange("p (b n) -> p b n", n=512),
                                   ps[:, 0:nq // 2, :], ACT.Silu).then_inc(ff_sd, 1)

            def expert_items(first):
                with act.Fori(first, first + EXPERTS) as i:
                    def silu(j):
                        act.wait_ge(chunk_done, i * EX_CHUNKS + (EX_AT + EX_POS[("g", j)] + 1))
                        if j:
                            act.wait_ge(act_done, i * EX_STEPS + j)
                        act.activation(ex_silu, ps[:, 0, :], ACT.Silu).then_inc(silu_done, 1)

                    def copyT(j):
                        act.wait_ge(actT_ps, i * EX_STEPS + (j + 1))
                        act.activation(ex_actT, ps[:, 4, :].rearrange("p (q n) -> p q n", q=4),
                                       ACT.Copy).then_inc(actT_done, 1)

                    silu(0)
                    for j in range(1, EX_STEPS):
                        silu(j)
                        copyT(j - 1)
                    copyT(EX_STEPS - 1)
                    act.wait_ge(chunk_done, i * EX_CHUNKS + (EX_AT + EX_CHUNKS))
                    for h in range(2):
                        act.activation(ex_out[:, xcols(h)], ps[:, 2 + h, :], ACT.Copy).then_inc(eo_done, 1)
                    copy_selT(i + 2)

            def copy_selT(n):
                act.wait_ge(selT_ps, n)
                act.activation(sel_gT, ps[:, 6, 0:SEQ], ACT.Copy).then_inc(selT_done, 1)

            act.wait_ge(small_in, SMALL_IN)
            act.wait_ge(lam_sum, 1)
            act.activation(lam_s[:, :, :], lam_s[:, :, :], ACT.Exp).then_inc(lam_exp, 1)
            for l in range(DEPTH):
                mixer(l)
                norm(2 * l + 1)
                if l == 0:
                    dense_ff()
            act.wait_ge(hT_done, 4 * 4)
            act.dma_start(g_fin, w["g_final"].partition_broadcast(P)).then_inc(gfin_in, 16)
            act.wait_ge(top_done, 1)
            act.activation(route[:, 1, :], route[:, 0, :], ACT.Exp).then_inc(route_exp, 1)
            copy_selT(1)
            expert_items(0)
            act.wait_ge(count_done, 1)
            count = act.value_load(most_i[0:1, 0:1], min_val=0, max_val=SEQ)
            with act.If(count > SLOTS):
                expert_items(EXPERTS)
            act.wait_ge(x_final, 1)
            for t in range(TILES):
                squares(2 * DEPTH, t)

        @block.vector
        def _(dve):
            links = [0]

            def link(ins):
                links[0] += 1
                ins.then_inc(dve_c, 1)
                dve.wait_ge(dve_c, links[0])

            def norm_T(n):
                for b in range(4):
                    t, half = divmod(b, 2)
                    dve.wait_ge(hT_ps, 4 * n + b + 1)
                    g = bc(gains[:, n, 4 * half:4 * half + 4], 2, [P, 4, P])
                    dve.tensor_tensor(hT[:, 4 * half:4 * half + 4, t * P:(t + 1) * P],
                                      ps[:, b % 2, :].rearrange("p (c n) -> p c n", c=4), g,
                                      ALU.mult).then_inc(hT_done, 1)

            def rope(v, n, half, t):
                a = tmp_a[:, 0:n * 2 * half].rearrange("p (h i d) -> p h i d", h=n, i=2)
                b = tmp_b[:, 0:n * 2 * half].rearrange("p (h i d) -> p h i d", h=n, i=2)
                for i in range(2):
                    dve.tensor_tensor(a[:, :, i, :], v[:, :, i, :],
                                      bc(cst(f"cos{half}_{t}"), 1, [P, n, half]), ALU.mult)
                dve.tensor_tensor(b[:, :, 0, :], v[:, :, 1, :],
                                  bc(cst(f"nsin{half}_{t}"), 1, [P, n, half]), ALU.mult)
                link(dve.tensor_tensor(b[:, :, 1, :], v[:, :, 0, :],
                                       bc(cst(f"sin{half}_{t}"), 1, [P, n, half]), ALU.mult))
                return dve.tensor_tensor(v, a, b, ALU.add)

            def mixer(l):
                def batch(b):
                    dve.wait_ge(bt_ps[l], b + 1)
                    return ps[:, b % 2, :]

                def latents():
                    dve.wait_ge(z_done[l], 2)
                    for t in range(TILES):
                        for i, (a, n) in enumerate(((CQ, Q_RANK), (CKV, KV_RANK))):
                            link(dve.tensor_tensor(tmp_a[:, 0:n], z[:, t, a:a + n], z[:, t, a:a + n], ALU.mult))
                            ins = dve.tensor_reduce(lat_ss[:, t, i:i + 1], tmp_a[:, 0:n], AX.X, ALU.add)
                            if (t, i) != (TILES - 1, 1):
                                link(ins)
                    ins.then_inc(lat_sq[l], 1)
                    dve.wait_ge(lat_sq[l], 1)
                    for t in range(TILES):
                        kr = z[:, t, KR:KR + ROT].rearrange("p (h i d) -> p h i d", h=1, i=2)
                        link(rope(kr, 1, ROT // 2, t))
                        link(dve.tensor_copy(kA[:, t, :, NOPE:],
                                             bc(z[:, t, KR:KR + ROT], 1, [P, HEADS, ROT])))
                    dve.wait_ge(lat_rs[l], 1)
                    for t in range(TILES):
                        dve.tensor_scalar(latn[:, t, 0:Q_RANK], z[:, t, CQ:CQ + Q_RANK],
                                          lat_r[:, t, 0:1], None, ALU.mult)
                        dve.tensor_scalar(latn[:, t, Q_RANK:], z[:, t, CKV:CKV + KV_RANK],
                                          lat_r[:, t, 1:2], None, ALU.mult).then_inc(lat_done[l], 1)
                    dve.wait_ge(lat_done[l], 2)

                def rope_qk(first, n, half):
                    for t in range(TILES):
                        v = z[:, t, first:first + 2 * GROUP].rearrange("p (h i d) -> p h i d", h=n, i=2)
                        ins = rope(v, n, half, t)
                        ins.then_inc(rope_done[l], 1)
                        ropes[0] += 1
                        dve.wait_ge(rope_done[l], ropes[0])

                def forget():
                    f = z[:, :, FCOL:FCOL + HEADS]
                    link(dve.tensor_tensor(fg[:, 0], f, bc(b_f[:, l, :], 1, [P, TILES, HEADS]), ALU.add))
                    link(dve.tensor_scalar(fg[:, 1], fg[:, 0], 0.0, None, ALU.min))
                    link(dve.tensor_scalar(fg[:, 2], fg[:, 0], 0.0, None, ALU.max))
                    link(dve.tensor_tensor(fg[:, 2], fg[:, 1], fg[:, 2], ALU.subtract))
                    dve.sem_inc(f_in[l], 1)
                    dve.wait_ge(f_log[l], 1)
                    dve.tensor_tensor(fg[:, 5], fg[:, 1], fg[:, 4], ALU.subtract).then_inc(lf_done[l], 1)

                def mask(k):
                    g, t, n, _, nk = JOBS[k]
                    dve.wait_ge(s_ps[l], k + 1)
                    m = cst("dilated" if g == "B" else "causal")[:, SEQ - nk:]
                    e = E[:, k % 2, 0:n * nk].rearrange("p (s n) -> p s n", s=n)
                    s = score_places(k)[:, :, 0:nk]
                    dve.scalar_tensor_tensor(e, s, SCALE[g], bc(m, 1, [P, n, nk]), ALU.mult,
                                             ALU.add).then_inc(mask_done[l], 1)
                    dve.wait_ge(mask_done[l], k + 1)
                    dve.tensor_reduce(neg_max[:, k, 0:n], e, AX.X, ALU.max, negate=True).then_inc(max_done[l], 1)

                def combine(k):
                    _, _, n, _, nk = JOBS[k]
                    dve.wait_ge(exp_done[l], k + 1)
                    link(dve.reciprocal(row_inv[:, k, 0:n], row_sum[:, k, 0:n]))
                    r = row_inv[:, k, 0:n].rearrange("p (m i r) -> p m i r", m=2, i=2)
                    link(dve.tensor_scalar(r[:, :, 1], r[:, :, 1], neg_lam[:, l:l + 1], None, ALU.mult))
                    e = E[:, k % 2, 0:n * nk].rearrange("p (s n) -> p s n", s=n)
                    link(dve.tensor_tensor(e, e, bc(row_inv[:, k, 0:n], 2, [P, n, nk]), ALU.mult))
                    e = E[:, k % 2, 0:n * nk].rearrange("p (m i r) -> p m i r", m=2, i=2)
                    dve.tensor_tensor(e[:, :, 0, :], e[:, :, 0, :], e[:, :, 1, :], ALU.add).then_inc(comb_done[l], 1)

                def output(k):
                    g, t, n, s0, _ = JOBS[k]
                    nh = n // 2 if g == "D" else n
                    c0 = YCOL[g] + (s0 // 2) * HEAD_DIM
                    o = ps[:, 6, 0:nh * HEAD_DIM]
                    dst = y[:, t, c0:c0 + nh * HEAD_DIM]
                    if g != "D":
                        dve.wait_ge(exp_done[l], k + 1)
                        link(dve.reciprocal(row_inv[:, k, 0:n], row_sum[:, k, 0:n]))
                    dve.wait_ge(pv_ps[l], k + 1)
                    if g == "D":
                        ins = dve.tensor_copy(dst, o)
                    elif g == "B":
                        ins = dve.tensor_tensor(dst.rearrange("p (b a d) -> p a b d", a=2, b=2),
                                                o.rearrange("p (b a d) -> p a b d", a=2, b=2),
                                                bc(row_inv[:, k, 0:4].rearrange("p (a b) -> p a b", a=2), 3,
                                                   [P, 2, 2, HEAD_DIM]), ALU.mult)
                    else:
                        ins = dve.tensor_tensor(dst.rearrange("p (h d) -> p h d", h=nh),
                                                o.rearrange("p (h d) -> p h d", h=nh),
                                                bc(row_inv[:, k, 0:nh], 2, [P, nh, HEAD_DIM]), ALU.mult)
                    ins.then_inc(y_done[l], 1)

                ropes = [0]
                norm_T(2 * l)
                for step in MIXER:
                    if step == "Z0":
                        latents()
                    elif step == "Z1":
                        dve.wait_ge(z_done[l], 4)
                        rope_qk(QB, 2 * HEADS, HEAD_DIM // 2)
                    elif step == "LT":
                        for t, b in enumerate(BATCH["LT"]):
                            src = batch(b)[:, 0:3 * P].rearrange("p (c n) -> p c n", c=3)
                            dve.tensor_tensor(latT[:, :, t * P:(t + 1) * P], src,
                                              bc(g_lat[:, l, :], 2, [P, 3, P]), ALU.mult).then_inc(bt_done[l], 1)
                    elif step == "LM":
                        for t in range(TILES):
                            dve.wait_ge(lm_ps[l], 2 * t + 1)
                            dve.tensor_copy(qA[:, t, :], ps[:, 6, 0:HEADS * QK_A]).then_inc(uq_done[l], 1)
                        dve.wait_ge(uq_done[l], 2)
                        for t in range(TILES):
                            v = qA[:, t, :].rearrange("p (h d) -> p h d", h=HEADS)[:, :, NOPE:]
                            ins = rope(v.rearrange("p h (i d) -> p h i d", i=2), HEADS, ROT // 2, t)
                            ins.then_inc(rope_done[l], 1)
                            ropes[0] += 1
                            dve.wait_ge(rope_done[l], ropes[0])
                    elif step in ("QB", "QD"):
                        if step == "QD":
                            rope_qk(QD, 4 * HEADS, DIFF_QK // 2)
                        for t, b in enumerate(BATCH[step]):
                            src = batch(b).rearrange("p (a h n) -> p a h n", a=2, h=2)
                            dve.tensor_copy(pairT[:, :, :, t * P:(t + 1) * P], src).then_inc(bt_done[l], 1)
                    elif step in ("QA", "QC"):
                        rows = QK_A if step == "QA" else AUG
                        for i, b in enumerate(BATCH[step]):
                            t, qk = divmod(i, 2)
                            src = batch(b)[0:rows, :].rearrange("p (h n) -> p h n", h=HEADS)
                            dve.tensor_copy(wideT[0:rows, qk, :, t * P:(t + 1) * P], src).then_inc(bt_done[l], 1)
                    elif step == "CS":
                        dve.wait_ge(z_done[l], 2 * NZ)
                        forget()
                        dve.memset(qC[:, :, :, HEAD_DIM + 1:AUG], 1.0)
                        dve.memset(kC[:, :, :, HEAD_DIM:HEAD_DIM + 1], 1.0)
                        src = batch(BATCH["CS"][0])[:, 0:TILES * HEADS].rearrange("p (t h) -> p t h", t=TILES)
                        dve.tensor_copy(qC[:, :, :, HEAD_DIM], src)
                        dve.tensor_scalar(kC[:, :, :, HEAD_DIM + 1], src, -1.0, None, ALU.mult).then_inc(bt_done[l], 1)
                    elif step[0] == "J":
                        k = int(step[1:])
                        if k < NJ:
                            mask(k)
                        if FIRST_D <= k - 1 < NJ:
                            combine(k - 1)
                        if k >= 2:
                            output(k - 2)

                dve.wait_ge(y_done[l], NJ)
                yd = y[:, :, 3 * GROUP:].rearrange("p t (h d) -> p t h d", h=HEADS)
                sq = tmp_a[:, :].rearrange("p (t h d) -> p t h d", t=TILES, h=HEADS)
                link(dve.tensor_tensor(sq, yd, yd, ALU.mult))
                dve.tensor_reduce(d_ss[:, :], tmp_a[:, :].rearrange("p (h d) -> p h d", h=8), AX.X,
                                  ALU.add).then_inc(d_sq[l], 1)
                dve.wait_ge(d_rs[l], 1)
                for t in range(TILES):
                    v = yd[:, t]
                    dve.tensor_tensor(v, v, bc(d_r[:, 4 * t:4 * t + 4], 2, [P, HEADS, HEAD_DIM]),
                                      ALU.mult).then_inc(yd_done[l], 1)
                lam_init = 0.8 - 0.6 * math.exp(-0.3 * l)
                for i, b in enumerate(BATCH["YT"]):
                    t, half = divmod(i, 2)
                    src = batch(b).rearrange("p (c n) -> p c n", c=4)
                    tok = slice(t * P, (t + 1) * P)
                    if half == 0:
                        dve.tensor_copy(yT[:, 0:4, tok], src).then_inc(bt_done[l], 1)
                    else:
                        dve.tensor_copy(yT[:, 4:6, tok], src[:, 0:2])
                        dve.tensor_scalar(yT[:, 6:8, tok], src[:, 2:4], g_sub[:, l:l + 1],
                                          1.0 - lam_init, ALU.mult, ALU.mult).then_inc(bt_done[l], 1)
                for h in range(2):
                    for t in range(TILES):
                        if t == 0:
                            dve.wait_ge(w_ps[l], h + 1)
                        else:
                            dve.wait_ge(chunk_done, mixer_chunk(l, f"W{h}") + 1)
                        ins = dve.tensor_tensor(x[:, t, xcols(h)], x[:, t, xcols(h)], ps[:, W_BANK[h][t], :], ALU.add)
                        if h == 1:
                            ins.then_inc(x_done, 1)

            def dense_ff():
                for s in range(FF_STEPS):
                    nq = min(4, (D_FF - s * FW) // P)
                    dve.wait_ge(ff_sd, s + 1)
                    dve.wait_ge(chunk_done, FF_POS[("u", s)] + 1)
                    dve.tensor_tensor(ff_act[:, 0:nq, :].rearrange("p (b q) n -> p b (q n)", q=2),
                                      ff_silu[:, 0:nq * SEQ].rearrange("p (b n) -> p b n", n=512),
                                      ps[:, 2:2 + nq // 2, :], ALU.mult).then_inc(ff_ad, 1)
                dve.wait_ge(chunk_done, FF_POS[("d", FF_STEPS - 1)] + 1)
                dve.wait_ge(x_done, 2)
                for t in range(TILES):
                    dve.tensor_tensor(x[:, t, :], x[:, t, :],
                                      ps[:, 4 + 2 * t:6 + 2 * t, :].rearrange("p a b -> p (a b)"),
                                      ALU.add).then_inc(x_done, 1)

            def router():
                dve.wait_ge(logit_ps, 1)
                link(dve.tensor_copy(logits[:, :, :].rearrange("p t e -> p (t e)"), ps[:, 0, 0:TILES * EXPERTS]))
                for t in range(TILES):
                    link(dve.max(top[:, t, :], logits[:, t, :]))
                    link(dve.max_index(top_i[:, t, :], top[:, t, :], logits[:, t, :]))
                link(dve.tensor_copy(top_f[:, :, :], top_i[:, :, :]))
                dve.tensor_tensor(route[:, 0, :], top[:, :, 1], top[:, :, 0], ALU.subtract).then_inc(top_done, 1)
                dve.wait_ge(route_exp, 1)
                link(dve.tensor_scalar(route[:, 2, :], route[:, 1, :], 1.0, None, ALU.add))
                link(dve.reciprocal(route[:, 2, :], route[:, 2, :]))
                link(dve.tensor_tensor(route[:, 3, :], route[:, 1, :], route[:, 2, :], ALU.mult))
                iota8 = cst("iota")[:, 0:EXPERTS]
                for t in range(TILES):
                    for r in range(2):
                        idx = top_f[:, t, r:r + 1]
                        link(dve.tensor_scalar(hot[:, r, t, :], iota8, idx, None, ALU.is_equal))
                        link(dve.tensor_scalar(hot[:, 2 + r, t, :], iota8, idx, route[:, 2 + r, t:t + 1],
                                               ALU.is_equal, ALU.mult))
                dve.tensor_tensor(chosen[:, :, :], hot[:, 0], hot[:, 1], ALU.add).then_inc(chosen_done, 1)
                link(dve.memset(gate[:, :, :], 0.0))
                link(dve.memset(place[:, :, :], -1.0))
                for r in range(ITEMS // EXPERTS):
                    link(dve.tensor_tensor(gate[:, :, r * EXPERTS:(r + 1) * EXPERTS], hot[:, 2], hot[:, 3], ALU.add))
                dve.wait_ge(count_ps, 1)
                dve.wait_ge(chosen_done, 1)
                rank = ps[:, 1, 0:TILES * EXPERTS].rearrange("p (t e) -> p t e", t=TILES)
                link(dve.tensor_tensor(place[:, :, 0:EXPERTS], rank, chosen[:, :, :], ALU.mult))
                link(dve.tensor_scalar(place[:, :, 0:EXPERTS], place[:, :, 0:EXPERTS], -1.0, None, ALU.add))
                for r in range(1, ITEMS // EXPERTS):
                    link(dve.tensor_scalar(place[:, :, r * EXPERTS:(r + 1) * EXPERTS], place[:, :, 0:EXPERTS],
                                           -float(r * SLOTS), None, ALU.add))
                link(dve.tensor_reduce(most[:, :], ps[:, 1, 16:16 + EXPERTS], AX.X, ALU.max))
                dve.tensor_copy(most_i[:, :], most[:, :]).then_inc(count_done, 1)
                dve.sem_inc(y_added, 4)

            def select(i, n):
                for t in range(TILES):
                    p_i = place[:, t, bass.ds(i, 1)]
                    dve.tensor_scalar(sel[:, t, :], cst("iota")[:, 0:SLOTS], p_i, None, ALU.is_equal)
                    ins = dve.tensor_scalar(sel_g[:, t, :], cst("iota")[:, 0:SLOTS], p_i,
                                            gate[:, t, bass.ds(i, 1)], ALU.is_equal, ALU.mult)
                ins.then_inc(sel_done, 1)

            def gathered(n):
                dve.wait_ge(gather_ps, n)
                dve.tensor_tensor(xgT, ps[:, 6:8, :].rearrange("p a (c n) -> p (a c) n", n=SLOTS),
                                  bc(gains[:, 3, :], 2, [P, KC, SLOTS]), ALU.mult).then_inc(xgT_done, 1)

            def expert_items(first):
                with dve.Fori(first, first + EXPERTS) as i:
                    for j in range(EX_STEPS):
                        dve.wait_ge(silu_done, i * EX_STEPS + (j + 1))
                        dve.wait_ge(chunk_done, i * EX_CHUNKS + (EX_AT + EX_POS[("u", j)] + 1))
                        dve.tensor_tensor(ex_act, ex_silu, ps[:, 1, :], ALU.mult).then_inc(act_done, 1)
                        if j == 0:
                            dve.wait_ge(selT_ps, i + 1)
                            select(i + 1, i + 2)
                    gathered(i + 2)
                    for q in range(4):
                        t, h = divmod(q, 2)
                        dve.wait_ge(scatter_ps, i * 4 + (q + 1))
                        dve.wait_ge(y_added, i * 4 + (q + 1))
                        dve.tensor_tensor(x[:, t, xcols(h)], x[:, t, xcols(h)], ps[:, SCATTER[q], :],
                                          ALU.add).then_inc(y_added, 1)

            dve.wait_ge(small_in, SMALL_IN)
            for i in range(2):
                for l in range(DEPTH):
                    link(dve.tensor_tensor(lam_junk[:, :], lam_in[:, 2 * i, l, :], lam_in[:, 2 * i + 1, l, :], ALU.mult))
                    link(dve.tensor_reduce(lam_s[:, i, l:l + 1], lam_junk[:, :], AX.X, ALU.add))
            dve.sem_inc(lam_sum, 1)
            dve.wait_ge(lam_exp, 1)
            link(dve.tensor_tensor(neg_lam[:, :], lam_s[:, 1, :], lam_s[:, 0, :], ALU.subtract))
            for l in range(DEPTH):
                link(dve.tensor_scalar(neg_lam[:, l:l + 1], neg_lam[:, l:l + 1],
                                       -(0.8 - 0.6 * math.exp(-0.3 * l)), None, ALU.add))
            for l in range(DEPTH):
                mixer(l)
                norm_T(2 * l + 1)
                if l == 0:
                    dense_ff()
            router()
            dve.wait_ge(count_done, 1)
            select(0, 1)
            gathered(1)
            expert_items(0)
            dve.wait_ge(y_added, 4 + 4 * EXPERTS)
            count = dve.value_load(most_i[0:1, 0:1], min_val=0, max_val=SEQ)
            with dve.If(count > SLOTS):
                expert_items(EXPERTS)
                dve.wait_ge(y_added, 4 + 8 * EXPERTS)
            dve.sem_inc(x_final, 1)
            dve.wait_ge(rstd_done, 2 * DEPTH + 1)
            dve.wait_ge(gfin_in, 16)
            for t in range(TILES):
                dve.scalar_tensor_tensor(x[:, t, :], x[:, t, :], rstd[:, 2 * DEPTH, t:t + 1], g_fin,
                                         ALU.mult, ALU.mult).then_inc(out_ready, 1)

        @block.tensor
        def _(pe):
            def norm_T(n):
                for b in range(4):
                    t, half = divmod(b, 2)
                    pe.wait_ge(hn_done, TILES * n + t + 1)
                    if b >= 2:
                        pe.wait_ge(hT_done, 4 * n + b - 1)
                    for c in range(4):
                        k = 4 * half + c
                        ins = pe.transpose(ps[:, b % 2, c * P:(c + 1) * P],
                                           hn[:, t, k * P:(k + 1) * P], ident)
                    ins.then_inc(hT_ps, 1)

            def arrived(n):
                pe.wait_ge(slot_in[n % RING], landed[n])

            def mixer(l):
                def batch(b):
                    if b >= 2:
                        pe.wait_ge(bt_done[l], b - 1)
                    return ps[:, b % 2, :]

                def z_chunk(c):
                    n = mixer_chunk(l, f"Z{c}")
                    wid = Z_CUTS[c + 1] - Z_CUTS[c]
                    arrived(n)
                    w_c = slot_view(n, 0, (KC, wid))
                    for t in range(TILES):
                        if c:
                            pe.wait_ge(z_done[l], 2 * (c - 1) + t + 1)
                        for k in range(KC):
                            ins = pe.matmul(ps[:, 2 + t, 0:wid], hT[:, k, t * P:(t + 1) * P], w_c[:, k, :],
                                            start=(k == 0), stop=(k == KC - 1))
                        ins.then_inc(chunk_done if t else z_ps[l], 1)

                def values(g, kb, h):
                    if g == "A":
                        return vA[:, kb, h * HEAD_DIM:(h + 1) * HEAD_DIM]
                    c = {"B": VB, "C": VCOL, "D": VD}[g] + h * HEAD_DIM
                    return z[:, kb, c:c + HEAD_DIM]

                def scores(k):
                    g, t, n, s0, nk = JOBS[k]
                    pe.wait_ge(bt_done[l], NEED[g])
                    if k:
                        pe.wait_ge(mask_done[l], k)
                    if g == "D":
                        pe.wait_ge(z_done[l], 2 * NZ)
                    places = score_places(k)
                    for s in range(n):
                        if g in "AC":
                            rows = QK_A if g == "A" else AUG
                            q, kk = wideT[0:rows, 0, s, :], wideT[0:rows, 1, s, :]
                        elif g == "B":
                            r = 64 * (s % 2)
                            q, kk = pairT[r:r + 64, 0, s // 2, :], pairT[r:r + 64, 1, s // 2, :]
                        else:
                            u, r = divmod(s0 + s, 4)
                            q, kk = pairT[32 * r:32 * r + 32, 0, u, :], pairT[32 * r:32 * r + 32, 1, u, :]
                        ins = pe.matmul(places[:, spot(k, s), 0:nk], q[:, t * P:(t + 1) * P], kk[:, 0:nk],
                                        start=True, stop=True)
                    ins.then_inc(s_ps[l], 1)

                def transposed(k):
                    g, _, _, _, nk = JOBS[k]
                    pe.wait_ge(exp_done[l], k + 1)
                    if g == "D":
                        pe.wait_ge(comb_done[l], k - FIRST_D + 1)
                    for b, blocks in enumerate(head_blocks(k)):
                        done = pt_done(k) - pt_batches(k) + b
                        if done:
                            pe.wait_ge(pt_ev[l], done)
                        else:
                            pe.wait_ge(ukv_done[l], TILES)
                        for i, (s, kb, _) in enumerate(blocks):
                            ins = pe.transpose(ps[:, 7, i * P:(i + 1) * P],
                                               E[:, k % 2, s * nk + kb * P:s * nk + (kb + 1) * P], ident)
                        ins.then_inc(pt_ps[l], 1)

                def times_values(k):
                    g, _, n, s0, nk = JOBS[k]
                    nh = n // 2 if g == "D" else n
                    pe.wait_ge(pt_ev[l], pt_done(k))
                    if k:
                        pe.wait_ge(y_done[l], k)
                    else:
                        pe.wait_ge(uq_done[l], TILES)
                    pe.wait_ge(z_done[l], {"B": 6, "A": 6, "C": 8, "D": 12}[g])
                    for h in range(nh):
                        c = h * HEAD_DIM
                        for kb in range(nk // P):
                            ins = pe.matmul(ps[:, 6, c:c + HEAD_DIM], pT[:, k % 2, kb * nh + h, :],
                                            values(g, kb, s0 // 2 + h),
                                            start=(kb == 0), stop=(kb == nk // P - 1))
                    ins.then_inc(pv_ps[l], 1)

                norm_T(2 * l)
                pe.wait_ge(hT_done, 4 * 2 * l + 4)
                for step in MIXER:
                    if step[0] == "Z":
                        z_chunk(int(step[1]))
                    elif step == "LT":
                        for t, b in enumerate(BATCH["LT"]):
                            pe.wait_ge(lat_done[l], t + 1)
                            bank = batch(b)
                            for c in range(3):
                                ins = pe.transpose(bank[:, c * P:(c + 1) * P], latn[:, t, c * P:(c + 1) * P], ident)
                            ins.then_inc(bt_ps[l], 1)
                    elif step == "LM":
                        n = mixer_chunk(l, "LM")
                        arrived(n)
                        w_uq = slot_view(n, 0, (2, HEADS * QK_A))
                        w_ukv = slot_view(n, 2 * HEADS * QK_A, (1, 2 * GROUP))
                        for t in range(TILES):
                            tok = slice(t * P, (t + 1) * P)
                            pe.wait_ge(bt_done[l], t + 1)
                            if t:
                                pe.wait_ge(uq_done[l], t)
                            for c in range(2):
                                ins = pe.matmul(ps[:, 6, 0:HEADS * QK_A], latT[:, c, tok], w_uq[:, c, :],
                                                start=(c == 0), stop=(c == 1))
                            ins.then_inc(lm_ps[l], 1)
                            if t:
                                pe.wait_ge(ukv_done[l], t)
                            ins = pe.matmul(ps[:, 7, :], latT[:, 2, tok], w_ukv[:, 0, :], start=True, stop=True)
                            ins.then_inc(chunk_done if t else lm_ps[l], 1)
                    elif step in ("QB", "QD"):
                        first = QB if step == "QB" else QD
                        for t, b in enumerate(BATCH[step]):
                            pe.wait_ge(rope_done[l], (0 if step == "QB" else 4) + t + 1)
                            bank = batch(b)
                            for c in range(4):
                                ins = pe.transpose(bank[:, c * P:(c + 1) * P],
                                                   z[:, t, first + c * P:first + (c + 1) * P], ident)
                            ins.then_inc(bt_ps[l], 1)
                    elif step in ("QA", "QC"):
                        for i, b in enumerate(BATCH[step]):
                            t, qk = divmod(i, 2)
                            if step == "QA":
                                pe.wait_ge(rope_done[l], 2 + t + 1)
                                pe.wait_ge(ukv_done[l], t + 1)
                                src = (kA[:, t] if qk else qA[:, t, :].rearrange("p (h d) -> p h d", h=HEADS))
                                rows = QK_A
                            else:
                                pe.wait_ge(aug_done[l], 2 * TILES)
                                pe.wait_ge(bt_done[l], BATCH["CS"][0] + 1)
                                src, rows = (kC if qk else qC)[:, t], AUG
                            bank = batch(b)
                            for h in range(HEADS):
                                ins = pe.transpose(bank[0:rows, h * P:(h + 1) * P], src[:, h, :], ident)
                            ins.then_inc(bt_ps[l], 1)
                    elif step == "CS":
                        pe.wait_ge(lf_done[l], 1)
                        bank = batch(BATCH["CS"][0])
                        pe.matmul(bank[:, 0:HEADS], tri, fg[:, 5, 0, :], start=True, stop=True)
                        pe.matmul(bank[:, HEADS:2 * HEADS], ones, fg[:, 5, 0, :], start=True, stop=False)
                        pe.matmul(bank[:, HEADS:2 * HEADS], tri, fg[:, 5, 1, :], start=False,
                                  stop=True).then_inc(bt_ps[l], 1)
                    else:
                        k = int(step[1:])
                        if k < NJ:
                            scores(k)
                        if 1 <= k <= NJ:
                            transposed(k - 1)
                        if k >= 2:
                            times_values(k - 2)

                for i, b in enumerate(BATCH["YT"]):
                    t, half = divmod(i, 2)
                    pe.wait_ge(yd_done[l], t + 1)
                    bank = batch(b)
                    for c in range(4):
                        k = 4 * half + c
                        ins = pe.transpose(bank[:, c * P:(c + 1) * P], y[:, t, k * P:(k + 1) * P], ident)
                    ins.then_inc(bt_ps[l], 1)
                for h in range(2):
                    n = mixer_chunk(l, f"W{h}")
                    arrived(n)
                    w_h = slot_view(n, 0, (KC, FW))
                    for t in range(TILES):
                        pe.wait_ge(bt_done[l], BATCH["YT"][2 * t + 1] + 1)
                        for k in range(KC):
                            ins = pe.matmul(ps[:, W_BANK[h][t], :], yT[:, k, t * P:(t + 1) * P], w_h[:, k, :],
                                            start=(k == 0), stop=(k == KC - 1))
                        ins.then_inc(chunk_done if t else w_ps[l], 1)

            def dense_ff():
                pe.wait_ge(hT_done, 4 * 2)
                for (kind, s), n in FF_POS.items():
                    nq = min(4, (D_FF - s * FW) // P)
                    arrived(n)
                    if kind == "d":
                        pe.wait_ge(ff_ad, s + 1)
                        w_c = slot_view(n, 0, (nq, D_MODEL))
                        for q in range(nq):
                            for t in range(TILES):
                                for h in range(2):
                                    ins = pe.matmul(ps[:, 4 + 2 * t + h, :], ff_act[:, q, t * P:(t + 1) * P],
                                                    w_c[:, q, xcols(h)], start=(s == 0 and q == 0),
                                                    stop=(s == FF_STEPS - 1 and q == nq - 1))
                    else:
                        if kind == "g" and s:
                            pe.wait_ge(ff_sd, s)
                        w_c = slot_view(n, 0, (KC, nq * P))
                        first = 0 if kind == "g" else 2
                        for q in range(nq):
                            dst = ps[:, first + q // 2, (q % 2) * SEQ:(q % 2 + 1) * SEQ]
                            for k in range(KC):
                                ins = pe.matmul(dst, w_c[:, k, q * P:(q + 1) * P], hT[:, k, :],
                                                start=(k == 0), stop=(k == KC - 1))
                    ins.then_inc(chunk_done, 1)

            def router():
                pe.wait_ge(hT_done, 4 * 4)
                pe.wait_ge(small_in, SMALL_IN)
                for t in range(TILES):
                    for k in range(KC):
                        ins = pe.matmul(ps[:, 0, t * EXPERTS:(t + 1) * EXPERTS], hT[:, k, t * P:(t + 1) * P],
                                        w_r[:, k, :], start=(k == 0), stop=(k == KC - 1))
                ins.then_inc(logit_ps, 1)
                pe.wait_ge(chosen_done, 1)
                bank = ps[:, 1, :]
                pe.matmul(bank[:, 0:8], tri, chosen[:, 0, :], start=True, stop=True)
                for first, last in ((8, tri), (16, ones)):
                    pe.matmul(bank[:, first:first + 8], ones, chosen[:, 0, :], start=True, stop=False)
                    ins = pe.matmul(bank[:, first:first + 8], last, chosen[:, 1, :], start=False, stop=True)
                ins.then_inc(count_ps, 1)

            def gather(n):
                pe.wait_ge(sel_done, n)
                for c in range(KC):
                    for t in range(TILES):
                        ins = pe.matmul(ps[:, 6 + c // 4, (c % 4) * SLOTS:(c % 4 + 1) * SLOTS],
                                        hn[:, t, c * P:(c + 1) * P], sel[:, t, :],
                                        start=(t == 0), stop=(t == TILES - 1))
                ins.then_inc(gather_ps, 1)

            def turn_selection(n):
                pe.wait_ge(xgT_done, n)
                for t in range(TILES):
                    ins = pe.transpose(ps[:, 6, t * P:(t + 1) * P], sel_g[:, t, :], ident)
                ins.then_inc(selT_ps, 1)

            def expert_items(first):
                with pe.Fori(first, first + EXPERTS) as i:
                    def chunk(kind, j):
                        c = EX_POS[(kind, j)]
                        n = EX_AT + c
                        pe.wait_ge(slot_in[n % RING], i * EX_LAND + landed_ex[c])
                        return slot_view(n, 0, (4, D_MODEL) if kind == "d" else (KC, FW))

                    def product(kind, j):
                        w_c = chunk(kind, j)
                        bank = 0 if kind == "g" else 1
                        if j == 0:
                            pe.wait_ge(y_added, i * 4 + (bank + 1))
                        elif kind == "g":
                            pe.wait_ge(silu_done, i * EX_STEPS + j)
                        for k in range(KC):
                            ins = pe.matmul(ps[:, bank, :], xgT[:, k, :], w_c[:, k, :],
                                            start=(k == 0), stop=(k == KC - 1))
                        ins.then_inc(chunk_done, 1)

                    def turn(j):
                        pe.wait_ge(act_done, i * EX_STEPS + (j + 1))
                        if j == 0:
                            pe.wait_ge(y_added, i * 4 + 4)
                        else:
                            pe.wait_ge(actT_done, i * EX_STEPS + j)
                        for q in range(4):
                            ins = pe.transpose(ps[:, 4, q * P:(q + 1) * P], ex_act[:, q * P:(q + 1) * P], ident)
                        ins.then_inc(actT_ps, 1)

                    def down(j):
                        w_c = chunk("d", j)
                        pe.wait_ge(actT_done, i * EX_STEPS + (j + 1))
                        for q in range(4):
                            for h in range(2):
                                ins = pe.matmul(ps[:, 2 + h, :], ex_actT[:, q, :], w_c[:, q, xcols(h)],
                                                start=(j == 0 and q == 0), stop=(j == EX_STEPS - 1 and q == 3))
                        ins.then_inc(chunk_done, 1)

                    pe.wait_ge(xgT_done, i + 1)
                    for j in range(EX_STEPS):
                        product("g", j)
                        if j:
                            turn(j - 1)
                        product("u", j)
                        if j:
                            down(j - 1)
                    turn(EX_STEPS - 1)
                    down(EX_STEPS - 1)
                    pe.wait_ge(selT_done, i + 1)
                    gather(i + 2)
                    for q in range(4):
                        t, h = divmod(q, 2)
                        pe.wait_ge(eo_done, i * 2 + (h + 1))
                        pe.matmul(ps[:, SCATTER[q], :], sel_gT[:, t * P:(t + 1) * P], ex_out[:, xcols(h)],
                                  start=True, stop=True).then_inc(scatter_ps, 1)
                    turn_selection(i + 2)

            pe.wait_ge(small_in, SMALL_IN)
            for l in range(DEPTH):
                mixer(l)
                norm_T(2 * l + 1)
                if l == 0:
                    dense_ff()
            router()
            gather(1)
            turn_selection(1)
            expert_items(0)
            pe.wait_ge(count_done, 1)
            count = pe.value_load(most_i[0:1, 0:1], min_val=0, max_val=SEQ)
            with pe.If(count > SLOTS):
                expert_items(EXPERTS)


W_BANK = ((4, 5), (2, 3))
SCATTER = (0, 1, 5, 4)
SMALL_IN = 16 * (2 + DEPTH * 11)

_INS = ["x", "g_mix", "w_in", "b_forget", "g_q_lat", "g_kv_lat", "w_uq", "w_ukv", "lambda_q1",
        "lambda_k1", "lambda_q2", "lambda_k2", "g_diff_sub", "w_out", "g_ffn", "w_ffn_gate",
        "w_ffn_up", "w_ffn_down", "w_router", "w_exp_gate", "w_exp_up", "w_exp_down", "g_final"]


def kernel(**inputs):
    import concourse.bacc as _bacc
    from concourse.bass_utils import run_bass_kernel_spmd as _run

    nc = _bacc.Bacc("TRN2", target_bir_lowering=False, num_devices=1)
    arrays = {n: np.ascontiguousarray(inputs[n]) for n in _INS}
    arrays["const"] = CONSTANTS
    w = {n: nc.dram_tensor(f"in_{n}", a.shape, F32, kind="ExternalInput").ap() for n, a in arrays.items()}
    out = nc.dram_tensor("out", (1, SEQ, D_MODEL), F32, kind="ExternalOutput").ap()
    with nc.allow_non_contiguous_dma(reason="gains of a few kilobytes, one element per partition"):
        build(nc, w, out)
    r = _run(nc, [{f"in_{n}": a for n, a in arrays.items()}], core_ids=[0])
    return r.results[0]["out"]
```

```python
import math
from contextlib import ExitStack

import concourse.bass as bass
import numpy as np
from concourse import mybir

F32 = mybir.dt.float32
F32R = mybir.dt.float32r
I32 = mybir.dt.int32
U32 = mybir.dt.uint32
ALU = mybir.AluOpType
ACT = mybir.ActivationFunctionType
AX = mybir.AxisListType

P = 128
D_MODEL, SEQ, DEPTH = 1024, 256, 2
TILES = SEQ // P
KC = D_MODEL // P
HEADS, HEAD_DIM = 4, 64
GROUP = HEADS * HEAD_DIM
Q_RANK, KV_RANK, NOPE, ROT = 256, 128, 64, 32
QK_A = NOPE + ROT
DIFF_QK = 32
IN_WIDTH = 2724
D_FF, D_FF_EXPERT, EXPERTS = 2816, 3584, 8
EPS = 1e-6
NEG = -1e30
DIL_CONFIGS = ((128, 1), (512, 4), (2048, 16))
AUG = HEAD_DIM + 2

CQ, CKV, KR = 0, 256, 384
QB, KB_, VB = 416, 672, 928
QCOL, KCOL, VCOL, FCOL = 1184, 1440, 1696, 1952
QD, KD, VD = 1956, 2212, 2468
Z_COLS = ((0, 416), (1952, 2464), (2464, 2724), (416, 928), (928, 1440), (1440, 1952))
NZ = len(Z_COLS)

RING = 7
SLOT = 4096
FW = 512
FF_STEPS = -(-D_FF // FW)
EX_STEPS = D_FF_EXPERT // FW
EX_CHUNKS = 3 * EX_STEPS
assert EX_CHUNKS % RING == 0
SLOTS = 128
ROUNDS = -(-SEQ // SLOTS)
ITEMS = EXPERTS * ROUNDS

JOBS = (("D", 0, 8, 0, 128), ("D", 1, 4, 0, 256), ("D", 1, 4, 4, 256), ("A", 0, 4, 0, 128),
        ("A", 1, 4, 0, 256), ("B", 0, 4, 0, 128), ("B", 1, 4, 0, 256), ("C", 0, 4, 0, 128),
        ("C", 1, 4, 0, 256))
NJ = len(JOBS)
SCALE = {"A": QK_A ** -0.5, "B": HEAD_DIM ** -0.5, "C": 1.0, "D": DIFF_QK ** -0.5}
YCOL = {"A": 0, "B": GROUP, "C": 2 * GROUP, "D": 3 * GROUP}
D_JOBS = 3

MIXER = ["Z00", "Z01", "Z10", "Z11", "LT", "Z20", "Z21", "LM", "CS", "QD", "J0", "Z30", "J1", "Z31",
         "J2", "QA", "Z40", "J3", "Z41", "QB", "J4", "Z50", "J5", "Z51", "QC", "J6", "J7", "J8",
         "Y0", "J9", "WA", "J10", "Y1"]

BATCH = {"LT": (0, 1), "CS": (2,), "QD": (3, 4), "QA": (5, 6, 7, 8), "QB": (9, 10),
         "QC": (11, 12, 13, 14), "Y0": (15, 16), "Y1": (17, 18)}
NEED = {"D": 5, "A": 9, "B": 11, "C": 15}
ROPES = {"D": 0, "A": 2, "B": 4}


def pt_batches(k):
    return JOBS[k][4] // P if JOBS[k][0] != "D" else 1


def spot(k, s):
    g, _, n, _, _ = JOBS[k]
    if g == "B":
        return (s % 2) * 2 + s // 2
    return (s % 4) * 2 + s // 4 if n == 8 else s


def head_blocks(k):
    g, _, n, _, nk = JOBS[k]
    heads = range(n) if g != "D" else range(0, n, 2)
    nh = len(heads)
    all_ = [(spot(k, s), kb, kb * nh + i) for kb in range(nk // P) for i, s in enumerate(heads)]
    return [all_[i:i + 4] for i in range(0, len(all_), 4)]


def pt_done(k):
    return sum(pt_batches(j) for j in range(k + 1))


CONST = {}


def _constants():
    p = np.arange(P)[:, None]
    d1 = P + p - np.arange(SEQ)[None, :]
    count = sum(((d1 >= 0) & (d1 % dil == 0) & (d1 <= win)).astype(int) for win, dil in DIL_CONFIGS)
    parts = [
        ("ident", np.eye(P)),
        ("causal", np.where(d1 >= 0, 0.0, NEG)),
        ("dilated", np.where(count > 0, np.log(np.maximum(count, 1)), NEG)),
        ("tri", (p <= np.arange(P)[None, :]).astype(float)),
        ("ones", np.ones((P, P))),
        ("iota", np.broadcast_to(np.arange(P), (P, P))),
    ]
    for half in (16, 32):
        inv = np.float32(10000.0) ** (-np.arange(half, dtype=np.float32) / np.float32(half))
        for t in range(TILES):
            ang = (np.arange(P, dtype=np.float32)[:, None] + P * t) * inv[None, :].astype(np.float32)
            parts += [(f"cos{half}_{t}", np.cos(ang)), (f"sin{half}_{t}", np.sin(ang)),
                      (f"nsin{half}_{t}", -np.sin(ang))]
    at = 0
    for name, a in parts:
        CONST[name] = (at, a.shape[1])
        at += a.shape[1]
    return np.ascontiguousarray(np.concatenate([a for _, a in parts], axis=1).astype(np.float32))


CONSTANTS = _constants()


def plan_chunks(w):
    chunks = []

    def rows(src):
        return src.rearrange("(c p) f -> p c f", p=P)

    for l in range(DEPTH):
        for c in range(NZ):
            a, b = Z_COLS[c]
            if c == 3:
                chunks.append([(0, (2, HEADS * QK_A), rows(w["w_uq"][l])),
                               (2 * HEADS * QK_A, (1, 2 * GROUP), rows(w["w_ukv"][l]))])
            chunks.append([(0, (KC, b - a), rows(w["w_in"][l][:, a:b]))])
        for h in range(2):
            chunks.append([(0, (KC, FW), rows(w["w_out"][l][:, h * FW:(h + 1) * FW]))])
        if l == 0:
            for kind, s in ff_order(FF_STEPS):
                a, b = s * FW, min((s + 1) * FW, D_FF)
                if kind == "d":
                    chunks.append([(0, ((b - a) // P, D_MODEL), rows(w["w_ffn_down"][0][a:b, :]))])
                else:
                    src = w["w_ffn_gate"] if kind == "g" else w["w_ffn_up"]
                    chunks.append([(0, (KC, b - a), rows(src[0][:, a:b]))])
    return chunks


def tasks(steps):
    order = ff_order(steps)
    out = {}
    for j in range(steps):
        at = order.index(("u", j))
        for what, n in (("silu", at), ("act", at + 1), ("parts", at + 2)):
            out.setdefault(min(n, len(order) - 1), []).append((what, j))
    return out


def ff_order(steps):
    out = []
    for s in range(steps):
        out += [("g", s), ("u", s)]
        if s:
            out.append(("d", s - 1))
    return out + [("d", steps - 1)]


UNITS = 4
EX_UNITS = 4 * EX_CHUNKS
assert EX_UNITS % UNITS == 0
FF_UNITS = 3 * D_FF // P

L_CHUNKS = NZ + 1 + 2
FF_AT = L_CHUNKS
L1_AT = L_CHUNKS + 3 * FF_STEPS
EX_AT = L1_AT + L_CHUNKS
EX_POS = {c: i for i, c in enumerate(ff_order(EX_STEPS))}
FF_POS = {c: FF_AT + i for i, c in enumerate(ff_order(FF_STEPS))}


MIXER_CHUNKS = ["Z0", "Z1", "Z2", "LM", "Z3", "Z4", "Z5", "W0", "W1"]


def mixer_chunk(l, name):
    return (L1_AT if l else 0) + MIXER_CHUNKS.index(name)


def mixer_used(l, name):
    return l * L_CHUNKS + MIXER_CHUNKS.index(name) + 1


def ff_quarters(s):
    return min(4, (D_FF - s * FW) // P)


FF_UNIT = {c: sum(ff_quarters(s) for _, s in ff_order(FF_STEPS)[:i]) for i, c in enumerate(ff_order(FF_STEPS))}


def build(nc, w, out):
    chunks = plan_chunks(w)
    assert len(chunks) == EX_AT
    landed, fill = [], [0] * RING
    for n, loads in enumerate(chunks):
        fill[n % RING] += 16 * len(loads)
        landed.append(fill[n % RING])
    landed_ex = []
    for c in range(EX_CHUNKS):
        fill[(EX_AT + c) % RING] += 16
        landed_ex.append(fill[(EX_AT + c) % RING])
    EX_LAND = 16 * EX_CHUNKS // RING

    with ExitStack() as ctx:
        def sb(name, shape, dt=F32):
            return ctx.enter_context(nc.sbuf_tensor(name, shape, dt))

        def sem(name):
            return ctx.enter_context(nc.semaphore(name))

        ps = ctx.enter_context(nc.psum_tensor("ps", [P, 8, 512], F32))
        mixer_mem = ExitStack()

        def mx(name, shape, dt=F32):
            return mixer_mem.enter_context(nc.sbuf_tensor(name, shape, dt))

        ring = sb("ring", [P, RING, SLOT])
        x = sb("x", [P, TILES, D_MODEL])
        hn = sb("hn", [P, TILES, D_MODEL])
        y = hn
        hT = sb("hT", [P, KC, SEQ])
        yT = hT
        const = sb("const", [P, CONSTANTS.shape[1]])
        g_rows = sb("g_rows", [GAIN_ROWS, P])
        g_cols = sb("g_cols", [P, GAIN_ROWS])
        b_f = sb("b_f", [P, DEPTH, HEADS])
        lam_in = sb("lam_in", [P, 4, DEPTH, DIFF_QK])
        lam_s = sb("lam_s", [P, 2, DEPTH])
        lam_junk = sb("lam_junk", [P, DIFF_QK])
        neg_lam = sb("neg_lam", [P, DEPTH])
        w_r = sb("w_r", [P, KC, EXPERTS])
        sumsq = sb("sumsq", [P, 5, TILES])
        rstd = sb("rstd", [P, 5, TILES])
        half_neg = sb("half_neg", [P, 8])

        neg_max = sb("neg_max", [P, NJ, 8])
        row_sum = sb("row_sum", [P, NJ, 8])
        row_inv = sb("row_inv", [P, NJ, 8])
        lat_ss = sb("lat_ss", [P, TILES, 2])
        lat_r = sb("lat_r", [P, TILES, 2])
        fg = sb("fg", [P, 6, TILES, HEADS])
        c_sum = sb("c_sum", [P, TILES, HEADS])
        d_ss = sb("d_ss", [P, 8])
        d_r = sb("d_r", [P, 8])
        logits = sb("logits", [P, TILES, EXPERTS])
        top = sb("top", [P, TILES, 8])
        top_i = sb("top_i", [P, TILES, 8], U32)
        top_f = sb("top_f", [P, TILES, 8])
        route = sb("route", [P, 4, TILES])
        hot = sb("hot", [P, 4, TILES, EXPERTS])
        most = sb("most", [P, 1])
        most_i = sb("most_i", [P, 1], I32)

        z = mx("z", [P, TILES, IN_WIDTH])
        kA = mx("kA", [P, TILES, HEADS, QK_A])
        vA = mx("vA", [P, TILES, GROUP])
        tmp_a = mx("tmp_a", [P, 512])
        tmp_b = mx("tmp_b", [P, 512])
        qC = mx("qC", [P, TILES, HEADS, AUG])
        kC = mx("kC", [P, TILES, HEADS, AUG])
        wideT = mx("wideT", [P, 2, HEADS, SEQ])
        pairT = mx("pairT", [P, 2, 2, SEQ])
        E = mx("E", [P, 2, 1024])
        pT = mx("pT", [P, 2, 8, P])
        qA = z[:, :, 0:HEADS * QK_A]
        latn = E[:, :, :].rearrange("p a b -> p (a b)")[:, 0:TILES * 384].rearrange("p (t n) -> p t n", t=TILES)
        latT = pT[:, :, :, :].rearrange("p a b c -> p (a b c)")[:, 0:3 * SEQ].rearrange("p (c n) -> p c n", c=3)

        mixer_mem.close()
        split = sb("split", [P, UNITS, 2, 1024], F32R)
        hTs = sb("hTs", [P, 2, KC, SEQ], F32R)
        acts = sb("acts", [P, 2, 4 * SEQ], F32R)
        ff_act = sb("ff_act", [P, 4 * SEQ])
        xgTs = hTs[:, :, :, :].rearrange("p i c n -> p (i c n)")[:, 0:2 * KC * SLOTS].rearrange(
            "p (i c n) -> p i c n", i=2, c=KC)
        ex_actTs = acts[:, :, 0:4 * SLOTS].rearrange("p i (q n) -> p i q n", q=4)
        ex_act = ff_act[:, 0:FW]
        ex_out = ff_act[:, 0:D_MODEL]
        xgT = hT[:, 0:4, :].rearrange("p c n -> p (c n)").rearrange("p (c n) -> p c n", c=KC)
        g_fin = hT[:, 0:4, :].rearrange("p c n -> p (c n)")
        sel = hT[:, 4, :].rearrange("p (t n) -> p t n", t=TILES)
        sel_g = hT[:, 5, :].rearrange("p (t n) -> p t n", t=TILES)
        sel_gT = hT[:, 6, :]
        at = TILES * EXPERTS
        chosen = hT[:, 7, 0:at].rearrange("p (t n) -> p t n", t=TILES)
        place, gate = (hT[:, 7, a:a + TILES * (ITEMS + 1)].rearrange("p (t n) -> p t n", t=TILES)
                       for a in (at, at + TILES * (ITEMS + 1)))

        def cst(name):
            a, n = CONST[name]
            return const[:, a:a + n]

        ident, tri, ones = cst("ident"), cst("tri"), cst("ones")

        x_in = [sem(f"x_in{t}") for t in range(TILES)]
        first_in = sem("first_in")
        small_in = sem("small_in")
        g_ps, g_done = sem("g_ps"), sem("g_done")
        gfin_in = sem("gfin_in")
        slot_in = [sem(f"slot_in{i}") for i in range(RING)]
        chunk_done = sem("chunk_done")
        sq_done = sem("sq_done")
        rstd_done = sem("rstd_done")
        hn_done = sem("hn_done")
        hT_ps = sem("hT_ps")
        hT_done = sem("hT_done")
        x_done = sem("x_done")
        dve_c, act_c, pool_c = sem("dve_c"), sem("act_c"), sem("pool_c")
        lam_sum, lam_exp = sem("lam_sum"), sem("lam_exp")

        def per_layer(name):
            return [sem(f"{name}_{l}") for l in range(DEPTH)]

        z_ps = per_layer("z_ps")
        z_done = per_layer("z_done")
        lat_sq = per_layer("lat_sq")
        lat_rs = per_layer("lat_rs")
        lat_done = per_layer("lat_done")
        lm_ps = per_layer("lm_ps")
        uq_done = per_layer("uq_done")
        ukv_done = per_layer("ukv_done")
        rope_done = per_layer("rope_done")
        bt_ps = per_layer("bt_ps")
        bt_done = per_layer("bt_done")
        f_in = per_layer("f_in")
        f_log = per_layer("f_log")
        lf_done = per_layer("lf_done")
        aug_done = per_layer("aug_done")
        c_done = per_layer("c_done")
        s_ps = per_layer("s_ps")
        mask_done = per_layer("mask_done")
        max_done = per_layer("max_done")
        exp_done = per_layer("exp_done")
        comb_done = per_layer("comb_done")
        pt_ps = per_layer("pt_ps")
        pt_ev = per_layer("pt_ev")
        pv_ps = per_layer("pv_ps")
        y_done = per_layer("y_done")
        d_sq = per_layer("d_sq")
        d_rs = per_layer("d_rs")
        yd_done = per_layer("yd_done")
        w_ps = per_layer("w_ps")
        hi_done = sem("hi_done")
        lo_done = sem("lo_done")
        unit_done = sem("unit_done")
        hTh_done = sem("hTh_done")
        hTl_done = sem("hTl_done")
        ff_sd = sem("ff_silu")
        ff_ad = sem("ff_act")
        ff_ah = sem("ff_ah")
        ff_al = sem("ff_al")
        ff_ps = sem("ff_ps")
        logit_ps, top_done, route_exp, chosen_done = sem("logit_ps"), sem("top_done"), sem("route_exp"), sem("chosen_done")
        count_ps, count_done = sem("count_ps"), sem("count_done")
        sel_done = sem("sel_done")
        gather_ps = sem("gather_ps")
        xg_done = sem("xg_done")
        xgh_done = sem("xgh_done")
        xgT_done = sem("xgT_done")
        selT_ps = sem("selT_ps")
        selT_done = sem("selT_done")
        silu_done = sem("silu_done")
        act_done = sem("act_done")
        actT_ps = sem("actT_ps")
        acth_done = sem("acth_done")
        actl_done = sem("actl_done")
        eo_done = sem("eo_done")
        scatter_ps = sem("scatter_ps")
        y_added = sem("y_added")
        x_final = sem("x_final")
        out_ready = sem("out_ready")
        stored = sem("stored")

        block = ctx.enter_context(nc.Block())

        def gains(n):
            a = GAIN_AT["g_ffn" if n % 2 else "g_mix"] + (n // 2) * KC
            return g_cols[:, a:a + KC]

        def bc(ap, axis, shape):
            return ap.unsqueeze(axis).to_broadcast(shape)

        def slot_view(n, first, shape):
            a, b = shape
            return ring[:, n % RING, first:first + a * b].rearrange("p (a b) -> p a b", a=a)

        def score_places(k):
            g, _, n, _, _ = JOBS[k]
            banks = ps[:, 2 if g == "D" else 4:6, :]
            return banks.rearrange("p a b -> p (a b)").rearrange("p (s n) -> p s n", s=n)

        def ex_unit(u, cols=1024):
            return split[:, u % UNITS, 0, 0:cols], split[:, u % UNITS, 1, 0:cols]

        def as_block(ap, n):
            return ap.rearrange("p (a b) -> p a b", a=n)

        def ff_parts(kind, s):
            n, nq = FF_POS[(kind, s)], ff_quarters(s)
            if kind == "d":
                w_c = slot_view(n, 0, (nq, D_MODEL))
                return [(FF_UNIT[(kind, s)] + q, w_c[:, q:q + 1, :]) for q in range(nq)]
            w_c = slot_view(n, 0, (KC, nq * P))
            return [(FF_UNIT[(kind, s)] + q, w_c[:, :, q * P:(q + 1) * P]) for q in range(nq)]

        def ex_part(c, u):
            return ring[:, (EX_AT + c) % RING, u * 1024:(u + 1) * 1024]

        def xcols(h):
            return slice(h * 512, (h + 1) * 512)

        @block.sync
        def _(sp):
            def load(n):
                m = n - RING
                if FF_AT <= m < L1_AT:
                    kind, s = ff_order(FF_STEPS)[m - FF_AT]
                    sp.wait_ge(lo_done, FF_UNIT[(kind, s)] + ff_quarters(s))
                elif m >= 0:
                    sp.wait_ge(chunk_done, m + 1 if m < L_CHUNKS else m - L1_AT + L_CHUNKS + 1)
                for first, shape, src in chunks[n]:
                    sp.dma_start(slot_view(n, first, shape), src).then_inc(slot_in[n % RING], 16)

            for t in range(TILES):
                sp.dma_start(x[:, t, :], w["x"][0].rearrange("(t p) d -> p t d", p=P)[:, t, :]).then_inc(x_in[t], 16)
            first = [(const[:, :], w["const"])]
            for name in ("g_mix", "g_ffn"):
                a = GAIN_AT[name]
                first.append((g_rows[a:a + DEPTH * KC, :], w[name].rearrange("l (c p) -> (l c) p", p=P)))
            for l in range(DEPTH):
                a = GAIN_AT["latent"] + 3 * l
                first += [(g_rows[a:a + 2, :], w["g_q_lat"][l].rearrange("(c p) -> c p", p=P)),
                          (g_rows[a + 2:a + 3, :], w["g_kv_lat"][l].rearrange("(c p) -> c p", p=P))]
            a = GAIN_AT["g_diff_sub"]
            first += [(g_rows[a:a + DEPTH, h * HEAD_DIM:(h + 1) * HEAD_DIM], w["g_diff_sub"]) for h in range(2)]
            assert 16 * len(first) == FIRST_IN
            for dst, src in first:
                sp.dma_start(dst, src).then_inc(first_in, 16)
            load(0)
            small = [(w_r[:, :, :], w["w_router"][0].rearrange("(c p) e -> p c e", p=P)),
                     (b_f[:, :, :].rearrange("p l h -> p (l h)"),
                      w["b_forget"].rearrange("l h -> (l h)").partition_broadcast(P))]
            for i, name in enumerate(("lambda_q1", "lambda_k1", "lambda_q2", "lambda_k2")):
                small.append((lam_in[:, i, :, :].rearrange("p l n -> p (l n)"),
                              w[name].rearrange("l n -> (l n)").partition_broadcast(P)))
            assert 16 * len(small) == SMALL_IN
            for dst, src in small:
                sp.dma_start(dst, src).then_inc(small_in, 16)
            for n in range(1, EX_AT):
                load(n)

            gate_w = w["w_exp_gate"].rearrange("l e (c p) f -> p (l e c) f", p=P)
            up_w = w["w_exp_up"].rearrange("l e (c p) f -> p (l e c) f", p=P)
            down_w = w["w_exp_down"].rearrange("l e (q p) d -> p (l e q) d", p=P)
            FQ = D_FF_EXPERT // P

            def expert_items(first):
                with sp.Fori(first, first + EXPERTS) as i:
                    e = i - first
                    for (kind, s), c in EX_POS.items():
                        n = EX_AT + c
                        if c < RING:
                            sp.wait_ge(chunk_done, 2 * L_CHUNKS - RING + c + 1)
                        sp.wait_ge(lo_done, i * EX_UNITS + (FF_UNITS + 4 * (c - RING + 1)))
                        if kind == "d":
                            dst = slot_view(n, 0, (4, D_MODEL))
                            src = down_w[:, bass.ds(e * FQ + 4 * s, 4), :]
                        else:
                            dst = slot_view(n, 0, (KC, FW))
                            src = (gate_w if kind == "g" else up_w)[:, bass.ds(e * KC, KC), s * FW:(s + 1) * FW]
                        sp.dma_start(dst, src).then_inc(slot_in[n % RING], 16)

            expert_items(0)
            sp.wait_ge(count_done, 1)
            count = sp.value_load(most_i[0:1, 0:1], min_val=0, max_val=SEQ)
            for r in range(1, ROUNDS):
                with sp.If(count > r * SLOTS):
                    expert_items(r * EXPERTS)
            for t in range(TILES):
                sp.wait_ge(out_ready, t + 1)
                sp.dma_start(out[0].rearrange("(t p) d -> p t d", p=P)[:, t, :], x[:, t, :]).then_inc(stored, 16)
            sp.wait_ge(stored, 16 * TILES)

        @block.gpsimd
        def _(pool):
            links = [0]

            def link(ins):
                links[0] += 1
                ins.then_inc(pool_c, 1)
                pool.wait_ge(pool_c, links[0])

            def rsqrt_mean(dst, src, n, width, signal):
                link(pool.tensor_scalar(dst, src, 1.0 / n, EPS, ALU.mult, ALU.add))
                pool.tensor_tensor(dst, dst, half_neg[:, 0:width], ALU.pow).then_inc(signal, 1)

            def norm(n):
                for t in range(TILES):
                    pool.wait_ge(sq_done, TILES * n + t + 1)
                    rsqrt_mean(rstd[:, n, t:t + 1], sumsq[:, n, t:t + 1], D_MODEL, 1, rstd_done)

            def mixer(l):
                norm(2 * l)
                pool.wait_ge(lat_sq[l], 1)
                link(pool.tensor_scalar(lat_r[:, :, 0], lat_ss[:, :, 0], 1.0 / Q_RANK, EPS, ALU.mult, ALU.add))
                link(pool.tensor_scalar(lat_r[:, :, 1], lat_ss[:, :, 1], 1.0 / KV_RANK, EPS, ALU.mult, ALU.add))
                flat = lat_r[:, :, :].rearrange("p a b -> p (a b)")
                pool.tensor_tensor(flat, flat, half_neg[:, 0:4], ALU.pow).then_inc(lat_rs[l], 1)
                pool.wait_ge(d_sq[l], 1)
                rsqrt_mean(d_r[:, :], d_ss[:, :], HEAD_DIM, 8, d_rs[l])
                pool.wait_ge(z_done[l], 2 * NZ)
                for t in range(TILES):
                    q = z[:, t, QCOL:QCOL + GROUP].rearrange("p (h d) -> p h d", h=HEADS)
                    k = z[:, t, KCOL:KCOL + GROUP].rearrange("p (h d) -> p h d", h=HEADS)
                    pool.tensor_scalar(qC[:, t, :, 0:HEAD_DIM], q, HEAD_DIM ** -0.5, None, ALU.mult).then_inc(aug_done[l], 1)
                    pool.tensor_copy(kC[:, t, :, 0:HEAD_DIM], k).then_inc(aug_done[l], 1)

            link(pool.memset(half_neg[:, :], -0.5))
            for l in range(DEPTH):
                mixer(l)
                norm(2 * l + 1)
            norm(2 * DEPTH)

        @block.scalar
        def _(act):
            links = [0]

            def link(ins):
                links[0] += 1
                ins.then_inc(act_c, 1)
                act.wait_ge(act_c, links[0])

            def squares(n, t):
                act.activation(hn[:, t, :], x[:, t, :], ACT.Square, accum_out=sumsq[:, n, t:t + 1]).then_inc(sq_done, 1)

            def norm(n):
                for t in range(TILES):
                    if n == 0:
                        act.wait_ge(x_in[t], 16)
                    else:
                        act.wait_ge(x_done, 2 * (n - 1) + t + 1)
                    squares(n, t)
                    act.wait_ge(rstd_done, TILES * n + t + 1)
                    act.wait_ge(sq_done, TILES * n + t + 1)
                    act.activation(hn[:, t, :], x[:, t, :], ACT.Copy, scale=rstd[:, n, t:t + 1]).then_inc(hn_done, 1)

            def mixer(l):
                def z_chunk(c, t):
                    a, b = Z_COLS[c]
                    if t == 0:
                        act.wait_ge(z_ps[l], c + 1)
                    else:
                        act.wait_ge(chunk_done, mixer_used(l, f"Z{c}"))
                    act.activation(z[:, t, a:b], ps[:, t, 0:b - a], ACT.Copy).then_inc(z_done[l], 1)

                def exps(k):
                    act.wait_ge(max_done[l], k + 1)
                    _, _, n, _, nk = JOBS[k]
                    for s in range(n):
                        e = E[:, k % 2, s * nk:(s + 1) * nk]
                        ins = act.activation(e, e, ACT.Exp, bias=neg_max[:, k, s:s + 1],
                                             accum_out=row_sum[:, k, s:s + 1])
                    ins.then_inc(exp_done[l], 1)

                def pt_copy(k):
                    for b in range(pt_batches(k)):
                        act.wait_ge(pt_ps[l], pt_done(k) - pt_batches(k) + b + 1)
                        act.activation(pT[:, k % 2, 4 * b:4 * b + 4, :],
                                       ps[:, 7, :].rearrange("p (b n) -> p b n", b=4),
                                       ACT.Copy).then_inc(pt_ev[l], 1)

                norm(2 * l)
                if l == 0:
                    act.wait_ge(lam_sum, 1)
                    act.activation(lam_s[:, :, :], lam_s[:, :, :], ACT.Exp).then_inc(lam_exp, 1)
                for step in MIXER:
                    if step[0] == "Z":
                        z_chunk(int(step[1]), int(step[2]))
                    elif step == "LM":
                        for t in range(TILES):
                            if t == 0:
                                act.wait_ge(lm_ps[l], 2)
                            else:
                                act.wait_ge(chunk_done, mixer_used(l, "LM"))
                            kv = ps[:, 7, :].rearrange("p (h d) -> p h d", h=HEADS)
                            act.activation(kA[:, t, :, 0:NOPE], kv[:, :, 0:NOPE], ACT.Copy)
                            act.activation(vA[:, t, :].rearrange("p (h d) -> p h d", h=HEADS),
                                           kv[:, :, NOPE:], ACT.Copy).then_inc(ukv_done[l], 1)
                    elif step == "CS":
                        act.wait_ge(f_in[l], 1)
                        link(act.activation(fg[:, 3], fg[:, 2], ACT.Exp))
                        act.activation(fg[:, 4], fg[:, 3], ACT.Ln, bias=1.0).then_inc(f_log[l], 1)
                    elif step[0] == "J":
                        k = int(step[1:])
                        if 1 <= k <= NJ:
                            pt_copy(k - 1)
                        if k < NJ:
                            exps(k)

            def dense_ff():
                def chunk(kind, s, first=0, last=4):
                    if first == 0:
                        act.wait_ge(slot_in[FF_POS[(kind, s)] % RING], landed[FF_POS[(kind, s)]])
                    for v, src in ff_parts(kind, s)[first:last]:
                        if v >= UNITS:
                            act.wait_ge(unit_done, v + 1 - UNITS)
                        dst = ex_unit(v, src.shape[1] * src.shape[2])[0]
                        act.activation(as_block(dst, src.shape[1]), src, ACT.Copy).then_inc(hi_done, 1)

                for b in range(4):
                    t, half = divmod(b, 2)
                    chunk("g", 0, b, b + 1)
                    act.wait_ge(hT_done, 4 + b + 1)
                    tok = slice(t * P, (t + 1) * P)
                    act.activation(hTs[:, 0, 4 * half:4 * half + 4, tok], hT[:, 4 * half:4 * half + 4, tok],
                                   ACT.Copy).then_inc(hTh_done, 1)
                after = tasks(FF_STEPS)
                for n, (kind, s) in enumerate(ff_order(FF_STEPS)):
                    if n:
                        chunk(kind, s)
                    for what, j in after.get(n, ()):
                        nq = ff_quarters(j)
                        if what == "silu":
                            act.wait_ge(unit_done, FF_UNIT[("g", j)] + nq)
                            if j:
                                act.wait_ge(ff_al, j)
                            act.activation(ff_act[:, 0:nq * SEQ].rearrange("p (b n) -> p b n", n=512),
                                           ps[:, 0:nq // 2, :], ACT.Silu).then_inc(ff_sd, 1)
                        elif what == "parts":
                            act.wait_ge(ff_ad, j + 1)
                            if j:
                                act.wait_ge(unit_done, FF_UNIT[("d", j - 1)] + ff_quarters(j - 1))
                            act.activation(acts[:, 0, 0:nq * SEQ], ff_act[:, 0:nq * SEQ], ACT.Copy).then_inc(ff_ah, 1)

            def expert_items(first):
                with act.Fori(first, first + EXPERTS) as i:
                    after = tasks(EX_STEPS)
                    for c, (kind, s) in enumerate(ff_order(EX_STEPS)):
                        act.wait_ge(slot_in[(EX_AT + c) % RING], i * EX_LAND + landed_ex[c])
                        for u in range(4):
                            v = FF_UNITS + 4 * c + u
                            act.wait_ge(unit_done, i * EX_UNITS + (v + 1 - UNITS))
                            act.activation(ex_unit(v)[0], ex_part(c, u), ACT.Copy).then_inc(hi_done, 1)
                        for what, j in after.get(c, ()):
                            if what == "silu":
                                act.wait_ge(unit_done, i * EX_UNITS + (FF_UNITS + 4 * EX_POS[("g", j)] + 4))
                                if j:
                                    act.wait_ge(actT_ps, i * EX_STEPS + j)
                                act.activation(ex_act, ps[:, 0, :], ACT.Silu).then_inc(silu_done, 1)
                            elif what == "parts":
                                act.wait_ge(actT_ps, i * EX_STEPS + (j + 1))
                                act.activation(ex_actTs[:, 0], ps[:, 4, :].rearrange("p (q n) -> p q n", q=4),
                                               ACT.Copy).then_inc(acth_done, 1)
                        if c == 0:
                            copy_selT(i + 1)
                    token_parts(i + 2)
                    act.wait_ge(unit_done, i * EX_UNITS + (FF_UNITS + EX_UNITS))
                    for h in range(2):
                        act.activation(ex_out[:, xcols(h)], ps[:, 2 + h, :], ACT.Copy).then_inc(eo_done, 1)

            def token_parts(n):
                act.wait_ge(xg_done, n)
                act.activation(xgTs[:, 0], xgT, ACT.Copy).then_inc(xgh_done, 1)

            def copy_selT(n):
                act.wait_ge(selT_ps, n)
                act.activation(sel_gT, ps[:, 6, 0:SEQ], ACT.Copy).then_inc(selT_done, 1)

            for l in range(DEPTH):
                mixer(l)
                norm(2 * l + 1)
                if l == 0:
                    dense_ff()
            act.wait_ge(top_done, 1)
            act.activation(route[:, 1, :], route[:, 0, :], ACT.Exp).then_inc(route_exp, 1)
            token_parts(1)
            expert_items(0)
            act.wait_ge(count_done, 1)
            count = act.value_load(most_i[0:1, 0:1], min_val=0, max_val=SEQ)
            for r in range(1, ROUNDS):
                with act.If(count > r * SLOTS):
                    expert_items(r * EXPERTS)
            act.wait_ge(x_final, 1)
            act.dma_start(g_fin, w["g_final"].partition_broadcast(P)).then_inc(gfin_in, 16)
            for t in range(TILES):
                squares(2 * DEPTH, t)

        @block.vector
        def _(dve):
            links = [0]

            def link(ins):
                links[0] += 1
                ins.then_inc(dve_c, 1)
                dve.wait_ge(dve_c, links[0])

            def norm_T(n):
                for b in range(4):
                    t, half = divmod(b, 2)
                    dve.wait_ge(hT_ps, 4 * n + b + 1)
                    g = bc(gains(n)[:, 4 * half:4 * half + 4], 2, [P, 4, P])
                    dve.tensor_tensor(hT[:, 4 * half:4 * half + 4, t * P:(t + 1) * P],
                                      ps[:, 2 + b % 2, :].rearrange("p (c n) -> p c n", c=4), g,
                                      ALU.mult).then_inc(hT_done, 1)

            def rope(v, n, half, t):
                a = tmp_a[:, 0:n * 2 * half].rearrange("p (h i d) -> p h i d", h=n, i=2)
                b = tmp_b[:, 0:n * 2 * half].rearrange("p (h i d) -> p h i d", h=n, i=2)
                for i in range(2):
                    dve.tensor_tensor(a[:, :, i, :], v[:, :, i, :],
                                      bc(cst(f"cos{half}_{t}"), 1, [P, n, half]), ALU.mult)
                dve.tensor_tensor(b[:, :, 0, :], v[:, :, 1, :],
                                  bc(cst(f"nsin{half}_{t}"), 1, [P, n, half]), ALU.mult)
                link(dve.tensor_tensor(b[:, :, 1, :], v[:, :, 0, :],
                                       bc(cst(f"sin{half}_{t}"), 1, [P, n, half]), ALU.mult))
                return dve.tensor_tensor(v, a, b, ALU.add)

            def mixer(l):
                def batch(b):
                    dve.wait_ge(bt_ps[l], b + 1)
                    return ps[:, 2 + b % 2, :]

                def latents():
                    dve.wait_ge(z_done[l], 2)
                    for t in range(TILES):
                        for i, (a, n) in enumerate(((CQ, Q_RANK), (CKV, KV_RANK))):
                            link(dve.tensor_tensor(tmp_a[:, 0:n], z[:, t, a:a + n], z[:, t, a:a + n], ALU.mult))
                            ins = dve.tensor_reduce(lat_ss[:, t, i:i + 1], tmp_a[:, 0:n], AX.X, ALU.add)
                            if (t, i) != (TILES - 1, 1):
                                link(ins)
                    ins.then_inc(lat_sq[l], 1)
                    dve.wait_ge(lat_sq[l], 1)
                    for t in range(TILES):
                        kr = z[:, t, KR:KR + ROT].rearrange("p (h i d) -> p h i d", h=1, i=2)
                        link(rope(kr, 1, ROT // 2, t))
                        link(dve.tensor_copy(kA[:, t, :, NOPE:],
                                             bc(z[:, t, KR:KR + ROT], 1, [P, HEADS, ROT])))
                    dve.wait_ge(lat_rs[l], 1)
                    for t in range(TILES):
                        dve.tensor_scalar(latn[:, t, 0:Q_RANK], z[:, t, CQ:CQ + Q_RANK],
                                          lat_r[:, t, 0:1], None, ALU.mult)
                        dve.tensor_scalar(latn[:, t, Q_RANK:], z[:, t, CKV:CKV + KV_RANK],
                                          lat_r[:, t, 1:2], None, ALU.mult).then_inc(lat_done[l], 1)
                    dve.wait_ge(lat_done[l], 2)

                def rope_qk(first, n, half):
                    for t in range(TILES):
                        v = z[:, t, first:first + 2 * GROUP].rearrange("p (h i d) -> p h i d", h=n, i=2)
                        ins = rope(v, n, half, t)
                        ins.then_inc(rope_done[l], 1)
                        ropes[0] += 1
                        dve.wait_ge(rope_done[l], ropes[0])

                def forget():
                    f = z[:, :, FCOL:FCOL + HEADS]
                    link(dve.tensor_tensor(fg[:, 0], f, bc(b_f[:, l, :], 1, [P, TILES, HEADS]), ALU.add))
                    link(dve.tensor_scalar(fg[:, 1], fg[:, 0], 0.0, None, ALU.min))
                    link(dve.tensor_scalar(fg[:, 2], fg[:, 0], 0.0, None, ALU.max))
                    link(dve.tensor_tensor(fg[:, 2], fg[:, 1], fg[:, 2], ALU.subtract))
                    dve.sem_inc(f_in[l], 1)
                    dve.wait_ge(f_log[l], 1)
                    dve.tensor_tensor(fg[:, 5], fg[:, 1], fg[:, 4], ALU.subtract).then_inc(lf_done[l], 1)

                def mask(k):
                    g, t, n, _, nk = JOBS[k]
                    dve.wait_ge(s_ps[l], k + 1)
                    m = cst("dilated" if g == "B" else "causal")[:, SEQ - nk:]
                    e = E[:, k % 2, 0:n * nk].rearrange("p (s n) -> p s n", s=n)
                    s = score_places(k)[:, :, 0:nk]
                    dve.scalar_tensor_tensor(e, s, SCALE[g], bc(m, 1, [P, n, nk]), ALU.mult,
                                             ALU.add).then_inc(mask_done[l], 1)
                    dve.wait_ge(mask_done[l], k + 1)
                    dve.tensor_reduce(neg_max[:, k, 0:n], e, AX.X, ALU.max, negate=True).then_inc(max_done[l], 1)

                def combine(k):
                    _, _, n, _, nk = JOBS[k]
                    dve.wait_ge(exp_done[l], k + 1)
                    link(dve.reciprocal(row_inv[:, k, 0:n], row_sum[:, k, 0:n]))
                    r = row_inv[:, k, 0:n].rearrange("p (m i r) -> p m i r", m=2, i=2)
                    link(dve.tensor_scalar(r[:, :, 1], r[:, :, 1], neg_lam[:, l:l + 1], None, ALU.mult))
                    e = E[:, k % 2, 0:n * nk].rearrange("p (s n) -> p s n", s=n)
                    link(dve.tensor_tensor(e, e, bc(row_inv[:, k, 0:n], 2, [P, n, nk]), ALU.mult))
                    e = E[:, k % 2, 0:n * nk].rearrange("p (m i r) -> p m i r", m=2, i=2)
                    dve.tensor_tensor(e[:, :, 0, :], e[:, :, 0, :], e[:, :, 1, :], ALU.add).then_inc(comb_done[l], 1)

                def output(k):
                    g, t, n, s0, _ = JOBS[k]
                    nh = n // 2 if g == "D" else n
                    c0 = YCOL[g] + (s0 // 2) * HEAD_DIM
                    o = ps[:, 6, 0:nh * HEAD_DIM]
                    dst = y[:, t, c0:c0 + nh * HEAD_DIM]
                    if g != "D":
                        dve.wait_ge(exp_done[l], k + 1)
                        link(dve.reciprocal(row_inv[:, k, 0:n], row_sum[:, k, 0:n]))
                    dve.wait_ge(pv_ps[l], k + 1)
                    if g == "D":
                        ins = dve.tensor_copy(dst, o)
                    elif g == "B":
                        ins = dve.tensor_tensor(dst.rearrange("p (b a d) -> p a b d", a=2, b=2),
                                                o.rearrange("p (b a d) -> p a b d", a=2, b=2),
                                                bc(row_inv[:, k, 0:4].rearrange("p (a b) -> p a b", a=2), 3,
                                                   [P, 2, 2, HEAD_DIM]), ALU.mult)
                    else:
                        ins = dve.tensor_tensor(dst.rearrange("p (h d) -> p h d", h=nh),
                                                o.rearrange("p (h d) -> p h d", h=nh),
                                                bc(row_inv[:, k, 0:nh], 2, [P, nh, HEAD_DIM]), ALU.mult)
                    ins.then_inc(y_done[l], 1)

                def norm_d():
                    dve.wait_ge(y_done[l], D_JOBS)
                    yd = y[:, :, 3 * GROUP:].rearrange("p t (h d) -> p t h d", h=HEADS)
                    sq = tmp_a[:, :].rearrange("p (t h d) -> p t h d", t=TILES, h=HEADS)
                    link(dve.tensor_tensor(sq, yd, yd, ALU.mult))
                    dve.tensor_reduce(d_ss[:, :], tmp_a[:, :].rearrange("p (h d) -> p h d", h=8), AX.X,
                                      ALU.add).then_inc(d_sq[l], 1)
                    dve.wait_ge(d_rs[l], 1)
                    for t in range(TILES):
                        dve.tensor_tensor(yd[:, t], yd[:, t], bc(d_r[:, 4 * t:4 * t + 4], 2, [P, HEADS, HEAD_DIM]),
                                          ALU.mult).then_inc(yd_done[l], 1)

                lam_init = 0.8 - 0.6 * math.exp(-0.3 * l)
                ropes = [0]
                norm_T(2 * l)
                if l == 0:
                    lambdas()
                for step in MIXER:
                    if step == "Z01":
                        latents()
                    elif step == "LT":
                        for t, b in enumerate(BATCH["LT"]):
                            src = batch(b)[:, 0:3 * P].rearrange("p (c n) -> p c n", c=3)
                            dve.tensor_tensor(latT[:, :, t * P:(t + 1) * P], src,
                                              bc(g_cols[:, GAIN_AT["latent"] + 3 * l:GAIN_AT["latent"] + 3 * l + 3], 2, [P, 3, P]), ALU.mult).then_inc(bt_done[l], 1)
                    elif step == "LM":
                        for t in range(TILES):
                            dve.wait_ge(lm_ps[l], 2 * t + 1)
                            dve.tensor_copy(qA[:, t, :], ps[:, 6, 0:HEADS * QK_A]).then_inc(uq_done[l], 1)
                        dve.wait_ge(uq_done[l], 2)
                        for t in range(TILES):
                            v = qA[:, t, :].rearrange("p (h d) -> p h d", h=HEADS)[:, :, NOPE:]
                            ins = rope(v.rearrange("p h (i d) -> p h i d", i=2), HEADS, ROT // 2, t)
                            ins.then_inc(rope_done[l], 1)
                            ropes[0] += 1
                            dve.wait_ge(rope_done[l], ropes[0])
                    elif step == "Z21":
                        dve.wait_ge(z_done[l], 2 * 3)
                        rope_qk(QD, 4 * HEADS, DIFF_QK // 2)
                    elif step == "Z31":
                        dve.wait_ge(z_done[l], 2 * 4)
                        rope_qk(QB, 2 * HEADS, HEAD_DIM // 2)
                    elif step in ("QB", "QD"):
                        for t, b in enumerate(BATCH[step]):
                            src = batch(b).rearrange("p (a h n) -> p a h n", a=2, h=2)
                            dve.tensor_copy(pairT[:, :, :, t * P:(t + 1) * P], src).then_inc(bt_done[l], 1)
                    elif step in ("QA", "QC"):
                        rows = QK_A if step == "QA" else AUG
                        for i, b in enumerate(BATCH[step]):
                            t, qk = divmod(i, 2)
                            src = batch(b)[0:rows, :].rearrange("p (h n) -> p h n", h=HEADS)
                            dve.tensor_copy(wideT[0:rows, qk, :, t * P:(t + 1) * P], src).then_inc(bt_done[l], 1)
                    elif step == "CS":
                        forget()
                        dve.memset(qC[:, :, :, HEAD_DIM + 1:AUG], 1.0)
                        dve.memset(kC[:, :, :, HEAD_DIM:HEAD_DIM + 1], 1.0)
                        src = batch(BATCH["CS"][0])[:, 0:TILES * HEADS].rearrange("p (t h) -> p t h", t=TILES)
                        dve.tensor_copy(qC[:, :, :, HEAD_DIM], src)
                        dve.tensor_scalar(kC[:, :, :, HEAD_DIM + 1], src, -1.0, None, ALU.mult).then_inc(bt_done[l], 1)
                    elif step[0] == "J":
                        k = int(step[1:])
                        if k < NJ:
                            mask(k)
                        if 1 <= k <= D_JOBS:
                            combine(k - 1)
                        if k >= 2:
                            output(k - 2)
                        if k - 2 == D_JOBS - 1:
                            norm_d()
                    elif step in ("Y0", "Y1"):
                        half = int(step[1])
                        for t, b in enumerate(BATCH[step]):
                            src = batch(b).rearrange("p (c n) -> p c n", c=4)
                            tok = slice(t * P, (t + 1) * P)
                            if half == 0:
                                dve.tensor_copy(yT[:, 0:4, tok], src).then_inc(bt_done[l], 1)
                            else:
                                dve.tensor_copy(yT[:, 4:6, tok], src[:, 0:2])
                                a = GAIN_AT["g_diff_sub"] + l
                                dve.tensor_scalar(yT[:, 6:8, tok], src[:, 2:4], g_cols[:, a:a + 1],
                                                  1.0 - lam_init, ALU.mult, ALU.mult).then_inc(bt_done[l], 1)

                for t in range(TILES):
                    for h in range(2):
                        if t == 0:
                            dve.wait_ge(w_ps[l], h + 1)
                        else:
                            dve.wait_ge(chunk_done, mixer_used(l, f"W{h}"))
                        ins = dve.tensor_tensor(x[:, t, xcols(h)], x[:, t, xcols(h)], ps[:, W_BANK[h][t], :], ALU.add)
                    ins.then_inc(x_done, 1)

            def low(dst, src, high, signal):
                dve.tensor_tensor(dst, src, high.bitcast(F32), ALU.subtract).then_inc(signal, 1)

            def dense_ff():
                def chunk(kind, s, first=0, last=4):
                    for v, src in ff_parts(kind, s)[first:last]:
                        n = src.shape[1]
                        high, lo = ex_unit(v, n * src.shape[2])
                        dve.wait_ge(hi_done, v + 1)
                        low(as_block(lo, n), src, as_block(high, n), lo_done)

                for b in range(4):
                    t, half = divmod(b, 2)
                    chunk("g", 0, b, b + 1)
                    dve.wait_ge(hTh_done, b + 1)
                    at = (slice(4 * half, 4 * half + 4), slice(t * P, (t + 1) * P))
                    low(hTs[:, 1, at[0], at[1]], hT[:, at[0], at[1]], hTs[:, 0, at[0], at[1]], hTl_done)
                after = tasks(FF_STEPS)
                for n, (kind, s) in enumerate(ff_order(FF_STEPS)):
                    if n:
                        chunk(kind, s)
                    for what, j in after.get(n, ()):
                        nq = ff_quarters(j)
                        if what == "act":
                            dve.wait_ge(ff_sd, j + 1)
                            dve.wait_ge(unit_done, FF_UNIT[("u", j)] + nq)
                            dve.tensor_tensor(ff_act[:, 0:nq * SEQ].rearrange("p (b n) -> p b n", n=512),
                                              ff_act[:, 0:nq * SEQ].rearrange("p (b n) -> p b n", n=512),
                                              ps[:, 2:2 + nq // 2, :], ALU.mult).then_inc(ff_ad, 1)
                        elif what == "parts":
                            dve.wait_ge(ff_ah, j + 1)
                            low(acts[:, 1, 0:nq * SEQ], ff_act[:, 0:nq * SEQ], acts[:, 0, 0:nq * SEQ], ff_al)
                dve.wait_ge(x_done, 2)
                for t in range(TILES):
                    if t == 0:
                        dve.wait_ge(ff_ps, 1)
                    else:
                        dve.wait_ge(unit_done, FF_UNITS)
                    dve.tensor_tensor(x[:, t, :], x[:, t, :],
                                      ps[:, 4 + 2 * t:6 + 2 * t, :].rearrange("p a b -> p (a b)"),
                                      ALU.add).then_inc(x_done, 1)

            def router():
                dve.wait_ge(logit_ps, 1)
                link(dve.tensor_copy(logits[:, :, :].rearrange("p t e -> p (t e)"), ps[:, 0, 0:TILES * EXPERTS]))
                for t in range(TILES):
                    link(dve.max(top[:, t, :], logits[:, t, :]))
                    link(dve.max_index(top_i[:, t, :], top[:, t, :], logits[:, t, :]))
                link(dve.tensor_copy(top_f[:, :, :], top_i[:, :, :]))
                dve.tensor_tensor(route[:, 0, :], top[:, :, 1], top[:, :, 0], ALU.subtract).then_inc(top_done, 1)
                dve.wait_ge(route_exp, 1)
                link(dve.tensor_scalar(route[:, 2, :], route[:, 1, :], 1.0, None, ALU.add))
                link(dve.reciprocal(route[:, 2, :], route[:, 2, :]))
                link(dve.tensor_tensor(route[:, 3, :], route[:, 1, :], route[:, 2, :], ALU.mult))
                iota8 = cst("iota")[:, 0:EXPERTS]
                for t in range(TILES):
                    for r in range(2):
                        idx = top_f[:, t, r:r + 1]
                        link(dve.tensor_scalar(hot[:, r, t, :], iota8, idx, None, ALU.is_equal))
                        link(dve.tensor_scalar(hot[:, 2 + r, t, :], iota8, idx, route[:, 2 + r, t:t + 1],
                                               ALU.is_equal, ALU.mult))
                dve.tensor_tensor(chosen[:, :, :], hot[:, 0], hot[:, 1], ALU.add).then_inc(chosen_done, 1)
                link(dve.memset(gate[:, :, :], 0.0))
                link(dve.memset(place[:, :, :], -1.0))
                for r in range(ROUNDS):
                    link(dve.tensor_tensor(gate[:, :, r * EXPERTS:(r + 1) * EXPERTS], hot[:, 2], hot[:, 3], ALU.add))
                dve.wait_ge(count_ps, 1)
                dve.wait_ge(chosen_done, 1)
                rank = ps[:, 1, 0:TILES * EXPERTS].rearrange("p (t e) -> p t e", t=TILES)
                link(dve.tensor_tensor(place[:, :, 0:EXPERTS], rank, chosen[:, :, :], ALU.mult))
                link(dve.tensor_scalar(place[:, :, 0:EXPERTS], place[:, :, 0:EXPERTS], -1.0, None, ALU.add))
                for r in range(1, ROUNDS):
                    link(dve.tensor_scalar(place[:, :, r * EXPERTS:(r + 1) * EXPERTS], place[:, :, 0:EXPERTS],
                                           -float(r * SLOTS), None, ALU.add))
                link(dve.tensor_reduce(most[:, :], ps[:, 1, 16:16 + EXPERTS], AX.X, ALU.max))
                dve.tensor_copy(most_i[:, :], most[:, :]).then_inc(count_done, 1)
                dve.sem_inc(y_added, 4)

            def select(i, n):
                for t in range(TILES):
                    p_i = place[:, t, bass.ds(i, 1)]
                    dve.tensor_scalar(sel[:, t, :], cst("iota")[:, 0:SLOTS], p_i, None, ALU.is_equal)
                    ins = dve.tensor_scalar(sel_g[:, t, :], cst("iota")[:, 0:SLOTS], p_i,
                                            gate[:, t, bass.ds(i, 1)], ALU.is_equal, ALU.mult)
                ins.then_inc(sel_done, 1)

            def gathered(n):
                dve.wait_ge(gather_ps, n)
                if not isinstance(n, int):
                    dve.wait_ge(xgh_done, n - 1)
                dve.tensor_tensor(xgT, ps[:, 6:8, :].rearrange("p a (c n) -> p (a c) n", n=SLOTS),
                                  bc(gains(3), 2, [P, KC, SLOTS]), ALU.mult).then_inc(xg_done, 1)
                dve.wait_ge(xgh_done, n)
                low(xgTs[:, 1], xgT, xgTs[:, 0], xgT_done)

            def expert_items(first):
                with dve.Fori(first, first + EXPERTS) as i:
                    after = tasks(EX_STEPS)
                    for c, (kind, s) in enumerate(ff_order(EX_STEPS)):
                        for u in range(4):
                            v = FF_UNITS + 4 * c + u
                            high, lo = ex_unit(v)
                            dve.wait_ge(hi_done, i * EX_UNITS + (v + 1))
                            low(lo, ex_part(c, u), high, lo_done)
                        for what, j in after.get(c, ()):
                            if what == "act":
                                dve.wait_ge(silu_done, i * EX_STEPS + (j + 1))
                                dve.wait_ge(unit_done, i * EX_UNITS + (FF_UNITS + 4 * EX_POS[("u", j)] + 4))
                                dve.tensor_tensor(ex_act, ex_act, ps[:, 1, :], ALU.mult).then_inc(act_done, 1)
                            elif what == "parts":
                                dve.wait_ge(acth_done, i * EX_STEPS + (j + 1))
                                low(ex_actTs[:, 1], ps[:, 4, :].rearrange("p (q n) -> p q n", q=4),
                                    ex_actTs[:, 0], actl_done)
                        if c == 1:
                            dve.wait_ge(selT_ps, i + 1)
                            select(i + 1, i + 2)
                    gathered(i + 2)
                    for q in range(4):
                        t, h = divmod(q, 2)
                        dve.wait_ge(scatter_ps, i * 4 + (q + 1))
                        dve.wait_ge(y_added, i * 4 + (q + 1))
                        dve.tensor_tensor(x[:, t, xcols(h)], x[:, t, xcols(h)], ps[:, SCATTER[q], :],
                                          ALU.add).then_inc(y_added, 1)

            def lambdas():
                dve.wait_ge(small_in, SMALL_IN)
                for i in range(2):
                    for l in range(DEPTH):
                        link(dve.tensor_tensor(lam_junk[:, :], lam_in[:, 2 * i, l, :], lam_in[:, 2 * i + 1, l, :], ALU.mult))
                        link(dve.tensor_reduce(lam_s[:, i, l:l + 1], lam_junk[:, :], AX.X, ALU.add))
                dve.sem_inc(lam_sum, 1)
                dve.wait_ge(lam_exp, 1)
                link(dve.tensor_tensor(neg_lam[:, :], lam_s[:, 1, :], lam_s[:, 0, :], ALU.subtract))
                for l in range(DEPTH):
                    link(dve.tensor_scalar(neg_lam[:, l:l + 1], neg_lam[:, l:l + 1],
                                           -(0.8 - 0.6 * math.exp(-0.3 * l)), None, ALU.add))

            dve.wait_ge(first_in, FIRST_IN)
            dve.wait_ge(g_ps, 1)
            dve.tensor_copy(g_cols[:, :], ps[:, 7, 0:GAIN_ROWS]).then_inc(g_done, 1)
            dve.wait_ge(g_done, 1)
            for l in range(DEPTH):
                mixer(l)
                norm_T(2 * l + 1)
                if l == 0:
                    dense_ff()
            router()
            dve.wait_ge(count_done, 1)
            select(0, 1)
            gathered(1)
            expert_items(0)
            dve.wait_ge(y_added, 4 + 4 * EXPERTS)
            count = dve.value_load(most_i[0:1, 0:1], min_val=0, max_val=SEQ)
            for r in range(1, ROUNDS):
                with dve.If(count > r * SLOTS):
                    expert_items(r * EXPERTS)
                    dve.wait_ge(y_added, 4 + 4 * (r + 1) * EXPERTS)
            dve.sem_inc(x_final, 1)
            dve.wait_ge(gfin_in, 16)
            for t in range(TILES):
                dve.wait_ge(rstd_done, 2 * TILES * DEPTH + t + 1)
                dve.scalar_tensor_tensor(x[:, t, :], x[:, t, :], rstd[:, 2 * DEPTH, t:t + 1], g_fin,
                                         ALU.mult, ALU.mult).then_inc(out_ready, 1)

        @block.tensor
        def _(pe):
            def norm_T(n):
                for b in range(4):
                    t, half = divmod(b, 2)
                    pe.wait_ge(hn_done, TILES * n + t + 1)
                    if b >= 2:
                        pe.wait_ge(hT_done, 4 * n + b - 1)
                    for c in range(4):
                        k = 4 * half + c
                        ins = pe.transpose(ps[:, 2 + b % 2, c * P:(c + 1) * P],
                                           hn[:, t, k * P:(k + 1) * P], ident)
                    ins.then_inc(hT_ps, 1)

            def arrived(n):
                pe.wait_ge(slot_in[n % RING], landed[n])

            def mixer(l):
                def batch(b):
                    if b >= 2:
                        pe.wait_ge(bt_done[l], b - 1)
                    return ps[:, 2 + b % 2, :]

                def z_chunk(c, t):
                    n = mixer_chunk(l, f"Z{c}")
                    wid = Z_COLS[c][1] - Z_COLS[c][0]
                    w_c = slot_view(n, 0, (KC, wid))
                    if t == 0:
                        arrived(n)
                    if c:
                        pe.wait_ge(z_done[l], 2 * (c - 1) + t + 1)
                    else:
                        pe.wait_ge(hT_done, 4 * 2 * l + 2 * t + 2)
                    for k in range(KC):
                        ins = pe.matmul(ps[:, t, 0:wid], hT[:, k, t * P:(t + 1) * P], w_c[:, k, :],
                                        start=(k == 0), stop=(k == KC - 1))
                    ins.then_inc(chunk_done if t else z_ps[l], 1)

                def values(g, kb, h):
                    if g == "A":
                        return vA[:, kb, h * HEAD_DIM:(h + 1) * HEAD_DIM]
                    c = {"B": VB, "C": VCOL, "D": VD}[g] + h * HEAD_DIM
                    return z[:, kb, c:c + HEAD_DIM]

                def y_times_w(h, t, ks):
                    w_h = slot_view(mixer_chunk(l, f"W{h}"), 0, (KC, FW))
                    for k in ks:
                        ins = pe.matmul(ps[:, W_BANK[h][t], :], yT[:, k, t * P:(t + 1) * P], w_h[:, k, :],
                                        start=(k == 0), stop=(k == KC - 1))
                    return ins

                def scores(k):
                    g, t, n, s0, nk = JOBS[k]
                    pe.wait_ge(bt_done[l], NEED[g])
                    if k:
                        pe.wait_ge(mask_done[l], k)
                    places = score_places(k)
                    for s in range(n):
                        if g in "AC":
                            rows = QK_A if g == "A" else AUG
                            q, kk = wideT[0:rows, 0, s, :], wideT[0:rows, 1, s, :]
                        elif g == "B":
                            r = 64 * (s % 2)
                            q, kk = pairT[r:r + 64, 0, s // 2, :], pairT[r:r + 64, 1, s // 2, :]
                        else:
                            u, r = divmod(s0 + s, 4)
                            q, kk = pairT[32 * r:32 * r + 32, 0, u, :], pairT[32 * r:32 * r + 32, 1, u, :]
                        ins = pe.matmul(places[:, spot(k, s), 0:nk], q[:, t * P:(t + 1) * P], kk[:, 0:nk],
                                        start=True, stop=True)
                    ins.then_inc(s_ps[l], 1)

                def transposed(k):
                    g, _, _, _, nk = JOBS[k]
                    pe.wait_ge(exp_done[l], k + 1)
                    if g == "D":
                        pe.wait_ge(comb_done[l], k + 1)
                    for b, blocks in enumerate(head_blocks(k)):
                        done = pt_done(k) - pt_batches(k) + b
                        if done:
                            pe.wait_ge(pt_ev[l], done)
                        else:
                            pe.wait_ge(ukv_done[l], TILES)
                        for i, (s, kb, _) in enumerate(blocks):
                            ins = pe.transpose(ps[:, 7, i * P:(i + 1) * P],
                                               E[:, k % 2, s * nk + kb * P:s * nk + (kb + 1) * P], ident)
                        ins.then_inc(pt_ps[l], 1)

                def times_values(k):
                    g, _, n, s0, nk = JOBS[k]
                    nh = n // 2 if g == "D" else n
                    pe.wait_ge(pt_ev[l], pt_done(k))
                    if k:
                        pe.wait_ge(y_done[l], k)
                    else:
                        pe.wait_ge(uq_done[l], TILES)
                    if g == "A":
                        pe.wait_ge(ukv_done[l], TILES)
                    pe.wait_ge(z_done[l], 2 * {"D": 3, "A": 1, "B": 5, "C": 6}[g])
                    for h in range(nh):
                        c = h * HEAD_DIM
                        for kb in range(nk // P):
                            ins = pe.matmul(ps[:, 6, c:c + HEAD_DIM], pT[:, k % 2, kb * nh + h, :],
                                            values(g, kb, s0 // 2 + h),
                                            start=(kb == 0), stop=(kb == nk // P - 1))
                    ins.then_inc(pv_ps[l], 1)

                norm_T(2 * l)
                for step in MIXER:
                    if step[0] == "Z":
                        z_chunk(int(step[1]), int(step[2]))
                    elif step == "LT":
                        for t, b in enumerate(BATCH["LT"]):
                            pe.wait_ge(lat_done[l], t + 1)
                            bank = batch(b)
                            for c in range(3):
                                ins = pe.transpose(bank[:, c * P:(c + 1) * P], latn[:, t, c * P:(c + 1) * P], ident)
                            ins.then_inc(bt_ps[l], 1)
                    elif step == "LM":
                        n = mixer_chunk(l, "LM")
                        arrived(n)
                        w_uq = slot_view(n, 0, (2, HEADS * QK_A))
                        w_ukv = slot_view(n, 2 * HEADS * QK_A, (1, 2 * GROUP))
                        for t in range(TILES):
                            tok = slice(t * P, (t + 1) * P)
                            pe.wait_ge(bt_done[l], t + 1)
                            if t:
                                pe.wait_ge(uq_done[l], t)
                            for c in range(2):
                                ins = pe.matmul(ps[:, 6, 0:HEADS * QK_A], latT[:, c, tok], w_uq[:, c, :],
                                                start=(c == 0), stop=(c == 1))
                            ins.then_inc(lm_ps[l], 1)
                            if t:
                                pe.wait_ge(ukv_done[l], t)
                            ins = pe.matmul(ps[:, 7, :], latT[:, 2, tok], w_ukv[:, 0, :], start=True, stop=True)
                            ins.then_inc(chunk_done if t else lm_ps[l], 1)
                    elif step in ("QB", "QD"):
                        first = QB if step == "QB" else QD
                        for t, b in enumerate(BATCH[step]):
                            pe.wait_ge(rope_done[l], ROPES[step[1]] + t + 1)
                            bank = batch(b)
                            for c in range(4):
                                ins = pe.transpose(bank[:, c * P:(c + 1) * P],
                                                   z[:, t, first + c * P:first + (c + 1) * P], ident)
                            ins.then_inc(bt_ps[l], 1)
                    elif step in ("QA", "QC"):
                        for i, b in enumerate(BATCH[step]):
                            t, qk = divmod(i, 2)
                            if step == "QA":
                                pe.wait_ge(mask_done[l], D_JOBS)
                                pe.wait_ge(rope_done[l], ROPES["A"] + t + 1)
                                pe.wait_ge(ukv_done[l], t + 1)
                                src = (kA[:, t] if qk else qA[:, t, :].rearrange("p (h d) -> p h d", h=HEADS))
                                rows = QK_A
                            else:
                                pe.wait_ge(aug_done[l], 2 * TILES)
                                pe.wait_ge(bt_done[l], BATCH["CS"][0] + 1)
                                src, rows = (kC if qk else qC)[:, t], AUG
                            bank = batch(b)
                            for h in range(HEADS):
                                ins = pe.transpose(bank[0:rows, h * P:(h + 1) * P], src[:, h, :], ident)
                            ins.then_inc(bt_ps[l], 1)
                    elif step == "CS":
                        pe.wait_ge(lf_done[l], 1)
                        bank = batch(BATCH["CS"][0])
                        pe.matmul(bank[:, 0:HEADS], tri, fg[:, 5, 0, :], start=True, stop=True)
                        pe.matmul(bank[:, HEADS:2 * HEADS], ones, fg[:, 5, 0, :], start=True, stop=False)
                        pe.matmul(bank[:, HEADS:2 * HEADS], tri, fg[:, 5, 1, :], start=False,
                                  stop=True).then_inc(bt_ps[l], 1)
                    elif step in ("Y0", "Y1"):
                        half = int(step[1])
                        pe.wait_ge(y_done[l], NJ if half else NJ - 2)
                        pe.wait_ge(yd_done[l], TILES)
                        for t, b in enumerate(BATCH[step]):
                            bank = batch(b)
                            for c in range(4):
                                k = 4 * half + c
                                ins = pe.transpose(bank[:, c * P:(c + 1) * P], y[:, t, k * P:(k + 1) * P], ident)
                            ins.then_inc(bt_ps[l], 1)
                    elif step == "WA":
                        arrived(mixer_chunk(l, "W0"))
                        for t in range(TILES):
                            pe.wait_ge(bt_done[l], BATCH["Y0"][t] + 1)
                            pe.wait_ge(z_done[l], 2 * NZ)
                            y_times_w(0, t, range(4))
                    else:
                        k = int(step[1:])
                        if k < NJ:
                            scores(k)
                        if 1 <= k <= NJ:
                            transposed(k - 1)
                        if k >= 2:
                            times_values(k - 2)

                arrived(mixer_chunk(l, "W1"))
                for t in range(TILES):
                    pe.wait_ge(bt_done[l], BATCH["Y1"][t] + 1)
                    y_times_w(0, t, range(4, KC)).then_inc(chunk_done if t else w_ps[l], 1)
                    y_times_w(1, t, range(KC)).then_inc(chunk_done if t else w_ps[l], 1)

            def three(dst, a, b, first, last):
                for i, (ia, ib) in enumerate(((0, 0), (0, 1), (1, 0))):
                    ins = pe.matmul(dst, a[ia], b[ib], start=(first and i == 0), stop=(last and i == 2))
                return ins

            def dense_ff():
                pe.wait_ge(hTl_done, 4)
                for kind, s in ff_order(FF_STEPS):
                    nq = ff_quarters(s)
                    if kind == "d":
                        pe.wait_ge(ff_al, s + 1)
                    elif kind == "g" and s:
                        pe.wait_ge(ff_sd, s)
                    elif s:
                        pe.wait_ge(ff_ad, s)
                    for q in range(nq):
                        v = FF_UNIT[(kind, s)] + q
                        pe.wait_ge(lo_done, v + 1)
                        parts = ex_unit(v)
                        if kind == "d":
                            last = s == FF_STEPS - 1 and q == nq - 1
                            for t in range(TILES):
                                a = q * SEQ + t * P
                                for h in range(2):
                                    ins = three(ps[:, 4 + 2 * t + h, :], [acts[:, i, a:a + P] for i in range(2)],
                                                [p[:, xcols(h)] for p in parts], s == 0 and q == 0, last)
                                if last and t == 0:
                                    ins.then_inc(ff_ps, 1)
                        else:
                            first = 0 if kind == "g" else 2
                            dst = ps[:, first + q // 2, (q % 2) * SEQ:(q % 2 + 1) * SEQ]
                            for k in range(KC):
                                ins = three(dst, [p[:, k * P:(k + 1) * P] for p in parts],
                                            [hTs[:, i, k, :] for i in range(2)], k == 0, k == KC - 1)
                        ins.then_inc(unit_done, 1)

            def router():
                pe.wait_ge(hT_done, 4 * 4)
                pe.wait_ge(small_in, SMALL_IN)
                for t in range(TILES):
                    for k in range(KC):
                        ins = pe.matmul(ps[:, 0, t * EXPERTS:(t + 1) * EXPERTS], hT[:, k, t * P:(t + 1) * P],
                                        w_r[:, k, :], start=(k == 0), stop=(k == KC - 1))
                ins.then_inc(logit_ps, 1)
                pe.wait_ge(chosen_done, 1)
                bank = ps[:, 1, :]
                pe.matmul(bank[:, 0:8], tri, chosen[:, 0, :], start=True, stop=True)
                for first, last in ((8, tri), (16, ones)):
                    pe.matmul(bank[:, first:first + 8], ones, chosen[:, 0, :], start=True, stop=False)
                    ins = pe.matmul(bank[:, first:first + 8], last, chosen[:, 1, :], start=False, stop=True)
                ins.then_inc(count_ps, 1)

            def gather(n):
                pe.wait_ge(sel_done, n)
                for c in range(KC):
                    for t in range(TILES):
                        ins = pe.matmul(ps[:, 6 + c // 4, (c % 4) * SLOTS:(c % 4 + 1) * SLOTS],
                                        hn[:, t, c * P:(c + 1) * P], sel[:, t, :],
                                        start=(t == 0), stop=(t == TILES - 1))
                ins.then_inc(gather_ps, 1)

            def turn_selection(n):
                pe.wait_ge(xg_done, n)
                for t in range(TILES):
                    ins = pe.transpose(ps[:, 6, t * P:(t + 1) * P], sel_g[:, t, :], ident)
                ins.then_inc(selT_ps, 1)

            def expert_items(first):
                with pe.Fori(first, first + EXPERTS) as i:
                    def unit(c, u):
                        v = FF_UNITS + 4 * c + u
                        pe.wait_ge(lo_done, i * EX_UNITS + (v + 1))
                        return ex_unit(v)

                    def product(kind, j):
                        bank = 0 if kind == "g" else 1
                        if j == 0:
                            pe.wait_ge(y_added, i * 4 + (bank + 1))
                        elif kind == "g":
                            pe.wait_ge(silu_done, i * EX_STEPS + j)
                        else:
                            pe.wait_ge(act_done, i * EX_STEPS + j)
                        for u in range(4):
                            parts = unit(EX_POS[(kind, j)], u)
                            for k in range(2):
                                ins = three(ps[:, bank, :], [xgTs[:, h, 2 * u + k, :] for h in range(2)],
                                            [p[:, k * FW:(k + 1) * FW] for p in parts],
                                            u == 0 and k == 0, u == 3 and k == 1)
                            ins.then_inc(unit_done, 1)

                    def turn(j):
                        pe.wait_ge(act_done, i * EX_STEPS + (j + 1))
                        if j == 0:
                            pe.wait_ge(y_added, i * 4 + 4)
                        else:
                            pe.wait_ge(actl_done, i * EX_STEPS + j)
                        for q in range(4):
                            ins = pe.transpose(ps[:, 4, q * P:(q + 1) * P], ex_act[:, q * P:(q + 1) * P], ident)
                        ins.then_inc(actT_ps, 1)

                    def down(j):
                        pe.wait_ge(actl_done, i * EX_STEPS + (j + 1))
                        for q in range(4):
                            parts = unit(EX_POS[("d", j)], q)
                            for h in range(2):
                                ins = three(ps[:, 2 + h, :], [ex_actTs[:, p, q, :] for p in range(2)],
                                            [p[:, xcols(h)] for p in parts],
                                            j == 0 and q == 0, j == EX_STEPS - 1 and q == 3)
                            ins.then_inc(unit_done, 1)

                    pe.wait_ge(xgT_done, i + 1)
                    after = tasks(EX_STEPS)
                    for c, (kind, s) in enumerate(ff_order(EX_STEPS)):
                        if kind == "d":
                            if s == EX_STEPS - 1:
                                pe.wait_ge(selT_done, i + 1)
                                gather(i + 2)
                            down(s)
                        else:
                            product(kind, s)
                        for what, j in after.get(c, ()):
                            if what == "act":
                                turn(j)
                    for q in range(4):
                        t, h = divmod(q, 2)
                        pe.wait_ge(eo_done, i * 2 + (h + 1))
                        pe.matmul(ps[:, SCATTER[q], :], sel_gT[:, t * P:(t + 1) * P], ex_out[:, xcols(h)],
                                  start=True, stop=True).then_inc(scatter_ps, 1)
                    turn_selection(i + 2)

            pe.wait_ge(first_in, FIRST_IN)
            pe.transpose(ps[:, 7, 0:GAIN_ROWS], g_rows[:, :], ident[0:GAIN_ROWS, 0:GAIN_ROWS]).then_inc(g_ps, 1)
            for l in range(DEPTH):
                mixer(l)
                norm_T(2 * l + 1)
                if l == 0:
                    dense_ff()
            router()
            gather(1)
            turn_selection(1)
            expert_items(0)
            pe.wait_ge(count_done, 1)
            count = pe.value_load(most_i[0:1, 0:1], min_val=0, max_val=SEQ)
            for r in range(1, ROUNDS):
                with pe.If(count > r * SLOTS):
                    expert_items(r * EXPERTS)


W_BANK = ((0, 1), (4, 5))
SCATTER = (0, 1, 5, 4)
FIRST_IN = 16 * 9
SMALL_IN = 16 * 6
GAIN_AT = {"g_mix": 0, "g_ffn": DEPTH * KC, "latent": 2 * DEPTH * KC, "g_diff_sub": 2 * DEPTH * KC + 3 * DEPTH}
GAIN_ROWS = 2 * DEPTH * KC + 4 * DEPTH

_INS = ["x", "g_mix", "w_in", "b_forget", "g_q_lat", "g_kv_lat", "w_uq", "w_ukv", "lambda_q1",
        "lambda_k1", "lambda_q2", "lambda_k2", "g_diff_sub", "w_out", "g_ffn", "w_ffn_gate",
        "w_ffn_up", "w_ffn_down", "w_router", "w_exp_gate", "w_exp_up", "w_exp_down", "g_final"]


def kernel(**inputs):
    import concourse.bacc as _bacc
    from concourse.bass_utils import run_bass_kernel_spmd as _run

    nc = _bacc.Bacc("TRN2", target_bir_lowering=False, num_devices=1)
    arrays = {n: np.ascontiguousarray(inputs[n]) for n in _INS}
    arrays["const"] = CONSTANTS
    w = {n: nc.dram_tensor(f"in_{n}", a.shape, F32, kind="ExternalInput").ap() for n, a in arrays.items()}
    out = nc.dram_tensor("out", (1, SEQ, D_MODEL), F32, kind="ExternalOutput").ap()
    with nc.allow_non_contiguous_dma(reason="gains of a few kilobytes, one element per partition"):
        build(nc, w, out)
    r = _run(nc, [{f"in_{n}": a for n, a in arrays.items()}], core_ids=[0])
    return r.results[0]["out"]
```

```python
import math
from contextlib import ExitStack

import concourse.bass as bass
import numpy as np
from concourse import mybir

F32 = mybir.dt.float32
F32R = mybir.dt.float32r
I32 = mybir.dt.int32
U32 = mybir.dt.uint32
ALU = mybir.AluOpType
ACT = mybir.ActivationFunctionType
AX = mybir.AxisListType

P = 128
D_MODEL, SEQ, DEPTH = 1024, 256, 2
TILES = SEQ // P
KC = D_MODEL // P
HEADS, HEAD_DIM = 4, 64
GROUP = HEADS * HEAD_DIM
Q_RANK, KV_RANK, NOPE, ROT = 256, 128, 64, 32
QK_A = NOPE + ROT
DIFF_QK = 32
IN_WIDTH = 2724
D_FF, D_FF_EXPERT, EXPERTS = 2816, 3584, 8
EPS = 1e-6
NEG = -1e30
DIL_CONFIGS = ((128, 1), (512, 4), (2048, 16))
AUG = HEAD_DIM + 2

CQ, CKV, KR = 0, 256, 384
QB, KB_, VB = 416, 672, 928
QCOL, KCOL, VCOL, FCOL = 1184, 1440, 1696, 1952
QD, KD, VD = 1956, 2212, 2468
Z_COLS = ((0, 416), (QD, VD), (VD, IN_WIDTH), (QB, VB), (VB, KCOL), (KCOL, FCOL))
NZ = len(Z_COLS)

RING = 7
SLOT = 4096
FW = 512
FF_STEPS = -(-D_FF // FW)
EX_STEPS = D_FF_EXPERT // FW
EX_CHUNKS = 3 * EX_STEPS
assert EX_CHUNKS % RING == 0
SLOTS = 128
ROUNDS = -(-SEQ // SLOTS)
ITEMS = EXPERTS * ROUNDS

JOBS = (("D", 0, 8, 0, 128), ("D", 1, 4, 0, 256), ("D", 1, 4, 4, 256), ("A", 0, 4, 0, 128),
        ("A", 1, 4, 0, 256), ("B", 0, 4, 0, 128), ("B", 1, 4, 0, 256), ("C", 0, 4, 0, 128),
        ("C", 1, 4, 0, 256))
NJ = len(JOBS)
SCALE = {"A": QK_A ** -0.5, "B": HEAD_DIM ** -0.5, "C": 1.0, "D": DIFF_QK ** -0.5}
YCOL = {"A": 0, "B": GROUP, "C": 2 * GROUP, "D": 3 * GROUP}
D_JOBS = 3

MIXER = ["Z00", "Z01", "Z10", "Z11", "LT", "Z20", "QD", "LM", "J0", "Z21", "Z30", "J1", "F1", "Z31", "J2",
         "F2", "Z40", "QA", "J3", "Z41", "J4", "QB", "Z50", "CS", "J5", "Z51", "J6", "QC", "Y0", "J7",
         "W0", "J8", "W1", "YB", "J9", "WB", "H0", "J10", "H1", "YC"]

BATCH = {"LT": (0, 1), "QD": (2, 3), "QA": (4, 5, 6, 7), "QB": (8, 9), "CS": (10,), "QC": (11, 12, 13, 14),
         "Y0": (15, 16), "YB": (17,), "YC": (18, 19)}
NEED = {"D": 4, "A": 8, "B": 10, "C": 15}
ROPES = {"D": 0, "A": 2}
Y_FIRST, Y_REST = (6, 7, 0, 1), (2, 3)


def pt_batches(k):
    return JOBS[k][4] // P if JOBS[k][0] != "D" else 1


def spot(k, s):
    g, _, n, _, _ = JOBS[k]
    if g == "B":
        return (s % 2) * 2 + s // 2
    return (s % 4) * 2 + s // 4 if n == 8 else s


def head_blocks(k):
    g, _, n, _, nk = JOBS[k]
    heads = range(n) if g != "D" else range(0, n, 2)
    nh = len(heads)
    all_ = [(spot(k, s), kb, kb * nh + i) for kb in range(nk // P) for i, s in enumerate(heads)]
    return [all_[i:i + 4] for i in range(0, len(all_), 4)]


def pt_done(k):
    return sum(pt_batches(j) for j in range(k + 1))


CONST = {}


def _constants():
    p = np.arange(P)[:, None]
    d1 = P + p - np.arange(SEQ)[None, :]
    count = sum(((d1 >= 0) & (d1 % dil == 0) & (d1 <= win)).astype(int) for win, dil in DIL_CONFIGS)
    parts = [
        ("ident", np.eye(P)),
        ("causal", np.where(d1 >= 0, 0.0, NEG)),
        ("dilated", np.where(count > 0, np.log(np.maximum(count, 1)), NEG)),
        ("tri", (p <= np.arange(P)[None, :]).astype(float)),
        ("ones", np.ones((P, P))),
        ("iota", np.broadcast_to(np.arange(P), (P, P))),
    ]
    for half in (16, 32):
        inv = np.float32(10000.0) ** (-np.arange(half, dtype=np.float32) / np.float32(half))
        for t in range(TILES):
            ang = (np.arange(P, dtype=np.float32)[:, None] + P * t) * inv[None, :].astype(np.float32)
            parts += [(f"cos{half}_{t}", np.cos(ang)), (f"sin{half}_{t}", np.sin(ang)),
                      (f"nsin{half}_{t}", -np.sin(ang))]
    at = 0
    for name, a in parts:
        CONST[name] = (at, a.shape[1])
        at += a.shape[1]
    return np.ascontiguousarray(np.concatenate([a for _, a in parts], axis=1).astype(np.float32))


CONSTANTS = _constants()


ALL = slice(None)


def plan_chunks(w):
    chunks = []

    def rows(src):
        return src.rearrange("(c p) f -> p c f", p=P)

    for l in range(DEPTH):
        for c in range(NZ):
            a, b = Z_COLS[c]
            if c == 2:
                chunks.append([(0, (2, HEADS * QK_A), ALL, rows(w["w_uq"][l])),
                               (2 * HEADS * QK_A, (1, 2 * GROUP), ALL, rows(w["w_ukv"][l]))])
            if c == 2:
                chunks.append([(0, (KC, b - a + HEADS), slice(0, b - a), rows(w["w_in"][l][:, a:b])),
                               (0, (KC, b - a + HEADS), slice(b - a, None),
                                rows(w["w_in"][l][:, FCOL:FCOL + HEADS]))])
            else:
                chunks.append([(0, (KC, b - a), ALL, rows(w["w_in"][l][:, a:b]))])
        for h in range(2):
            chunks.append([(0, (KC, FW), ALL, rows(w["w_out"][l][:, h * FW:(h + 1) * FW]))])
        if l == 0:
            for kind, s in ff_order(FF_STEPS):
                a, b = s * FW, min((s + 1) * FW, D_FF)
                if kind == "d":
                    chunks.append([(0, ((b - a) // P, D_MODEL), ALL, rows(w["w_ffn_down"][0][a:b, :]))])
                else:
                    src = w["w_ffn_gate"] if kind == "g" else w["w_ffn_up"]
                    chunks.append([(0, (KC, b - a), ALL, rows(src[0][:, a:b]))])
    return chunks


def tasks(steps):
    order = ff_order(steps)
    out = {}
    for j in range(steps):
        at = order.index(("u", j))
        for what, n in (("silu", at), ("act", at + 1), ("parts", at + 2)):
            out.setdefault(min(n, len(order) - 1), []).append((what, j))
    return out


def ff_order(steps):
    out = []
    for s in range(steps):
        out += [("g", s), ("u", s)]
        if s:
            out.append(("d", s - 1))
    return out + [("d", steps - 1)]


UNITS = 4
EX_UNITS = 4 * EX_CHUNKS
assert EX_UNITS % UNITS == 0
FF_UNITS = 3 * D_FF // P

L_CHUNKS = NZ + 1 + 2
FF_AT = L_CHUNKS
L1_AT = L_CHUNKS + 3 * FF_STEPS
EX_AT = L1_AT + L_CHUNKS
EX_POS = {c: i for i, c in enumerate(ff_order(EX_STEPS))}
FF_POS = {c: FF_AT + i for i, c in enumerate(ff_order(FF_STEPS))}


MIXER_CHUNKS = ["Z0", "Z1", "LM", "Z2", "Z3", "Z4", "Z5", "W0", "W1"]


def mixer_chunk(l, name):
    return (L1_AT if l else 0) + MIXER_CHUNKS.index(name)


def mixer_used(l, name):
    return l * L_CHUNKS + MIXER_CHUNKS.index(name) + 1


def ff_quarters(s):
    return min(4, (D_FF - s * FW) // P)


FF_UNIT = {c: sum(ff_quarters(s) for _, s in ff_order(FF_STEPS)[:i]) for i, c in enumerate(ff_order(FF_STEPS))}


def build(nc, w, out):
    chunks = plan_chunks(w)
    assert len(chunks) == EX_AT
    landed, fill = [], [0] * RING
    for n, loads in enumerate(chunks):
        fill[n % RING] += 16 * len(loads)
        landed.append(fill[n % RING])
    landed_ex = []
    for c in range(EX_CHUNKS):
        fill[(EX_AT + c) % RING] += 16
        landed_ex.append(fill[(EX_AT + c) % RING])
    EX_LAND = 16 * EX_CHUNKS // RING

    with ExitStack() as ctx:
        def sb(name, shape, dt=F32):
            return ctx.enter_context(nc.sbuf_tensor(name, shape, dt))

        def sem(name):
            return ctx.enter_context(nc.semaphore(name))

        ps = ctx.enter_context(nc.psum_tensor("ps", [P, 8, 512], F32))
        mixer_mem = ExitStack()

        def mx(name, shape, dt=F32):
            return mixer_mem.enter_context(nc.sbuf_tensor(name, shape, dt))

        ring = sb("ring", [P, RING, SLOT])
        x = sb("x", [P, TILES, D_MODEL])
        hn = sb("hn", [P, TILES, D_MODEL])
        y = hn
        hT = sb("hT", [P, KC, SEQ])
        yT = hT
        const = sb("const", [P, CONSTANTS.shape[1]])
        g_rows = sb("g_rows", [GAIN_ROWS, P])
        g_cols = sb("g_cols", [P, GAIN_ROWS])
        b_f = sb("b_f", [P, DEPTH, HEADS])
        lam_in = sb("lam_in", [P, 4, DEPTH, DIFF_QK])
        lam_s = sb("lam_s", [P, 2, DEPTH])
        lam_junk = sb("lam_junk", [P, DIFF_QK])
        neg_lam = sb("neg_lam", [P, DEPTH])
        w_r = sb("w_r", [P, KC, EXPERTS])
        sumsq = sb("sumsq", [P, 5, TILES])
        rstd = sb("rstd", [P, 5, TILES])
        half_neg = sb("half_neg", [P, 8])

        neg_max = sb("neg_max", [P, NJ, 8])
        row_sum = sb("row_sum", [P, NJ, 8])
        row_inv = sb("row_inv", [P, NJ, 8])
        lat_ss = sb("lat_ss", [P, TILES, 2])
        lat_r = sb("lat_r", [P, TILES, 2])
        fg = sb("fg", [P, 6, TILES, HEADS])
        d_ss = sb("d_ss", [P, 8])
        d_r = sb("d_r", [P, 8])
        logits = sb("logits", [P, TILES, EXPERTS])
        top = sb("top", [P, TILES, 8])
        top_i = sb("top_i", [P, TILES, 8], U32)
        top_f = sb("top_f", [P, TILES, 8])
        route = sb("route", [P, 4, TILES])
        hot = sb("hot", [P, 4, TILES, EXPERTS])
        most = sb("most", [P, 1])
        most_i = sb("most_i", [P, 1], I32)

        z = mx("z", [P, TILES, IN_WIDTH])
        kA = mx("kA", [P, TILES, HEADS, QK_A])
        vA = mx("vA", [P, TILES, GROUP])
        tmp_a = mx("tmp_a", [P, 512])
        tmp_b = mx("tmp_b", [P, 512])
        qC = mx("qC", [P, TILES, HEADS, AUG])
        kC = mx("kC", [P, TILES, HEADS, AUG])
        wideT = mx("wideT", [P, 2, HEADS, SEQ])
        pairT = mx("pairT", [P, 2, 2, SEQ])
        E = mx("E", [P, 2, 1024])
        pT = mx("pT", [P, 2, 8, P])
        qA = z[:, :, 0:HEADS * QK_A]
        latn = E[:, :, :].rearrange("p a b -> p (a b)")[:, 0:TILES * 384].rearrange("p (t n) -> p t n", t=TILES)
        latT = pT[:, :, :, :].rearrange("p a b c -> p (a b c)")[:, 0:3 * SEQ].rearrange("p (c n) -> p c n", c=3)

        mixer_mem.close()
        split = sb("split", [P, UNITS, 2, 1024], F32R)
        hTs = sb("hTs", [P, 2, KC, SEQ], F32R)
        acts = sb("acts", [P, 2, 4 * SEQ], F32R)
        ff_act = sb("ff_act", [P, 4 * SEQ])
        xgTs = hTs[:, :, :, :].rearrange("p i c n -> p (i c n)")[:, 0:2 * KC * SLOTS].rearrange(
            "p (i c n) -> p i c n", i=2, c=KC)
        ex_actTs = acts[:, :, 0:4 * SLOTS].rearrange("p i (q n) -> p i q n", q=4)
        ex_act = ff_act[:, 0:FW]
        ex_out = ff_act[:, 0:D_MODEL]
        xgT = hT[:, 0:4, :].rearrange("p c n -> p (c n)").rearrange("p (c n) -> p c n", c=KC)
        g_fin = hT[:, 0:4, :].rearrange("p c n -> p (c n)")
        logitT = ff_act[0:EXPERTS, 0:SEQ]
        sel = hT[:, 4, :].rearrange("p (t n) -> p t n", t=TILES)
        sel_g = hT[:, 5, :].rearrange("p (t n) -> p t n", t=TILES)
        sel_gT = hT[:, 6, :]
        at = TILES * EXPERTS
        chosen = hT[:, 7, 0:at].rearrange("p (t n) -> p t n", t=TILES)
        place, gate = (hT[:, 7, a:a + TILES * (ITEMS + 1)].rearrange("p (t n) -> p t n", t=TILES)
                       for a in (at, at + TILES * (ITEMS + 1)))

        def cst(name):
            a, n = CONST[name]
            return const[:, a:a + n]

        ident, tri, ones = cst("ident"), cst("tri"), cst("ones")

        x_in = [sem(f"x_in{t}") for t in range(TILES)]
        first_in = sem("first_in")
        small_in = sem("small_in")
        g_ps, g_done = sem("g_ps"), sem("g_done")
        gfin_in = sem("gfin_in")
        slot_in = [sem(f"slot_in{i}") for i in range(RING)]
        chunk_done = sem("chunk_done")
        sq_done = sem("sq_done")
        rstd_done = sem("rstd_done")
        hn_done = sem("hn_done")
        hT_ps = sem("hT_ps")
        hT_done = sem("hT_done")
        x_done = sem("x_done")
        dve_c, act_c, pool_c = sem("dve_c"), sem("act_c"), sem("pool_c")
        lam_sum, lam_exp = sem("lam_sum"), sem("lam_exp")

        def per_layer(name):
            return [sem(f"{name}_{l}") for l in range(DEPTH)]

        z_ps = per_layer("z_ps")
        z_done = per_layer("z_done")
        lat_sq = per_layer("lat_sq")
        lat_rs = per_layer("lat_rs")
        lat_done = per_layer("lat_done")
        lm_ps = per_layer("lm_ps")
        uq_done = per_layer("uq_done")
        ukv_done = per_layer("ukv_done")
        rope_done = per_layer("rope_done")
        rope_b = per_layer("rope_b")
        bt_ps = per_layer("bt_ps")
        bt_done = per_layer("bt_done")
        f_in = per_layer("f_in")
        f_log = per_layer("f_log")
        lf_done = per_layer("lf_done")
        aug_done = per_layer("aug_done")
        augq_done = per_layer("augq_done")
        s_ps = per_layer("s_ps")
        mask_done = per_layer("mask_done")
        max_done = per_layer("max_done")
        exp_done = per_layer("exp_done")
        comb_done = per_layer("comb_done")
        pt_ps = per_layer("pt_ps")
        pt_ev = per_layer("pt_ev")
        pv_ps = per_layer("pv_ps")
        y_done = per_layer("y_done")
        d_sq = per_layer("d_sq")
        d_rs = per_layer("d_rs")
        yd_done = per_layer("yd_done")
        w_ps = per_layer("w_ps")
        hi_done = sem("hi_done")
        lo_done = sem("lo_done")
        unit_done = sem("unit_done")
        hTh_done = sem("hTh_done")
        hTl_done = sem("hTl_done")
        ff_sd = sem("ff_silu")
        ff_ad = sem("ff_act")
        ff_ah = sem("ff_ah")
        ff_al = sem("ff_al")
        ff_ps = sem("ff_ps")
        logit_ps, top_done, route_exp, chosen_done = sem("logit_ps"), sem("top_done"), sem("route_exp"), sem("chosen_done")
        logitT_done = sem("logitT_done")
        count_ps, count_done = sem("count_ps"), sem("count_done")
        sel_done = sem("sel_done")
        gather_ps = sem("gather_ps")
        xg_done = sem("xg_done")
        xgh_done = sem("xgh_done")
        xgT_done = sem("xgT_done")
        selT_ps = sem("selT_ps")
        selT_done = sem("selT_done")
        silu_done = sem("silu_done")
        act_done = sem("act_done")
        actT_ps = sem("actT_ps")
        acth_done = sem("acth_done")
        actl_done = sem("actl_done")
        eo_done = sem("eo_done")
        scatter_ps = sem("scatter_ps")
        y_added = sem("y_added")
        x_final = sem("x_final")
        out_ready = sem("out_ready")
        stored = sem("stored")

        block = ctx.enter_context(nc.Block())

        def gains(n):
            a = GAIN_AT["g_ffn" if n % 2 else "g_mix"] + (n // 2) * KC
            return g_cols[:, a:a + KC]

        def bc(ap, axis, shape):
            return ap.unsqueeze(axis).to_broadcast(shape)

        def slot_view(n, first, shape):
            a, b = shape
            return ring[:, n % RING, first:first + a * b].rearrange("p (a b) -> p a b", a=a)

        def score_places(k):
            g, _, n, _, _ = JOBS[k]
            banks = ps[:, 2 if g == "D" else 4:6, :]
            return banks.rearrange("p a b -> p (a b)").rearrange("p (s n) -> p s n", s=n)

        def ex_unit(u, cols=1024):
            return split[:, u % UNITS, 0, 0:cols], split[:, u % UNITS, 1, 0:cols]

        def as_block(ap, n):
            return ap.rearrange("p (a b) -> p a b", a=n)

        def ff_parts(kind, s):
            n, nq = FF_POS[(kind, s)], ff_quarters(s)
            if kind == "d":
                w_c = slot_view(n, 0, (nq, D_MODEL))
                return [(FF_UNIT[(kind, s)] + q, w_c[:, q:q + 1, :]) for q in range(nq)]
            w_c = slot_view(n, 0, (KC, nq * P))
            return [(FF_UNIT[(kind, s)] + q, w_c[:, :, q * P:(q + 1) * P]) for q in range(nq)]

        def ex_part(c, u):
            return ring[:, (EX_AT + c) % RING, u * 1024:(u + 1) * 1024]

        def xcols(h):
            return slice(h * 512, (h + 1) * 512)

        @block.sync
        def _(sp):
            def load(n):
                m = n - RING
                if FF_AT <= m < L1_AT:
                    kind, s = ff_order(FF_STEPS)[m - FF_AT]
                    sp.wait_ge(lo_done, FF_UNIT[(kind, s)] + ff_quarters(s))
                elif m >= 0:
                    sp.wait_ge(chunk_done, m + 1 if m < L_CHUNKS else m - L1_AT + L_CHUNKS + 1)
                for first, shape, cols, src in chunks[n]:
                    sp.dma_start(slot_view(n, first, shape)[:, :, cols], src).then_inc(slot_in[n % RING], 16)

            def load_x(t):
                sp.dma_start(x[:, t, :], w["x"][0].rearrange("(t p) d -> p t d", p=P)[:, t, :]).then_inc(x_in[t], 16)

            load_x(0)
            first = [(const[:, :], w["const"])]
            for name in ("g_mix", "g_ffn"):
                a = GAIN_AT[name]
                first.append((g_rows[a:a + DEPTH * KC, :], w[name].rearrange("l (c p) -> (l c) p", p=P)))
            for l in range(DEPTH):
                a = GAIN_AT["latent"] + 3 * l
                first += [(g_rows[a:a + 2, :], w["g_q_lat"][l].rearrange("(c p) -> c p", p=P)),
                          (g_rows[a + 2:a + 3, :], w["g_kv_lat"][l].rearrange("(c p) -> c p", p=P))]
            a = GAIN_AT["g_diff_sub"]
            first += [(g_rows[a:a + DEPTH, h * HEAD_DIM:(h + 1) * HEAD_DIM], w["g_diff_sub"]) for h in range(2)]
            assert 16 * len(first) == FIRST_IN
            for dst, src in first:
                sp.dma_start(dst, src).then_inc(first_in, 16)
            load_x(1)
            load(0)
            small = [(w_r[:, :, :], w["w_router"][0].rearrange("(c p) e -> p c e", p=P)),
                     (b_f[:, :, :].rearrange("p l h -> p (l h)"),
                      w["b_forget"].rearrange("l h -> (l h)").partition_broadcast(P))]
            for i, name in enumerate(("lambda_q1", "lambda_k1", "lambda_q2", "lambda_k2")):
                small.append((lam_in[:, i, :, :].rearrange("p l n -> p (l n)"),
                              w[name].rearrange("l n -> (l n)").partition_broadcast(P)))
            assert 16 * len(small) == SMALL_IN
            for dst, src in small:
                sp.dma_start(dst, src).then_inc(small_in, 16)
            for n in range(1, EX_AT):
                load(n)

            gate_w = w["w_exp_gate"].rearrange("l e (c p) f -> p (l e c) f", p=P)
            up_w = w["w_exp_up"].rearrange("l e (c p) f -> p (l e c) f", p=P)
            down_w = w["w_exp_down"].rearrange("l e (q p) d -> p (l e q) d", p=P)
            FQ = D_FF_EXPERT // P

            def expert_chunk(i, e, c):
                n = EX_AT + c
                if c < RING:
                    sp.wait_ge(chunk_done, 2 * L_CHUNKS - RING + c + 1)
                sp.wait_ge(lo_done, i * EX_UNITS + (FF_UNITS + 4 * (c - RING + 1)))
                kind, s = ff_order(EX_STEPS)[c % EX_CHUNKS]
                if kind == "d":
                    dst = slot_view(n, 0, (4, D_MODEL))
                    src = down_w[:, bass.ds(e * FQ + 4 * s, 4), :]
                else:
                    dst = slot_view(n, 0, (KC, FW))
                    src = (gate_w if kind == "g" else up_w)[:, bass.ds(e * KC, KC), s * FW:(s + 1) * FW]
                sp.dma_start(dst, src).then_inc(slot_in[n % RING], 16)

            def expert_items(first):
                with sp.Fori(first, first + EXPERTS - 1) as i:
                    for c in range(1, EX_CHUNKS):
                        expert_chunk(i, i - first, c)
                    expert_chunk(i, i - first + 1, EX_CHUNKS)
                last = first + EXPERTS - 1
                for c in range(1, EX_CHUNKS):
                    expert_chunk(last, EXPERTS - 1, c)
                expert_chunk(last, 0, EX_CHUNKS)

            expert_chunk(0, 0, 0)
            expert_items(0)
            sp.wait_ge(count_done, 1)
            count = sp.value_load(most_i[0:1, 0:1], min_val=0, max_val=SEQ)
            for r in range(1, ROUNDS):
                with sp.If(count > r * SLOTS):
                    expert_items(r * EXPERTS)
            sp.wait_ge(x_final, 1)
            sp.dma_start(g_fin, w["g_final"].partition_broadcast(P)).then_inc(gfin_in, 16)
            for t in range(TILES):
                sp.wait_ge(out_ready, t + 1)
                sp.dma_start(out[0].rearrange("(t p) d -> p t d", p=P)[:, t, :], x[:, t, :]).then_inc(stored, 16)
            sp.wait_ge(stored, 16 * TILES)

        @block.gpsimd
        def _(pool):
            links = [0]

            def link(ins):
                links[0] += 1
                ins.then_inc(pool_c, 1)
                pool.wait_ge(pool_c, links[0])

            def rsqrt_mean(dst, src, n, width, signal):
                link(pool.tensor_scalar(dst, src, 1.0 / n, EPS, ALU.mult, ALU.add))
                pool.tensor_tensor(dst, dst, half_neg[:, 0:width], ALU.pow).then_inc(signal, 1)

            def norm(n):
                for t in range(TILES):
                    pool.wait_ge(sq_done, TILES * n + t + 1)
                    rsqrt_mean(rstd[:, n, t:t + 1], sumsq[:, n, t:t + 1], D_MODEL, 1, rstd_done)

            def rope_b_tile(l, t):
                shape = [P, 2 * HEADS, HEAD_DIM // 2]
                v = z[:, t, QB:QB + 2 * GROUP].rearrange("p (h i d) -> p h i d", h=2 * HEADS, i=2)
                a, b = (hn[:, i, GROUP:3 * GROUP].rearrange("p (h i d) -> p h i d", h=2 * HEADS, i=2)
                        for i in range(2))
                for i in range(2):
                    pool.tensor_tensor(a[:, :, i, :], v[:, :, i, :], bc(cst(f"cos32_{t}"), 1, shape), ALU.mult)
                pool.tensor_tensor(b[:, :, 0, :], v[:, :, 1, :], bc(cst(f"nsin32_{t}"), 1, shape), ALU.mult)
                link(pool.tensor_tensor(b[:, :, 1, :], v[:, :, 0, :], bc(cst(f"sin32_{t}"), 1, shape), ALU.mult))
                pool.tensor_tensor(v, a, b, ALU.add).then_inc(rope_b[l], 1)

            def mixer(l):
                norm(2 * l)
                pool.wait_ge(lat_sq[l], 1)
                link(pool.tensor_scalar(lat_r[:, :, 0], lat_ss[:, :, 0], 1.0 / Q_RANK, EPS, ALU.mult, ALU.add))
                link(pool.tensor_scalar(lat_r[:, :, 1], lat_ss[:, :, 1], 1.0 / KV_RANK, EPS, ALU.mult, ALU.add))
                flat = lat_r[:, :, :].rearrange("p a b -> p (a b)")
                pool.tensor_tensor(flat, flat, half_neg[:, 0:4], ALU.pow).then_inc(lat_rs[l], 1)
                for t in range(TILES):
                    pool.wait_ge(z_done[l], 2 * 3 + t + 1)
                    if t:
                        pool.wait_ge(rope_b[l], t)
                    rope_b_tile(l, t)
                pool.wait_ge(d_sq[l], 1)
                rsqrt_mean(d_r[:, :], d_ss[:, :], HEAD_DIM, 8, d_rs[l])
                for t in range(TILES):
                    pool.wait_ge(z_done[l], 2 * 4 + t + 1)
                    q = z[:, t, QCOL:QCOL + GROUP].rearrange("p (h d) -> p h d", h=HEADS)
                    pool.tensor_scalar(qC[:, t, :, 0:HEAD_DIM], q, HEAD_DIM ** -0.5, None,
                                       ALU.mult).then_inc(augq_done[l], 1)

            link(pool.memset(half_neg[:, :], -0.5))
            for l in range(DEPTH):
                mixer(l)
                norm(2 * l + 1)
            norm(2 * DEPTH)

        @block.scalar
        def _(act):
            links = [0]

            def link(ins):
                links[0] += 1
                ins.then_inc(act_c, 1)
                act.wait_ge(act_c, links[0])

            def squares(n, t):
                act.activation(hn[:, t, :], x[:, t, :], ACT.Square, accum_out=sumsq[:, n, t:t + 1]).then_inc(sq_done, 1)

            def norm(n):
                for t in range(TILES):
                    if n == 0:
                        act.wait_ge(x_in[t], 16)
                    else:
                        act.wait_ge(x_done, 2 * (n - 1) + t + 1)
                    squares(n, t)
                    if n == 1 and t == 0:
                        dense_chunk("g", 0, 0, 1)
                    elif n == 1:
                        high_hT(0)
                        high_hT(1)
                    elif n == 3:
                        expert_chunk(0, 0, t, t + 1)
                    if n % 2:
                        act.wait_ge(rstd_done, TILES * n + t + 1)
                        act.wait_ge(sq_done, TILES * n + t + 1)
                        act.activation(hn[:, t, :], x[:, t, :], ACT.Copy,
                                       scale=rstd[:, n, t:t + 1]).then_inc(hn_done, 1)
                if n == 3:
                    expert_chunk(0, 0, 2, 4)

            def mixer(l):
                def z_chunk(c, t):
                    a, b = Z_COLS[c]
                    if t == 0:
                        act.wait_ge(z_ps[l], c + 1)
                    else:
                        act.wait_ge(chunk_done, mixer_used(l, f"Z{c}"))
                    if c == 0:
                        act.wait_ge(rstd_done, TILES * 2 * l + t + 1)
                    rms = rstd[:, 2 * l, t:t + 1]
                    if c == 2:
                        act.activation(z[:, t, FCOL:FCOL + HEADS], ps[:, t, b - a:b - a + HEADS], ACT.Copy, scale=rms)
                    if c == NZ - 1:
                        act.activation(kC[:, t, :, 0:HEAD_DIM], as_block(ps[:, t, 0:GROUP], HEADS), ACT.Copy,
                                       scale=rms).then_inc(aug_done[l], 1)
                        a += GROUP
                    first = Z_COLS[c][0]
                    act.activation(z[:, t, a:b], ps[:, t, a - first:b - first], ACT.Copy,
                                   scale=rms).then_inc(z_done[l], 1)

                def exps(k):
                    act.wait_ge(max_done[l], k + 1)
                    _, _, n, _, nk = JOBS[k]
                    for s in range(n):
                        e = E[:, k % 2, s * nk:(s + 1) * nk]
                        ins = act.activation(e, e, ACT.Exp, bias=neg_max[:, k, s:s + 1],
                                             accum_out=row_sum[:, k, s:s + 1])
                    ins.then_inc(exp_done[l], 1)

                def pt_copy(k):
                    for b in range(pt_batches(k)):
                        act.wait_ge(pt_ps[l], pt_done(k) - pt_batches(k) + b + 1)
                        act.activation(pT[:, k % 2, 4 * b:4 * b + 4, :],
                                       ps[:, 7, :].rearrange("p (b n) -> p b n", b=4),
                                       ACT.Copy).then_inc(pt_ev[l], 1)

                norm(2 * l)
                if l == 0:
                    act.wait_ge(lam_sum, 1)
                    act.activation(lam_s[:, :, :], lam_s[:, :, :], ACT.Exp).then_inc(lam_exp, 1)
                for step in MIXER:
                    if step[0] == "Z":
                        z_chunk(int(step[1]), int(step[2]))
                    elif step == "LM":
                        for t in range(TILES):
                            act.wait_ge(lm_ps[l], 2 * t + 1)
                            act.activation(qA[:, t, :], ps[:, LM_BANK[t], 0:HEADS * QK_A],
                                           ACT.Copy).then_inc(uq_done[l], 1)
                            if t == 0:
                                act.wait_ge(lm_ps[l], 2)
                            else:
                                act.wait_ge(chunk_done, mixer_used(l, "LM"))
                            kv = ps[:, LM_BANK[t] + 1, :].rearrange("p (h d) -> p h d", h=HEADS)
                            act.activation(kA[:, t, :, 0:NOPE], kv[:, :, 0:NOPE], ACT.Copy)
                            act.activation(vA[:, t, :].rearrange("p (h d) -> p h d", h=HEADS),
                                           kv[:, :, NOPE:], ACT.Copy).then_inc(ukv_done[l], 1)
                    elif step == "F1":
                        act.wait_ge(f_in[l], 1)
                        link(act.activation(fg[:, 3], fg[:, 2], ACT.Exp))
                        act.activation(fg[:, 4], fg[:, 3], ACT.Ln, bias=1.0).then_inc(f_log[l], 1)
                    elif step[0] == "J":
                        k = int(step[1:])
                        if 1 <= k <= NJ:
                            pt_copy(k - 1)
                        if k < NJ:
                            exps(k)

            def dense_chunk(kind, s, first=0, last=4):
                n = FF_POS[(kind, s)]
                if first == 0:
                    act.wait_ge(slot_in[n % RING], landed[n])
                for v, src in ff_parts(kind, s)[first:last]:
                    if v >= UNITS:
                        act.wait_ge(unit_done, v + 1 - UNITS)
                    dst = ex_unit(v, src.shape[1] * src.shape[2])[0]
                    act.activation(as_block(dst, src.shape[1]), src, ACT.Copy).then_inc(hi_done, 1)

            def expert_chunk(i, c, first=0, last=4):
                if first == 0:
                    act.wait_ge(slot_in[(EX_AT + c) % RING],
                                i * EX_LAND + (landed_ex[c % EX_CHUNKS] + (c // EX_CHUNKS) * EX_LAND))
                for u in range(first, last):
                    v = FF_UNITS + 4 * c + u
                    act.wait_ge(unit_done, i * EX_UNITS + (v + 1 - UNITS))
                    act.activation(ex_unit(v)[0], ex_part(c, u), ACT.Copy).then_inc(hi_done, 1)

            def high_hT(b):
                t, half = divmod(b, 2)
                act.wait_ge(hT_done, 4 + b + 1)
                at = (slice(4 * half, 4 * half + 4), slice(t * P, (t + 1) * P))
                act.activation(hTs[:, 0, at[0], at[1]], hT[:, at[0], at[1]], ACT.Copy).then_inc(hTh_done, 1)

            def dense_ff():
                high_hT(2)
                high_hT(3)
                dense_chunk("g", 0, 1, 4)
                after = tasks(FF_STEPS)
                for n, (kind, s) in enumerate(ff_order(FF_STEPS)):
                    if n:
                        dense_chunk(kind, s)
                    for what, j in after.get(n, ()):
                        nq = ff_quarters(j)
                        if what == "silu":
                            act.wait_ge(unit_done, FF_UNIT[("g", j)] + nq)
                            if j:
                                act.wait_ge(ff_al, j)
                            act.activation(ff_act[:, 0:nq * SEQ].rearrange("p (b n) -> p b n", n=512),
                                           ps[:, 0:nq // 2, :], ACT.Silu).then_inc(ff_sd, 1)
                        elif what == "parts":
                            act.wait_ge(ff_ad, j + 1)
                            if j:
                                act.wait_ge(unit_done, FF_UNIT[("d", j - 1)] + ff_quarters(j - 1))
                            act.activation(acts[:, 0, 0:nq * SEQ], ff_act[:, 0:nq * SEQ], ACT.Copy).then_inc(ff_ah, 1)

            def expert_items(first):
                with act.Fori(first, first + EXPERTS) as i:
                    after = tasks(EX_STEPS)
                    for c in range(1, EX_CHUNKS):
                        expert_chunk(i, c)
                        for what, j in after.get(c, ()):
                            if what == "silu":
                                act.wait_ge(unit_done, i * EX_UNITS + (FF_UNITS + 4 * EX_POS[("g", j)] + 4))
                                if j:
                                    act.wait_ge(actT_ps, i * EX_STEPS + j)
                                act.activation(ex_act, ps[:, 0, :], ACT.Silu).then_inc(silu_done, 1)
                            elif what == "parts":
                                act.wait_ge(actT_ps, i * EX_STEPS + (j + 1))
                                act.activation(ex_actTs[:, 0], ps[:, 4, :].rearrange("p (q n) -> p q n", q=4),
                                               ACT.Copy).then_inc(acth_done, 1)
                        if c == 1:
                            copy_selT(i + 1)
                    token_parts(i + 2)
                    expert_chunk(i, EX_CHUNKS, 0, 3)
                    act.wait_ge(unit_done, i * EX_UNITS + (FF_UNITS + EX_UNITS))
                    for h in range(2):
                        act.activation(ex_out[:, xcols(h)], ps[:, 2 + h, :], ACT.Copy).then_inc(eo_done, 1)
                    expert_chunk(i, EX_CHUNKS, 3)

            def token_parts(n):
                act.wait_ge(xg_done, n)
                act.activation(xgTs[:, 0], xgT, ACT.Copy).then_inc(xgh_done, 1)

            def copy_selT(n):
                act.wait_ge(selT_ps, n)
                act.activation(sel_gT, ps[:, 6, 0:SEQ], ACT.Copy).then_inc(selT_done, 1)

            for l in range(DEPTH):
                mixer(l)
                norm(2 * l + 1)
                if l == 0:
                    dense_ff()
            act.wait_ge(top_done, 1)
            act.activation(route[:, 1, :], route[:, 0, :], ACT.Exp).then_inc(route_exp, 1)
            token_parts(1)
            expert_items(0)
            act.wait_ge(count_done, 1)
            count = act.value_load(most_i[0:1, 0:1], min_val=0, max_val=SEQ)
            for r in range(1, ROUNDS):
                with act.If(count > r * SLOTS):
                    expert_items(r * EXPERTS)
            act.wait_ge(x_final, 1)
            for t in range(TILES):
                squares(2 * DEPTH, t)

        @block.vector
        def _(dve):
            links = [0]

            def link(ins):
                links[0] += 1
                ins.then_inc(dve_c, 1)
                dve.wait_ge(dve_c, links[0])

            def norm_T(n):
                for b in range(4):
                    t, half = divmod(b, 2)
                    if b == 2 and n == 1:
                        dense_chunk("g", 0, 0, 1)
                        low_hT(0)
                        low_hT(1)
                    elif b == 2 and n == 3:
                        expert_chunk(0, 0, 0, 1)
                    dve.wait_ge(hT_ps, 4 * n + b + 1)
                    g = bc(gains(n)[:, 4 * half:4 * half + 4], 2, [P, 4, P])
                    dve.tensor_tensor(hT[:, 4 * half:4 * half + 4, t * P:(t + 1) * P],
                                      ps[:, 2 + b % 2, :].rearrange("p (c n) -> p c n", c=4), g,
                                      ALU.mult).then_inc(hT_done, 1)

            def rope(v, n, half, t):
                a = tmp_a[:, 0:n * 2 * half].rearrange("p (h i d) -> p h i d", h=n, i=2)
                b = tmp_b[:, 0:n * 2 * half].rearrange("p (h i d) -> p h i d", h=n, i=2)
                for i in range(2):
                    dve.tensor_tensor(a[:, :, i, :], v[:, :, i, :],
                                      bc(cst(f"cos{half}_{t}"), 1, [P, n, half]), ALU.mult)
                dve.tensor_tensor(b[:, :, 0, :], v[:, :, 1, :],
                                  bc(cst(f"nsin{half}_{t}"), 1, [P, n, half]), ALU.mult)
                link(dve.tensor_tensor(b[:, :, 1, :], v[:, :, 0, :],
                                       bc(cst(f"sin{half}_{t}"), 1, [P, n, half]), ALU.mult))
                return dve.tensor_tensor(v, a, b, ALU.add)

            def mixer(l):
                def batch(b):
                    dve.wait_ge(bt_ps[l], b + 1)
                    return ps[:, 2 + b % 2, :]

                def latents():
                    dve.wait_ge(z_done[l], 2)
                    for t in range(TILES):
                        for i, (a, n) in enumerate(((CQ, Q_RANK), (CKV, KV_RANK))):
                            link(dve.tensor_tensor(tmp_a[:, 0:n], z[:, t, a:a + n], z[:, t, a:a + n], ALU.mult))
                            ins = dve.tensor_reduce(lat_ss[:, t, i:i + 1], tmp_a[:, 0:n], AX.X, ALU.add)
                            if (t, i) != (TILES - 1, 1):
                                link(ins)
                    ins.then_inc(lat_sq[l], 1)
                    dve.wait_ge(lat_sq[l], 1)
                    for t in range(TILES):
                        kr = z[:, t, KR:KR + ROT].rearrange("p (h i d) -> p h i d", h=1, i=2)
                        link(rope(kr, 1, ROT // 2, t))
                        link(dve.tensor_copy(kA[:, t, :, NOPE:],
                                             bc(z[:, t, KR:KR + ROT], 1, [P, HEADS, ROT])))
                    dve.wait_ge(lat_rs[l], 1)
                    for t in range(TILES):
                        dve.tensor_scalar(latn[:, t, 0:Q_RANK], z[:, t, CQ:CQ + Q_RANK],
                                          lat_r[:, t, 0:1], None, ALU.mult)
                        dve.tensor_scalar(latn[:, t, Q_RANK:], z[:, t, CKV:CKV + KV_RANK],
                                          lat_r[:, t, 1:2], None, ALU.mult).then_inc(lat_done[l], 1)
                    dve.wait_ge(lat_done[l], 2)

                def rope_d(t):
                    dve.wait_ge(z_done[l], 2 * 1 + t + 1)
                    rotate(z[:, t, QD:QD + 2 * GROUP].rearrange("p (h i d) -> p h i d", h=4 * HEADS, i=2),
                           4 * HEADS, t)

                def rotate(v, n, t):
                    rope(v, n, ROT // 2, t).then_inc(rope_done[l], 1)
                    ropes[0] += 1
                    dve.wait_ge(rope_done[l], ropes[0])

                def forget():
                    dve.wait_ge(z_done[l], 2 * 3)
                    f = z[:, :, FCOL:FCOL + HEADS]
                    link(dve.tensor_tensor(fg[:, 0], f, bc(b_f[:, l, :], 1, [P, TILES, HEADS]), ALU.add))
                    link(dve.tensor_scalar(fg[:, 1], fg[:, 0], 0.0, None, ALU.min))
                    link(dve.tensor_scalar(fg[:, 2], fg[:, 0], 0.0, None, ALU.max))
                    dve.tensor_tensor(fg[:, 2], fg[:, 1], fg[:, 2], ALU.subtract).then_inc(f_in[l], 1)

                def mask(k):
                    g, t, n, _, nk = JOBS[k]
                    dve.wait_ge(s_ps[l], k + 1)
                    m = cst("dilated" if g == "B" else "causal")[:, SEQ - nk:]
                    e = E[:, k % 2, 0:n * nk].rearrange("p (s n) -> p s n", s=n)
                    s = score_places(k)[:, :, 0:nk]
                    dve.scalar_tensor_tensor(e, s, SCALE[g], bc(m, 1, [P, n, nk]), ALU.mult,
                                             ALU.add).then_inc(mask_done[l], 1)
                    dve.wait_ge(mask_done[l], k + 1)
                    dve.tensor_reduce(neg_max[:, k, 0:n], e, AX.X, ALU.max, negate=True).then_inc(max_done[l], 1)

                def combine(k):
                    _, _, n, _, nk = JOBS[k]
                    dve.wait_ge(exp_done[l], k + 1)
                    link(dve.reciprocal(row_inv[:, k, 0:n], row_sum[:, k, 0:n]))
                    r = row_inv[:, k, 0:n].rearrange("p (m i r) -> p m i r", m=2, i=2)
                    link(dve.tensor_scalar(r[:, :, 1], r[:, :, 1], neg_lam[:, l:l + 1], None, ALU.mult))
                    e = E[:, k % 2, 0:n * nk].rearrange("p (s n) -> p s n", s=n)
                    link(dve.tensor_tensor(e, e, bc(row_inv[:, k, 0:n], 2, [P, n, nk]), ALU.mult))
                    e = E[:, k % 2, 0:n * nk].rearrange("p (m i r) -> p m i r", m=2, i=2)
                    dve.tensor_tensor(e[:, :, 0, :], e[:, :, 0, :], e[:, :, 1, :], ALU.add).then_inc(comb_done[l], 1)

                def output(k):
                    g, t, n, s0, _ = JOBS[k]
                    nh = n // 2 if g == "D" else n
                    c0 = YCOL[g] + (s0 // 2) * HEAD_DIM
                    o = ps[:, 6, 0:nh * HEAD_DIM]
                    dst = y[:, t, c0:c0 + nh * HEAD_DIM]
                    if g != "D":
                        dve.wait_ge(exp_done[l], k + 1)
                        link(dve.reciprocal(row_inv[:, k, 0:n], row_sum[:, k, 0:n]))
                    dve.wait_ge(pv_ps[l], k + 1)
                    if g == "D":
                        ins = dve.tensor_copy(dst, o)
                    elif g == "B":
                        ins = dve.tensor_tensor(dst.rearrange("p (b a d) -> p a b d", a=2, b=2),
                                                o.rearrange("p (b a d) -> p a b d", a=2, b=2),
                                                bc(row_inv[:, k, 0:4].rearrange("p (a b) -> p a b", a=2), 3,
                                                   [P, 2, 2, HEAD_DIM]), ALU.mult)
                    else:
                        ins = dve.tensor_tensor(dst.rearrange("p (h d) -> p h d", h=nh),
                                                o.rearrange("p (h d) -> p h d", h=nh),
                                                bc(row_inv[:, k, 0:nh], 2, [P, nh, HEAD_DIM]), ALU.mult)
                    ins.then_inc(y_done[l], 1)

                def squares_d():
                    dve.wait_ge(y_done[l], D_JOBS)
                    sq = tmp_a[:, :].rearrange("p (t h d) -> p t h d", t=TILES, h=HEADS)
                    link(dve.tensor_tensor(sq, yd, yd, ALU.mult))
                    dve.tensor_reduce(d_ss[:, :], tmp_a[:, :].rearrange("p (h d) -> p h d", h=8), AX.X,
                                      ALU.add).then_inc(d_sq[l], 1)

                def norm_d():
                    dve.wait_ge(d_rs[l], 1)
                    for t in range(TILES):
                        dve.tensor_tensor(yd[:, t], yd[:, t], bc(d_r[:, 4 * t:4 * t + 4], 2, [P, HEADS, HEAD_DIM]),
                                          ALU.mult).then_inc(yd_done[l], 1)

                def gained(dst, src):
                    a = GAIN_AT["g_diff_sub"] + l
                    return dve.tensor_scalar(dst, src, g_cols[:, a:a + 1], 1.0 - lam_init, ALU.mult, ALU.mult)

                yd = y[:, :, 3 * GROUP:].rearrange("p t (h d) -> p t h d", h=HEADS)
                lam_init = 0.8 - 0.6 * math.exp(-0.3 * l)
                ropes = [0]
                norm_T(2 * l)
                if l == 0:
                    lambdas()
                for step in MIXER:
                    if step == "Z01":
                        latents()
                    elif step == "LT":
                        for t, b in enumerate(BATCH["LT"]):
                            src = batch(b)[:, 0:3 * P].rearrange("p (c n) -> p c n", c=3)
                            a = GAIN_AT["latent"] + 3 * l
                            dve.tensor_tensor(latT[:, :, t * P:(t + 1) * P], src, bc(g_cols[:, a:a + 3], 2, [P, 3, P]),
                                              ALU.mult).then_inc(bt_done[l], 1)
                    elif step == "Z10":
                        rope_d(0)
                    elif step == "Z20":
                        rope_d(1)
                    elif step == "LM":
                        for t in range(TILES):
                            dve.wait_ge(uq_done[l], t + 1)
                            v = qA[:, t, :].rearrange("p (h d) -> p h d", h=HEADS)[:, :, NOPE:]
                            rotate(v.rearrange("p h (i d) -> p h i d", i=2), HEADS, t)
                    elif step in ("QB", "QD"):
                        for t, b in enumerate(BATCH[step]):
                            src = batch(b).rearrange("p (a h n) -> p a h n", a=2, h=2)
                            dve.tensor_copy(pairT[:, :, :, t * P:(t + 1) * P], src).then_inc(bt_done[l], 1)
                    elif step in ("QA", "QC"):
                        rows = QK_A if step == "QA" else AUG
                        for i, b in enumerate(BATCH[step]):
                            t, qk = divmod(i, 2)
                            src = batch(b)[0:rows, :].rearrange("p (h n) -> p h n", h=HEADS)
                            dve.tensor_copy(wideT[0:rows, qk, :, t * P:(t + 1) * P], src).then_inc(bt_done[l], 1)
                    elif step == "F1":
                        forget()
                        dve.memset(qC[:, :, :, HEAD_DIM + 1:AUG], 1.0)
                        dve.memset(kC[:, :, :, HEAD_DIM:HEAD_DIM + 1], 1.0)
                    elif step == "F2":
                        dve.wait_ge(f_log[l], 1)
                        dve.tensor_tensor(fg[:, 5], fg[:, 1], fg[:, 4], ALU.subtract).then_inc(lf_done[l], 1)
                    elif step == "CS":
                        src = batch(BATCH["CS"][0])[:, 0:TILES * HEADS].rearrange("p (t h) -> p t h", t=TILES)
                        dve.tensor_copy(qC[:, :, :, HEAD_DIM], src)
                        dve.tensor_scalar(kC[:, :, :, HEAD_DIM + 1], src, -1.0, None, ALU.mult).then_inc(bt_done[l], 1)
                    elif step[0] == "J":
                        k = int(step[1:])
                        if 1 <= k <= D_JOBS:
                            combine(k - 1)
                        if k < NJ:
                            mask(k)
                        if k >= 2:
                            output(k - 2)
                        if k - 2 == D_JOBS - 1:
                            squares_d()
                    elif step == "Z50":
                        norm_d()
                    elif step == "Y0":
                        for t, b in enumerate(BATCH[step]):
                            src = batch(b).rearrange("p (c n) -> p c n", c=4)
                            tok = slice(t * P, (t + 1) * P)
                            gained(yT[:, 6:8, tok], src[:, 0:2])
                            dve.tensor_copy(yT[:, 0:2, tok], src[:, 2:4]).then_inc(bt_done[l], 1)
                    elif step == "YB":
                        src = batch(BATCH["YB"][0]).rearrange("p (c n) -> p c n", c=2)
                        dve.tensor_copy(yT[:, 2:4, :], src).then_inc(bt_done[l], 1)
                    elif step == "YC":
                        for t, b in enumerate(BATCH[step]):
                            src = batch(b)[:, 0:2 * P].rearrange("p (c n) -> p c n", c=2)
                            dve.tensor_copy(yT[:, 4:6, t * P:(t + 1) * P], src).then_inc(bt_done[l], 1)

                for t in range(TILES):
                    for h in range(2):
                        if t == 0:
                            dve.wait_ge(w_ps[l], h + 1)
                        else:
                            dve.wait_ge(chunk_done, mixer_used(l, f"W{h}"))
                        ins = dve.tensor_tensor(x[:, t, xcols(h)], x[:, t, xcols(h)], ps[:, W_BANK[h][t], :], ALU.add)
                    ins.then_inc(x_done, 1)

            def low(dst, src, high, signal):
                dve.tensor_tensor(dst, src, high.bitcast(F32), ALU.subtract).then_inc(signal, 1)

            def dense_chunk(kind, s, first=0, last=4):
                for v, src in ff_parts(kind, s)[first:last]:
                    n = src.shape[1]
                    high, lo = ex_unit(v, n * src.shape[2])
                    dve.wait_ge(hi_done, v + 1)
                    low(as_block(lo, n), src, as_block(high, n), lo_done)

            def expert_chunk(i, c, first=0, last=4):
                for u in range(first, last):
                    v = FF_UNITS + 4 * c + u
                    high, lo = ex_unit(v)
                    dve.wait_ge(hi_done, i * EX_UNITS + (v + 1))
                    low(lo, ex_part(c, u), high, lo_done)

            def low_hT(b):
                t, half = divmod(b, 2)
                dve.wait_ge(hTh_done, b + 1)
                at = (slice(4 * half, 4 * half + 4), slice(t * P, (t + 1) * P))
                low(hTs[:, 1, at[0], at[1]], hT[:, at[0], at[1]], hTs[:, 0, at[0], at[1]], hTl_done)

            def dense_ff():
                low_hT(2)
                low_hT(3)
                dense_chunk("g", 0, 1, 4)
                after = tasks(FF_STEPS)
                for n, (kind, s) in enumerate(ff_order(FF_STEPS)):
                    if n:
                        dense_chunk(kind, s)
                    for what, j in after.get(n, ()):
                        nq = ff_quarters(j)
                        if what == "act":
                            dve.wait_ge(ff_sd, j + 1)
                            dve.wait_ge(unit_done, FF_UNIT[("u", j)] + nq)
                            dve.tensor_tensor(ff_act[:, 0:nq * SEQ].rearrange("p (b n) -> p b n", n=512),
                                              ff_act[:, 0:nq * SEQ].rearrange("p (b n) -> p b n", n=512),
                                              ps[:, 2:2 + nq // 2, :], ALU.mult).then_inc(ff_ad, 1)
                        elif what == "parts":
                            dve.wait_ge(ff_ah, j + 1)
                            low(acts[:, 1, 0:nq * SEQ], ff_act[:, 0:nq * SEQ], acts[:, 0, 0:nq * SEQ], ff_al)
                dve.wait_ge(x_done, 2)
                for t in range(TILES):
                    if t == 0:
                        dve.wait_ge(ff_ps, 1)
                    else:
                        dve.wait_ge(unit_done, FF_UNITS)
                    dve.tensor_tensor(x[:, t, :], x[:, t, :],
                                      ps[:, 4 + 2 * t:6 + 2 * t, :].rearrange("p a b -> p (a b)"),
                                      ALU.add).then_inc(x_done, 1)

            def router():
                expert_chunk(0, 0, 1, 4)
                dve.wait_ge(logit_ps, 1)
                dve.tensor_copy(logitT, ps[0:EXPERTS, 0, 0:SEQ]).then_inc(logitT_done, 1)
                dve.wait_ge(logit_ps, 2)
                link(dve.tensor_copy(logits[:, :, :].rearrange("p t e -> p (t e)"),
                                     ps[:, 0, SEQ:SEQ + TILES * EXPERTS]))
                for t in range(TILES):
                    ins = dve.max(top[:, t, :], logits[:, t, :])
                link(ins)
                dve.tensor_tensor(route[:, 0, :], top[:, :, 1], top[:, :, 0], ALU.subtract).then_inc(top_done, 1)
                for t in range(TILES):
                    ins = dve.max_index(top_i[:, t, :], top[:, t, :], logits[:, t, :])
                link(ins)
                link(dve.tensor_copy(top_f[:, :, :], top_i[:, :, :]))
                iota8 = cst("iota")[:, 0:EXPERTS]
                for t in range(TILES):
                    for r in range(2):
                        ins = dve.tensor_scalar(hot[:, r, t, :], iota8, top_f[:, t, r:r + 1], None, ALU.is_equal)
                link(ins)
                dve.tensor_tensor(chosen[:, :, :], hot[:, 0], hot[:, 1], ALU.add).then_inc(chosen_done, 1)
                dve.memset(gate[:, :, :], 0.0)
                dve.memset(place[:, :, :], -1.0)
                dve.wait_ge(route_exp, 1)
                link(dve.tensor_scalar(route[:, 2, :], route[:, 1, :], 1.0, None, ALU.add))
                link(dve.reciprocal(route[:, 2, :], route[:, 2, :]))
                link(dve.tensor_tensor(route[:, 3, :], route[:, 1, :], route[:, 2, :], ALU.mult))
                for t in range(TILES):
                    for r in range(2):
                        ins = dve.tensor_scalar(hot[:, 2 + r, t, :], iota8, top_f[:, t, r:r + 1],
                                                route[:, 2 + r, t:t + 1], ALU.is_equal, ALU.mult)
                link(ins)
                for r in range(ROUNDS):
                    ins = dve.tensor_tensor(gate[:, :, r * EXPERTS:(r + 1) * EXPERTS], hot[:, 2], hot[:, 3], ALU.add)
                link(ins)
                dve.wait_ge(count_ps, 1)
                dve.wait_ge(chosen_done, 1)
                rank = ps[:, 1, 0:TILES * EXPERTS].rearrange("p (t e) -> p t e", t=TILES)
                link(dve.tensor_tensor(place[:, :, 0:EXPERTS], rank, chosen[:, :, :], ALU.mult))
                link(dve.tensor_scalar(place[:, :, 0:EXPERTS], place[:, :, 0:EXPERTS], -1.0, None, ALU.add))
                select(0, 1)
                for r in range(1, ROUNDS):
                    dve.tensor_scalar(place[:, :, r * EXPERTS:(r + 1) * EXPERTS], place[:, :, 0:EXPERTS],
                                      -float(r * SLOTS), None, ALU.add)
                link(dve.tensor_reduce(most[:, :], ps[:, 1, 16:16 + EXPERTS], AX.X, ALU.max))
                dve.tensor_copy(most_i[:, :], most[:, :]).then_inc(count_done, 1)
                dve.sem_inc(y_added, 4)

            def select(i, n):
                for t in range(TILES):
                    p_i = place[:, t, bass.ds(i, 1)]
                    dve.tensor_scalar(sel[:, t, :], cst("iota")[:, 0:SLOTS], p_i, None, ALU.is_equal)
                    ins = dve.tensor_scalar(sel_g[:, t, :], cst("iota")[:, 0:SLOTS], p_i,
                                            gate[:, t, bass.ds(i, 1)], ALU.is_equal, ALU.mult)
                ins.then_inc(sel_done, 1)

            def gathered(n):
                dve.wait_ge(gather_ps, n)
                if not isinstance(n, int):
                    dve.wait_ge(xgh_done, n - 1)
                dve.tensor_tensor(xgT, ps[:, 6:8, :].rearrange("p a (c n) -> p (a c) n", n=SLOTS),
                                  bc(gains(3), 2, [P, KC, SLOTS]), ALU.mult).then_inc(xg_done, 1)
                dve.wait_ge(xgh_done, n)
                low(xgTs[:, 1], xgT, xgTs[:, 0], xgT_done)

            def expert_items(first):
                with dve.Fori(first, first + EXPERTS) as i:
                    after = tasks(EX_STEPS)
                    for c in range(1, EX_CHUNKS):
                        expert_chunk(i, c)
                        for what, j in after.get(c, ()):
                            if what == "act":
                                dve.wait_ge(silu_done, i * EX_STEPS + (j + 1))
                                dve.wait_ge(unit_done, i * EX_UNITS + (FF_UNITS + 4 * EX_POS[("u", j)] + 4))
                                dve.tensor_tensor(ex_act, ex_act, ps[:, 1, :], ALU.mult).then_inc(act_done, 1)
                            elif what == "parts":
                                dve.wait_ge(acth_done, i * EX_STEPS + (j + 1))
                                low(ex_actTs[:, 1], ps[:, 4, :].rearrange("p (q n) -> p q n", q=4),
                                    ex_actTs[:, 0], actl_done)
                        if c == 1:
                            dve.wait_ge(selT_ps, i + 1)
                            select(i + 1, i + 2)
                    gathered(i + 2)
                    expert_chunk(i, EX_CHUNKS, 0, 3)
                    scattered(i, 0)
                    scattered(i, 1)
                    expert_chunk(i, EX_CHUNKS, 3)
                    scattered(i, 2)
                    scattered(i, 3)

            def scattered(i, q):
                t, h = divmod(q, 2)
                dve.wait_ge(scatter_ps, i * 4 + (q + 1))
                dve.wait_ge(y_added, i * 4 + (q + 1))
                dve.tensor_tensor(x[:, t, xcols(h)], x[:, t, xcols(h)], ps[:, SCATTER[q], :],
                                  ALU.add).then_inc(y_added, 1)

            def lambdas():
                dve.wait_ge(small_in, SMALL_IN)
                for i in range(2):
                    for l in range(DEPTH):
                        link(dve.tensor_tensor(lam_junk[:, :], lam_in[:, 2 * i, l, :], lam_in[:, 2 * i + 1, l, :], ALU.mult))
                        link(dve.tensor_reduce(lam_s[:, i, l:l + 1], lam_junk[:, :], AX.X, ALU.add))
                dve.sem_inc(lam_sum, 1)
                dve.wait_ge(lam_exp, 1)
                link(dve.tensor_tensor(neg_lam[:, :], lam_s[:, 1, :], lam_s[:, 0, :], ALU.subtract))
                for l in range(DEPTH):
                    link(dve.tensor_scalar(neg_lam[:, l:l + 1], neg_lam[:, l:l + 1],
                                           -(0.8 - 0.6 * math.exp(-0.3 * l)), None, ALU.add))

            dve.wait_ge(first_in, FIRST_IN)
            dve.wait_ge(g_ps, 1)
            dve.tensor_copy(g_cols[:, :], ps[:, 7, 0:GAIN_ROWS]).then_inc(g_done, 1)
            dve.wait_ge(g_done, 1)
            for l in range(DEPTH):
                mixer(l)
                norm_T(2 * l + 1)
                if l == 0:
                    dense_ff()
            router()
            gathered(1)
            expert_items(0)
            dve.wait_ge(y_added, 4 + 4 * EXPERTS)
            count = dve.value_load(most_i[0:1, 0:1], min_val=0, max_val=SEQ)
            for r in range(1, ROUNDS):
                with dve.If(count > r * SLOTS):
                    expert_items(r * EXPERTS)
                    dve.wait_ge(y_added, 4 + 4 * (r + 1) * EXPERTS)
            dve.sem_inc(x_final, 1)
            dve.wait_ge(gfin_in, 16)
            for t in range(TILES):
                dve.wait_ge(rstd_done, 2 * TILES * DEPTH + t + 1)
                dve.scalar_tensor_tensor(x[:, t, :], x[:, t, :], rstd[:, 2 * DEPTH, t:t + 1], g_fin,
                                         ALU.mult, ALU.mult).then_inc(out_ready, 1)

        @block.tensor
        def _(pe):
            def norm_T(n):
                for b in range(4):
                    t, half = divmod(b, 2)
                    if n % 2:
                        pe.wait_ge(hn_done, TILES * (n // 2) + t + 1)
                    elif n:
                        pe.wait_ge(x_done, 2 * (n - 1) + t + 1)
                    else:
                        pe.wait_ge(x_in[t], 16)
                    if b >= 2:
                        pe.wait_ge(hT_done, 4 * n + b - 1)
                    for c in range(4):
                        k = 4 * half + c
                        ins = pe.transpose(ps[:, 2 + b % 2, c * P:(c + 1) * P],
                                           (hn if n % 2 else x)[:, t, k * P:(k + 1) * P], ident)
                    ins.then_inc(hT_ps, 1)

            def arrived(n):
                pe.wait_ge(slot_in[n % RING], landed[n])

            def mixer(l):
                def batch(b):
                    if b >= 2:
                        pe.wait_ge(bt_done[l], b - 1)
                    return ps[:, 2 + b % 2, :]

                def z_chunk(c, t):
                    n = mixer_chunk(l, f"Z{c}")
                    wid = Z_COLS[c][1] - Z_COLS[c][0] + (HEADS if c == 2 else 0)
                    w_c = slot_view(n, 0, (KC, wid))
                    if t == 0:
                        arrived(n)
                    if (c, t) == (2, 1):
                        pe.wait_ge(ukv_done[l], TILES)
                    elif (c, t) == (3, 0):
                        pe.wait_ge(uq_done[l], TILES)
                    if c:
                        pe.wait_ge(z_done[l], 2 * (c - 1) + t + 1)
                    else:
                        pe.wait_ge(hT_done, 4 * 2 * l + 2 * t + 2)
                    for k in range(KC):
                        ins = pe.matmul(ps[:, t, 0:wid], hT[:, k, t * P:(t + 1) * P], w_c[:, k, :],
                                        start=(k == 0), stop=(k == KC - 1))
                    ins.then_inc(chunk_done if t else z_ps[l], 1)

                def values(g, kb, h):
                    if g == "A":
                        return vA[:, kb, h * HEAD_DIM:(h + 1) * HEAD_DIM]
                    c = {"B": VB, "C": VCOL, "D": VD}[g] + h * HEAD_DIM
                    return z[:, kb, c:c + HEAD_DIM]

                def y_times_w(h, t, ks):
                    w_h = slot_view(mixer_chunk(l, f"W{h}"), 0, (KC, FW))
                    for k in ks:
                        ins = pe.matmul(ps[:, W_BANK[h][t], :], yT[:, k, t * P:(t + 1) * P], w_h[:, k, :],
                                        start=(k == Y_FIRST[0]), stop=(k == 5))
                    return ins

                def scores(k):
                    g, t, n, s0, nk = JOBS[k]
                    pe.wait_ge(bt_done[l], NEED[g])
                    if k:
                        pe.wait_ge(mask_done[l], k)
                    places = score_places(k)
                    for s in range(n):
                        if g in "AC":
                            rows = QK_A if g == "A" else AUG
                            q, kk = wideT[0:rows, 0, s, :], wideT[0:rows, 1, s, :]
                        elif g == "B":
                            r = 64 * (s % 2)
                            q, kk = pairT[r:r + 64, 0, s // 2, :], pairT[r:r + 64, 1, s // 2, :]
                        else:
                            u, r = divmod(s0 + s, 4)
                            q, kk = pairT[32 * r:32 * r + 32, 0, u, :], pairT[32 * r:32 * r + 32, 1, u, :]
                        ins = pe.matmul(places[:, spot(k, s), 0:nk], q[:, t * P:(t + 1) * P], kk[:, 0:nk],
                                        start=True, stop=True)
                    ins.then_inc(s_ps[l], 1)

                def transposed(k, b):
                    g, _, _, _, nk = JOBS[k]
                    pe.wait_ge(exp_done[l], k + 1)
                    if g == "D":
                        pe.wait_ge(comb_done[l], k + 1)
                    done = pt_done(k) - pt_batches(k) + b
                    if done:
                        pe.wait_ge(pt_ev[l], done)
                    else:
                        pe.wait_ge(ukv_done[l], 1)
                    for i, (s, kb, _) in enumerate(head_blocks(k)[b]):
                        ins = pe.transpose(ps[:, 7, i * P:(i + 1) * P],
                                           E[:, k % 2, s * nk + kb * P:s * nk + (kb + 1) * P], ident)
                    ins.then_inc(pt_ps[l], 1)

                def times_values(k):
                    g, _, n, s0, nk = JOBS[k]
                    nh = n // 2 if g == "D" else n
                    pe.wait_ge(pt_ev[l], pt_done(k))
                    if k:
                        pe.wait_ge(y_done[l], k)
                    else:
                        pe.wait_ge(uq_done[l], 1)
                    if g == "A":
                        pe.wait_ge(ukv_done[l], TILES)
                    pe.wait_ge(z_done[l], 2 * {"D": 3, "A": 1, "B": 5, "C": 6}[g])
                    for h in range(nh):
                        c = h * HEAD_DIM
                        for kb in range(nk // P):
                            ins = pe.matmul(ps[:, 6, c:c + HEAD_DIM], pT[:, k % 2, kb * nh + h, :],
                                            values(g, kb, s0 // 2 + h),
                                            start=(kb == 0), stop=(kb == nk // P - 1))
                    ins.then_inc(pv_ps[l], 1)

                norm_T(2 * l)
                for step in MIXER:
                    if step[0] == "Z":
                        z_chunk(int(step[1]), int(step[2]))
                    elif step == "LT":
                        for t, b in enumerate(BATCH["LT"]):
                            pe.wait_ge(lat_done[l], t + 1)
                            bank = batch(b)
                            for c in range(3):
                                ins = pe.transpose(bank[:, c * P:(c + 1) * P], latn[:, t, c * P:(c + 1) * P], ident)
                            ins.then_inc(bt_ps[l], 1)
                    elif step == "LM":
                        n = mixer_chunk(l, "LM")
                        arrived(n)
                        w_uq = slot_view(n, 0, (2, HEADS * QK_A))
                        w_ukv = slot_view(n, 2 * HEADS * QK_A, (1, 2 * GROUP))
                        for t in range(TILES):
                            tok = slice(t * P, (t + 1) * P)
                            pe.wait_ge(bt_done[l], t + 1)
                            if t:
                                pe.wait_ge(z_done[l], 2 * 2 + 1)
                            for c in range(2):
                                ins = pe.matmul(ps[:, LM_BANK[t], 0:HEADS * QK_A], latT[:, c, tok], w_uq[:, c, :],
                                                start=(c == 0), stop=(c == 1))
                            ins.then_inc(lm_ps[l], 1)
                            ins = pe.matmul(ps[:, LM_BANK[t] + 1, :], latT[:, 2, tok], w_ukv[:, 0, :],
                                            start=True, stop=True)
                            ins.then_inc(chunk_done if t else lm_ps[l], 1)
                    elif step in ("QB", "QD"):
                        first = QB if step == "QB" else QD
                        for t, b in enumerate(BATCH[step]):
                            if step == "QB":
                                pe.wait_ge(rope_b[l], t + 1)
                            else:
                                pe.wait_ge(rope_done[l], ROPES["D"] + t + 1)
                            bank = batch(b)
                            for c in range(4):
                                ins = pe.transpose(bank[:, c * P:(c + 1) * P],
                                                   z[:, t, first + c * P:first + (c + 1) * P], ident)
                            ins.then_inc(bt_ps[l], 1)
                    elif step in ("QA", "QC"):
                        for i, b in enumerate(BATCH[step]):
                            t, qk = divmod(i, 2)
                            if step == "QA":
                                pe.wait_ge(mask_done[l], D_JOBS)
                                pe.wait_ge(rope_done[l], ROPES["A"] + t + 1)
                                pe.wait_ge(ukv_done[l], t + 1)
                                src = (kA[:, t] if qk else qA[:, t, :].rearrange("p (h d) -> p h d", h=HEADS))
                                rows = QK_A
                            else:
                                pe.wait_ge((aug_done if qk else augq_done)[l], t + 1)
                                pe.wait_ge(bt_done[l], BATCH["CS"][0] + 1)
                                src, rows = (kC if qk else qC)[:, t], AUG
                            bank = batch(b)
                            for h in range(HEADS):
                                ins = pe.transpose(bank[0:rows, h * P:(h + 1) * P], src[:, h, :], ident)
                            ins.then_inc(bt_ps[l], 1)
                    elif step == "CS":
                        pe.wait_ge(lf_done[l], 1)
                        bank = batch(BATCH["CS"][0])
                        pe.matmul(bank[:, 0:HEADS], tri, fg[:, 5, 0, :], start=True, stop=True)
                        pe.matmul(bank[:, HEADS:2 * HEADS], ones, fg[:, 5, 0, :], start=True, stop=False)
                        pe.matmul(bank[:, HEADS:2 * HEADS], tri, fg[:, 5, 1, :], start=False,
                                  stop=True).then_inc(bt_ps[l], 1)
                    elif step == "Y0":
                        pe.wait_ge(y_done[l], 5)
                        for t, b in enumerate(BATCH[step]):
                            pe.wait_ge(yd_done[l], t + 1)
                            bank = batch(b)
                            for c, k in enumerate(Y_FIRST):
                                ins = pe.transpose(bank[:, c * P:(c + 1) * P], y[:, t, k * P:(k + 1) * P], ident)
                            ins.then_inc(bt_ps[l], 1)
                    elif step == "YB":
                        pe.wait_ge(y_done[l], 7)
                        bank = batch(BATCH["YB"][0])
                        for c, k in enumerate(Y_REST):
                            for t in range(TILES):
                                a = (2 * c + t) * P
                                ins = pe.transpose(bank[:, a:a + P], y[:, t, k * P:(k + 1) * P], ident)
                        ins.then_inc(bt_ps[l], 1)
                    elif step == "YC":
                        for t, b in enumerate(BATCH[step]):
                            pe.wait_ge(y_done[l], NJ - 1 + t)
                            bank = batch(b)
                            for c, k in enumerate((4, 5)):
                                ins = pe.transpose(bank[:, c * P:(c + 1) * P], y[:, t, k * P:(k + 1) * P], ident)
                            ins.then_inc(bt_ps[l], 1)
                    elif step in ("W0", "W1"):
                        t = int(step[1])
                        arrived(mixer_chunk(l, "W0"))
                        pe.wait_ge(bt_done[l], BATCH["Y0"][t] + 1)
                        pe.wait_ge(z_done[l], 2 * NZ)
                        y_times_w(0, t, Y_FIRST)
                    elif step == "WB":
                        pe.wait_ge(bt_done[l], BATCH["YB"][0] + 1)
                        for t in range(TILES):
                            y_times_w(0, t, Y_REST)
                    elif step in ("H0", "H1"):
                        t = int(step[1])
                        arrived(mixer_chunk(l, "W1"))
                        pe.wait_ge(mask_done[l], NJ)
                        y_times_w(1, t, Y_FIRST + Y_REST)
                    elif step[0] == "J":
                        k = int(step[1:])
                        late = 1 <= k <= D_JOBS or k == NJ - 1
                        if k < NJ and late:
                            scores(k)
                        if 1 <= k <= NJ:
                            transposed(k - 1, 0)
                        if k < NJ and not late:
                            scores(k)
                        if k >= 2:
                            times_values(k - 2)
                        if 1 <= k <= NJ and pt_batches(k - 1) == 2:
                            transposed(k - 1, 1)

                for t in range(TILES):
                    pe.wait_ge(bt_done[l], BATCH["YC"][t] + 1)
                    for h in range(2):
                        y_times_w(h, t, (4, 5)).then_inc(chunk_done if t else w_ps[l], 1)

            def three(dst, a, b, first, last):
                for i, (ia, ib) in enumerate(((0, 0), (0, 1), (1, 0))):
                    ins = pe.matmul(dst, a[ia], b[ib], start=(first and i == 0), stop=(last and i == 2))
                return ins

            def dense_ff():
                pe.wait_ge(hTl_done, 4)
                for kind, s in ff_order(FF_STEPS):
                    nq = ff_quarters(s)
                    if kind == "d":
                        pe.wait_ge(ff_al, s + 1)
                    elif kind == "g" and s:
                        pe.wait_ge(ff_sd, s)
                    elif s:
                        pe.wait_ge(ff_ad, s)
                    for q in range(nq):
                        v = FF_UNIT[(kind, s)] + q
                        pe.wait_ge(lo_done, v + 1)
                        parts = ex_unit(v)
                        if kind == "d":
                            last = s == FF_STEPS - 1 and q == nq - 1
                            for t in range(TILES):
                                a = q * SEQ + t * P
                                for h in range(2):
                                    ins = three(ps[:, 4 + 2 * t + h, :], [acts[:, i, a:a + P] for i in range(2)],
                                                [p[:, xcols(h)] for p in parts], s == 0 and q == 0, last)
                                if last and t == 0:
                                    ins.then_inc(ff_ps, 1)
                        else:
                            first = 0 if kind == "g" else 2
                            dst = ps[:, first + q // 2, (q % 2) * SEQ:(q % 2 + 1) * SEQ]
                            for k in range(KC):
                                ins = three(dst, [p[:, k * P:(k + 1) * P] for p in parts],
                                            [hTs[:, i, k, :] for i in range(2)], k == 0, k == KC - 1)
                        ins.then_inc(unit_done, 1)

            def router():
                pe.wait_ge(hT_done, 4 * 4)
                pe.wait_ge(small_in, SMALL_IN)
                for k in range(KC):
                    ins = pe.matmul(ps[0:EXPERTS, 0, 0:SEQ], w_r[:, k, :], hT[:, k, :],
                                    start=(k == 0), stop=(k == KC - 1))
                ins.then_inc(logit_ps, 1)
                pe.wait_ge(logitT_done, 1)
                for t in range(TILES):
                    a = SEQ + t * EXPERTS
                    ins = pe.transpose(ps[:, 0, a:a + EXPERTS], logitT[:, t * P:(t + 1) * P],
                                       ident[0:EXPERTS, 0:EXPERTS])
                ins.then_inc(logit_ps, 1)
                pe.wait_ge(chosen_done, 1)
                bank = ps[:, 1, :]
                pe.matmul(bank[:, 0:8], tri, chosen[:, 0, :], start=True, stop=True)
                for first, last in ((8, tri), (16, ones)):
                    pe.matmul(bank[:, first:first + 8], ones, chosen[:, 0, :], start=True, stop=False)
                    ins = pe.matmul(bank[:, first:first + 8], last, chosen[:, 1, :], start=False, stop=True)
                ins.then_inc(count_ps, 1)

            def gather(n):
                pe.wait_ge(sel_done, n)
                for c in range(KC):
                    for t in range(TILES):
                        ins = pe.matmul(ps[:, 6 + c // 4, (c % 4) * SLOTS:(c % 4 + 1) * SLOTS],
                                        hn[:, t, c * P:(c + 1) * P], sel[:, t, :],
                                        start=(t == 0), stop=(t == TILES - 1))
                ins.then_inc(gather_ps, 1)

            def turn_selection(n):
                pe.wait_ge(xg_done, n)
                for t in range(TILES):
                    ins = pe.transpose(ps[:, 6, t * P:(t + 1) * P], sel_g[:, t, :], ident)
                ins.then_inc(selT_ps, 1)

            def expert_items(first):
                with pe.Fori(first, first + EXPERTS) as i:
                    def unit(c, u):
                        v = FF_UNITS + 4 * c + u
                        pe.wait_ge(lo_done, i * EX_UNITS + (v + 1))
                        return ex_unit(v)

                    def product(kind, j):
                        bank = 0 if kind == "g" else 1
                        if j == 0:
                            pe.wait_ge(y_added, i * 4 + (bank + 1))
                        elif kind == "g":
                            pe.wait_ge(silu_done, i * EX_STEPS + j)
                        else:
                            pe.wait_ge(act_done, i * EX_STEPS + j)
                        for u in range(4):
                            parts = unit(EX_POS[(kind, j)], u)
                            for k in range(2):
                                ins = three(ps[:, bank, :], [xgTs[:, h, 2 * u + k, :] for h in range(2)],
                                            [p[:, k * FW:(k + 1) * FW] for p in parts],
                                            u == 0 and k == 0, u == 3 and k == 1)
                            ins.then_inc(unit_done, 1)

                    def turn(j):
                        pe.wait_ge(act_done, i * EX_STEPS + (j + 1))
                        if j == 0:
                            pe.wait_ge(y_added, i * 4 + 4)
                        else:
                            pe.wait_ge(actl_done, i * EX_STEPS + j)
                        for q in range(4):
                            ins = pe.transpose(ps[:, 4, q * P:(q + 1) * P], ex_act[:, q * P:(q + 1) * P], ident)
                        ins.then_inc(actT_ps, 1)

                    def down(j):
                        pe.wait_ge(actl_done, i * EX_STEPS + (j + 1))
                        for q in range(4):
                            parts = unit(EX_POS[("d", j)], q)
                            for h in range(2):
                                ins = three(ps[:, 2 + h, :], [ex_actTs[:, p, q, :] for p in range(2)],
                                            [p[:, xcols(h)] for p in parts],
                                            j == 0 and q == 0, j == EX_STEPS - 1 and q == 3)
                            ins.then_inc(unit_done, 1)

                    pe.wait_ge(xgT_done, i + 1)
                    after = tasks(EX_STEPS)
                    for c, (kind, s) in enumerate(ff_order(EX_STEPS)):
                        if kind == "d":
                            if s == EX_STEPS - 1:
                                pe.wait_ge(selT_done, i + 1)
                                gather(i + 2)
                            down(s)
                        else:
                            product(kind, s)
                        for what, j in after.get(c, ()):
                            if what == "act":
                                turn(j)
                    for q in range(4):
                        t, h = divmod(q, 2)
                        pe.wait_ge(eo_done, i * 2 + (h + 1))
                        pe.matmul(ps[:, SCATTER[q], :], sel_gT[:, t * P:(t + 1) * P], ex_out[:, xcols(h)],
                                  start=True, stop=True).then_inc(scatter_ps, 1)
                    turn_selection(i + 2)

            pe.wait_ge(first_in, FIRST_IN)
            pe.transpose(ps[:, 7, 0:GAIN_ROWS], g_rows[:, :], ident[0:GAIN_ROWS, 0:GAIN_ROWS]).then_inc(g_ps, 1)
            for l in range(DEPTH):
                mixer(l)
                norm_T(2 * l + 1)
                if l == 0:
                    dense_ff()
            router()
            gather(1)
            turn_selection(1)
            expert_items(0)
            pe.wait_ge(count_done, 1)
            count = pe.value_load(most_i[0:1, 0:1], min_val=0, max_val=SEQ)
            for r in range(1, ROUNDS):
                with pe.If(count > r * SLOTS):
                    expert_items(r * EXPERTS)


LM_BANK = (6, 0)
W_BANK = ((0, 1), (4, 5))
SCATTER = (0, 1, 5, 4)
FIRST_IN = 16 * 9
SMALL_IN = 16 * 6
GAIN_AT = {"g_mix": 0, "g_ffn": DEPTH * KC, "latent": 2 * DEPTH * KC, "g_diff_sub": 2 * DEPTH * KC + 3 * DEPTH}
GAIN_ROWS = 2 * DEPTH * KC + 4 * DEPTH

_INS = ["x", "g_mix", "w_in", "b_forget", "g_q_lat", "g_kv_lat", "w_uq", "w_ukv", "lambda_q1",
        "lambda_k1", "lambda_q2", "lambda_k2", "g_diff_sub", "w_out", "g_ffn", "w_ffn_gate",
        "w_ffn_up", "w_ffn_down", "w_router", "w_exp_gate", "w_exp_up", "w_exp_down", "g_final"]


def kernel(**inputs):
    import concourse.bacc as _bacc
    from concourse.bass_utils import run_bass_kernel_spmd as _run

    nc = _bacc.Bacc("TRN2", target_bir_lowering=False, num_devices=1)
    arrays = {n: np.ascontiguousarray(inputs[n]) for n in _INS}
    arrays["const"] = CONSTANTS
    w = {n: nc.dram_tensor(f"in_{n}", a.shape, F32, kind="ExternalInput").ap() for n, a in arrays.items()}
    out = nc.dram_tensor("out", (1, SEQ, D_MODEL), F32, kind="ExternalOutput").ap()
    with nc.allow_non_contiguous_dma(reason="gains of a few kilobytes, one element per partition"):
        build(nc, w, out)
    r = _run(nc, [{f"in_{n}": a for n, a in arrays.items()}], core_ids=[0])
    return r.results[0]["out"]
```
